# Optimizing a Trainium2 kernel written in Bass

```python
import jax, jax.numpy as jnp
from jax import lax
import numpy as np

D_MODEL = 1024
BATCH = 1
SEQ = 256
DEPTH = 2
DEC_BATCH = 8
DEC_SEQ = 1
PAST_LEN = 2048
PAGE_SIZE = 128

HD_A = 64
H_A = D_MODEL // HD_A
D_A = H_A * HD_A
W_LORA = 64
A_LORA = 64
G_LORA = 128
A_COLS = 3 * D_A + W_LORA + A_LORA + G_LORA
RWKV_GN_EPS = 6.4e-4
HD_B = 128
H_B = D_MODEL // HD_B
D_B = H_B * HD_B
CONV_W = 4
GDN_CHUNK = 64
B_COLS = 4 * D_B + 2 * H_B
IN_COLS = A_COLS + B_COLS + 2 * D_MODEL
D_FF = 2816
N_SUB = 3
FFN_RES = 0.5
RMS_EPS = 1e-6

kernel_name = 'hybrid_rwkv7_gdn_macaron_decoder_step'

def split_cols(x, sizes):
    offsets = np.cumsum(sizes)[:-1].tolist()
    return jnp.split(x, offsets, axis=-1)

def rmsnorm(x, w):
    x32 = x.astype(jnp.float32)
    y = x32 * lax.rsqrt(jnp.mean(x32 * x32, axis=-1, keepdims=True) + RMS_EPS)
    return (y * w.astype(jnp.float32)).astype(x.dtype)

def l2norm(x, eps):
    return x * lax.rsqrt(jnp.sum(x * x, axis=-1, keepdims=True) + eps)

def swiglu(h, up, down):
    gate, val = jnp.split(h @ up, 2, axis=-1)
    return (jax.nn.silu(gate) * val) @ down

def rwkv7_step(S, inp):
    r, w, k, v, kk, b = inp
    sa = jnp.einsum('bhvk,bhk->bhv', S, -kk)
    S = S * w[:, :, None, :] + sa[..., None] * b[:, :, None, :] + v[..., None] * k[:, :, None, :]
    y = jnp.einsum('bhvk,bhk->bhv', S, r)
    return S, y

def rwkv7_branch(pa, shift0, wkv0, mu, w0, w2, a0, a2, g2, k_k, k_a, r_k, ln_w, ln_b):
    B, T, _ = pa.shape
    f32 = jnp.float32
    prev = jnp.concatenate([shift0[:, None, :].astype(pa.dtype), pa[:, :-1]], axis=1)
    xs = (pa + mu * (prev - pa)).astype(f32)
    r, k, v, wd, ad, gd = split_cols(xs, [D_A, D_A, D_A, W_LORA, A_LORA, G_LORA])
    w_log = -jax.nn.softplus(-(w0 + jnp.tanh(wd) @ w2)) - 0.5
    decay = jnp.exp(-jnp.exp(w_log))
    a = jax.nn.sigmoid(a0 + ad @ a2)
    g = jax.nn.sigmoid(gd) @ g2
    heads = lambda t: t.reshape(B, T, H_A, HD_A)
    kk = l2norm(heads(k * k_k), 1e-12)
    k = k * (1.0 + (a - 1.0) * k_a)
    r_h, k_h, v_h, w_h, a_h = heads(r), heads(k), heads(v), heads(decay), heads(a)
    tmaj = lambda t: jnp.moveaxis(t, 1, 0)
    S, y = lax.scan(rwkv7_step, wkv0.astype(f32),
                    (tmaj(r_h), tmaj(w_h), tmaj(k_h), tmaj(v_h), tmaj(kk), tmaj(kk * a_h)))
    y = jnp.moveaxis(y, 0, 1)
    mean = jnp.mean(y, axis=-1, keepdims=True)
    var = jnp.mean(jnp.square(y - mean), axis=-1, keepdims=True)
    y = ((y - mean) * lax.rsqrt(var + RWKV_GN_EPS)).reshape(B, T, D_A) * ln_w + ln_b
    bonus = jnp.sum(r_h * k_h * r_k, axis=-1, keepdims=True) * v_h
    out = (y + bonus.reshape(B, T, D_A)) * g
    return out, pa[:, -1], S

def gated_delta_chunked(q, k, v, g, beta, S0):
    B, T, H, _ = q.shape
    DV = v.shape[-1]
    C = GDN_CHUNK
    n = (T + C - 1) // C
    pad = n * C - T

    def blocks(t):
        t = jnp.pad(t, [(0, 0), (0, pad)] + [(0, 0)] * (t.ndim - 2))
        t = t.reshape((B, n, C) + t.shape[2:])
        return jnp.moveaxis(t, (1, 3), (0, 2))

    qb, kb, vb, gb, bb = blocks(q), blocks(k), blocks(v), blocks(g), blocks(beta)
    gc = jnp.cumsum(gb, axis=-1)
    idx = jnp.arange(C)
    incl = idx[:, None] >= idx[None, :]
    strict = idx[:, None] > idx[None, :]
    decay = jnp.exp(jnp.where(incl, gc[..., :, None] - gc[..., None, :], -jnp.inf))
    k_beta = kb * bb[..., None]
    v_beta = vb * bb[..., None]
    L = jnp.where(strict, jnp.einsum('nbhcd,nbhsd->nbhcs', k_beta, kb) * decay, 0.0)
    eye = jnp.eye(C, dtype=L.dtype)
    tinv = lax.linalg.triangular_solve(eye + L, jnp.broadcast_to(eye, L.shape),
                                       left_side=True, lower=True, unit_diagonal=True)
    u = jnp.einsum('nbhcs,nbhse->nbhce', tinv, v_beta)
    w = jnp.einsum('nbhcs,nbhsd->nbhcd', tinv, k_beta * jnp.exp(gc)[..., None])
    attn = jnp.einsum('nbhcd,nbhsd->nbhcs', qb, kb) * decay
    g_last = gc[..., -1]
    q_dec = qb * jnp.exp(gc)[..., None]
    k_dec = kb * jnp.exp(g_last[..., None] - gc)[..., None]

    def step(S, inp):
        q_c, k_c, u_c, w_c, a_c, gl_c = inp
        v_new = u_c - jnp.einsum('bhcd,bhde->bhce', w_c, S)
        o = jnp.einsum('bhcd,bhde->bhce', q_c, S) + jnp.einsum('bhcs,bhse->bhce', a_c, v_new)
        S = S * jnp.exp(gl_c)[..., None, None] + jnp.einsum('bhcd,bhce->bhde', k_c, v_new)
        return S, o

    S, o = lax.scan(step, S0, (q_dec, k_dec, u, w, attn, g_last))
    o = jnp.moveaxis(o, (0, 2), (1, 3)).reshape(B, n * C, H, DV)[:, :T]
    return o, S

def gdn_branch(pb, conv0, ssm0, conv_w, a_log, dt_bias, norm_w):
    B, T, _ = pb.shape
    f32 = jnp.float32
    qkv, a_in, b_in, z = split_cols(pb, [3 * D_B, H_B, H_B, D_B])
    xc = jnp.concatenate([conv0.astype(qkv.dtype), qkv], axis=1)
    conv = sum(xc[:, j:j + T] * conv_w[j] for j in range(CONV_W))
    qkv_c = jax.nn.silu(conv).astype(f32)
    q, k, v = split_cols(qkv_c, [D_B, D_B, D_B])
    q = l2norm(q.reshape(B, T, H_B, HD_B), 1e-6) * (HD_B ** -0.5)
    k = l2norm(k.reshape(B, T, H_B, HD_B), 1e-6)
    v = v.reshape(B, T, H_B, HD_B)
    beta = jax.nn.sigmoid(b_in.astype(f32))
    g = -jnp.exp(a_log.astype(f32)) * jax.nn.softplus(a_in.astype(f32) + dt_bias)
    o, S = gated_delta_chunked(q, k, v, g, beta, ssm0.astype(f32))
    o = o * lax.rsqrt(jnp.mean(o * o, axis=-1, keepdims=True) + RMS_EPS) * norm_w
    o = o * jax.nn.silu(z.astype(f32).reshape(B, T, H_B, HD_B))
    return o.reshape(B, T, D_B), xc[:, T:], S

def decoder_layer(x, c, shift0, wkv0, conv0, ssm0, w_ada, b_ada, norm_pre, norm_post,
                  ffn_up, ffn_down, w_in, w_out, rwkv_mu, rwkv_w0, rwkv_w2, rwkv_a0, rwkv_a2,
                  rwkv_g2, rwkv_k_k, rwkv_k_a, rwkv_r_k, rwkv_ln_w, rwkv_ln_b,
                  gdn_conv, gdn_a_log, gdn_dt_bias, gdn_norm_w):
    B = x.shape[0]
    mod = (jax.nn.silu(c) @ w_ada + b_ada).reshape(B, N_SUB, 3, D_MODEL)
    m_shift, m_scale, m_gate = mod[:, :, 0], mod[:, :, 1], mod[:, :, 2]

    def sub_in(t, i):
        return rmsnorm(t, norm_pre[i]) * (1.0 + m_scale[:, i, None]) + m_shift[:, i, None]

    def sub_out(t, y, i, res):
        return t + res * m_gate[:, i, None] * rmsnorm(y, norm_post[i])

    x = sub_out(x, swiglu(sub_in(x, 0), ffn_up[0], ffn_down[0]), 0, FFN_RES)
    h = sub_in(x, 1)
    pa, pb, pg = split_cols(h @ w_in, [A_COLS, B_COLS, 2 * D_MODEL])
    ya, shift_new, wkv_new = rwkv7_branch(pa, shift0, wkv0, rwkv_mu, rwkv_w0, rwkv_w2, rwkv_a0,
                                          rwkv_a2, rwkv_g2, rwkv_k_k, rwkv_k_a, rwkv_r_k,
                                          rwkv_ln_w, rwkv_ln_b)
    yb, conv_new, ssm_new = gdn_branch(pb, conv0, ssm0, gdn_conv, gdn_a_log, gdn_dt_bias, gdn_norm_w)
    g_a, g_b = jnp.split(jax.nn.sigmoid(pg), 2, axis=-1)
    merged = (g_a * ya.astype(x.dtype) + g_b * yb.astype(x.dtype)) @ w_out
    x = sub_out(x, merged, 1, 1.0)
    x = sub_out(x, swiglu(sub_in(x, 2), ffn_up[1], ffn_down[1]), 2, FFN_RES)
    return x, shift_new, wkv_new, conv_new, ssm_new

def setup_inputs(seed: int = 0) -> dict:
    key = jax.random.key(seed)
    ks = jax.random.split(key, 40)
    f32 = jnp.float32

    def nrm(k, shape, s):
        return jax.random.normal(k, shape, f32) * s

    def uni(k, shape, lo, hi):
        return jax.random.uniform(k, shape, f32, minval=lo, maxval=hi)

    return {
        'x_prompt': nrm(ks[0], (BATCH, SEQ, D_MODEL), 1.0),
        'x_sample': nrm(ks[1], (DEC_BATCH, DEC_SEQ, D_MODEL), 1.0),
        'c_prompt': nrm(ks[2], (BATCH, D_MODEL), 1.0),
        'c_sample': nrm(ks[3], (DEC_BATCH, D_MODEL), 1.0),
        'state_rwkv_shift': nrm(ks[4], (DEPTH, DEC_BATCH, A_COLS), 1.0),
        'state_rwkv_wkv': nrm(ks[5], (DEPTH, DEC_BATCH, H_A, HD_A, HD_A), 0.1),
        'state_gdn_conv': nrm(ks[6], (DEPTH, DEC_BATCH, CONV_W - 1, 3 * D_B), 0.5),
        'state_gdn_ssm': nrm(ks[7], (DEPTH, DEC_BATCH, H_B, HD_B, HD_B), 0.05),
        'w_ada': nrm(ks[8], (DEPTH, D_MODEL, 3 * N_SUB * D_MODEL), 0.5 * D_MODEL ** -0.5),
        'b_ada': nrm(ks[9], (DEPTH, 3 * N_SUB * D_MODEL), 0.02),
        'norm_pre': 1.0 + nrm(ks[10], (DEPTH, N_SUB, D_MODEL), 0.1),
        'norm_post': 1.0 + nrm(ks[11], (DEPTH, N_SUB, D_MODEL), 0.1),
        'ffn_up': nrm(ks[12], (DEPTH, 2, D_MODEL, 2 * D_FF), D_MODEL ** -0.5),
        'ffn_down': nrm(ks[13], (DEPTH, 2, D_FF, D_MODEL), D_FF ** -0.5),
        'w_in': nrm(ks[14], (DEPTH, D_MODEL, IN_COLS), D_MODEL ** -0.5),
        'w_out': nrm(ks[15], (DEPTH, D_MODEL, D_MODEL), D_MODEL ** -0.5),
        'rwkv_mu': uni(ks[16], (DEPTH, A_COLS), 0.0, 1.0),
        'rwkv_w0': uni(ks[17], (DEPTH, D_A), -6.0, -1.0),
        'rwkv_w2': nrm(ks[18], (DEPTH, W_LORA, D_A), 0.5 * W_LORA ** -0.5),
        'rwkv_a0': nrm(ks[19], (DEPTH, D_A), 0.1),
        'rwkv_a2': nrm(ks[20], (DEPTH, A_LORA, D_A), A_LORA ** -0.5),
        'rwkv_g2': nrm(ks[21], (DEPTH, G_LORA, D_A), G_LORA ** -0.5),
        'rwkv_k_k': 0.85 + nrm(ks[22], (DEPTH, D_A), 0.05),
        'rwkv_k_a': 1.0 + nrm(ks[23], (DEPTH, D_A), 0.05),
        'rwkv_r_k': nrm(ks[24], (DEPTH, H_A, HD_A), 0.1),
        'rwkv_ln_w': 1.0 + nrm(ks[25], (DEPTH, D_A), 0.1),
        'rwkv_ln_b': nrm(ks[26], (DEPTH, D_A), 0.02),
        'gdn_conv': nrm(ks[27], (DEPTH, CONV_W, 3 * D_B), CONV_W ** -0.5),
        'gdn_a_log': jnp.log(uni(ks[28], (DEPTH, H_B), 1.0, 16.0)),
        'gdn_dt_bias': jnp.log(jnp.expm1(uni(ks[29], (DEPTH, H_B), 0.001, 0.1))),
        'gdn_norm_w': 1.0 + nrm(ks[30], (DEPTH, HD_B), 0.1),
    }

def reference(x_prompt, x_sample, c_prompt, c_sample, state_rwkv_shift, state_rwkv_wkv,
              state_gdn_conv, state_gdn_ssm, w_ada, b_ada, norm_pre, norm_post, ffn_up, ffn_down,
              w_in, w_out, rwkv_mu, rwkv_w0, rwkv_w2, rwkv_a0, rwkv_a2, rwkv_g2, rwkv_k_k,
              rwkv_k_a, rwkv_r_k, rwkv_ln_w, rwkv_ln_b, gdn_conv, gdn_a_log, gdn_dt_bias,
              gdn_norm_w):
    bp = x_prompt.shape[0]
    dt = x_prompt.dtype
    p_shift0 = jnp.zeros((bp, A_COLS), dt)
    p_wkv0 = jnp.zeros((bp, H_A, HD_A, HD_A), jnp.float32)
    p_conv0 = jnp.zeros((bp, CONV_W - 1, 3 * D_B), dt)
    p_ssm0 = jnp.zeros((bp, H_B, HD_B, HD_B), jnp.float32)
    yp, ys = x_prompt, x_sample
    ps_l, pw_l, pc_l, pm_l = [], [], [], []
    ss_l, sw_l, sc_l, sm_l = [], [], [], []
    for l in range(DEPTH):
        lp = (w_ada[l], b_ada[l], norm_pre[l], norm_post[l], ffn_up[l], ffn_down[l], w_in[l],
              w_out[l], rwkv_mu[l], rwkv_w0[l], rwkv_w2[l], rwkv_a0[l], rwkv_a2[l], rwkv_g2[l],
              rwkv_k_k[l], rwkv_k_a[l], rwkv_r_k[l], rwkv_ln_w[l], rwkv_ln_b[l], gdn_conv[l],
              gdn_a_log[l], gdn_dt_bias[l], gdn_norm_w[l])
        yp, ps, pw, pc, pm = decoder_layer(yp, c_prompt, p_shift0, p_wkv0, p_conv0, p_ssm0, *lp)
        ys, ss, sw, sc, sm = decoder_layer(ys, c_sample, state_rwkv_shift[l], state_rwkv_wkv[l],
                                           state_gdn_conv[l], state_gdn_ssm[l], *lp)
        ps_l.append(ps); pw_l.append(pw); pc_l.append(pc); pm_l.append(pm)
        ss_l.append(ss); sw_l.append(sw); sc_l.append(sc); sm_l.append(sm)
    return (yp, ys, jnp.stack(ps_l), jnp.stack(pw_l), jnp.stack(pc_l), jnp.stack(pm_l),
            jnp.stack(ss_l), jnp.stack(sw_l), jnp.stack(sc_l), jnp.stack(sm_l))


_drawn_inputs = setup_inputs


def setup_inputs(seed=0):
    import zlib

    import numpy as np

    out = dict(_drawn_inputs(seed))
    spreads = {}
    factors = {'rwkv_ln_b': 8.0}
    for name, (base, spread) in spreads.items():
        noise = np.random.default_rng([zlib.crc32(name.encode()), seed]).standard_normal(out[name].shape)
        drawn = base * np.exp(spread * noise) if base else spread * noise
        out[name] = __import__('jax').numpy.asarray(drawn.astype(out[name].dtype))
    for name, factor in factors.items():
        out[name] = (out[name] * factor).astype(out[name].dtype)
    return out
```

```python
from contextlib import ExitStack

import concourse.bass as bass
from concourse import mybir

F32 = mybir.dt.float32
ALU = mybir.AluOpType
ACT = mybir.ActivationFunctionType
AX_X = mybir.AxisListType.X

P = 128
DEPTH, D = 2, 1024
NT = D // P
NPR, NS = 256, 8
T = NPR + NS
C = 64
NC = NPR // C
NROW = NS + 1
H_A, HD_A = 16, 64
H_B, HD_B = 8, 128
A_COLS = 3 * D + 64 + 64 + 128
A_TILES = A_COLS // P
Q_COLS = 3 * D
Q_TILES = Q_COLS // P
AB_COL = A_COLS + Q_COLS
Z_COL = AB_COL + 2 * H_B
IN_COLS = Z_COL + D + 2 * D
D_FF = 2816
FT = D_FF // P
ADA_TILES = 9 * NT
FFN_RES = 0.5
RMS_EPS, L2A_EPS, L2B_EPS, GN_EPS = 1e-6, 1e-12, 1e-6, 6.4e-4
EXP_MHALF = 0.6065306597126334
RING = 4
SLOT = 2048
GRP = 4
UNITS = GRP * NC
HALVES = (slice(0, 64), slice(64, 128))


class Signal:

    def __init__(self, sem, step=1):
        self.sem, self.step = sem, step
        self.reset()

    def reset(self):
        self.posted, self.taken = 0, {}

    def one(self):
        self.posted += 1
        return self.step

    def all(self):
        return self.at(self.posted)

    def next(self, eng, n=1):
        self.taken[id(eng)] = self.taken.get(id(eng), 0) + n
        return self.at(self.taken[id(eng)])

    def at(self, n):
        assert n > 0
        return self.step * n


def weight_plan():
    plan = [("ada", n) for n in range(ADA_TILES // 2)]
    plan += [("up0", n) for n in range(FT)] + [("down0", n) for n in range(2 * NT)]
    plan += [("in", n) for n in range(AB_COL // 256)] + [("ab", 0)]
    plan += [("zg", n) for n in range((IN_COLS - Z_COL) // 256)]
    plan += [("lora", 0)] + [("out", n) for n in range(D // 256)]
    plan += [("up1", n) for n in range(FT)] + [("down1", n) for n in range(2 * NT)]
    return plan


BLOCKS = {"ada": 2, "up0": 2, "up1": 2, "down0": 1, "down1": 1, "in": 2, "ab": 2, "zg": 2, "lora": 3 * NT, "out": 2}


def build(nc, I, O):
    ctx = ExitStack()
    with ctx:
        ctx.enter_context(nc.allow_non_contiguous_dma(reason="two [8] vectors a layer"))

        def sb(name, *free):
            return ctx.enter_context(nc.sbuf_tensor(name, [P, *free], F32))

        signals = []

        def signal(name, step=1):
            s = Signal(ctx.enter_context(nc.semaphore(name)), step)
            signals.append(s)
            return s

        ident = sb("ident", P)
        ident64 = sb("ident64", 64)
        mean_all = sb("mean_all", P)
        ones_all = sb("ones_all", P)
        ones_half = sb("ones_half", P)
        strict = sb("strict", 64)
        incl = sb("incl", 64)
        level = sb("level", 6, 64)
        carry = sb("carry", T)
        delta = sb("delta", NS)
        epsc = sb("epsc", 4)
        xT = sb("xT", NT, T)
        h = sb("h", NT, T)
        y = sb("y", NT, T)
        c9 = sb("c9", NT, NROW)
        ring = sb("ring", RING, SLOT)
        BIG_A, BIG_Q = A_TILES * (T + 1), Q_TILES * (T + 3)
        BIG_Z = NT * T
        big = sb("big", BIG_A + BIG_Q + 3 * BIG_Z)

        def part(buf, at, *shape):
            n = 1
            for s in shape:
                n *= s
            v = buf[:, at:at + n]
            if len(shape) == 2:
                return v.rearrange("p (a b) -> p a b", a=shape[0])
            if len(shape) == 3:
                return v.rearrange("p (a b c) -> p a b c", a=shape[0], b=shape[1])
            return v

        pa = part(big, 0, A_TILES, T + 1)
        qk = part(big, BIG_A, Q_TILES, T + 3)
        zs = part(big, BIG_A + BIG_Q, NT, T)
        gates = part(big, BIG_A + BIG_Q + BIG_Z, 2 * NT, T)
        hid = part(big, 0, FT, T)
        sq_out = part(big, 0, NT, T)
        silu_g = part(big, FT * T, 2, T)
        mix = sb("mix", 8448)
        lt_all = part(mix, 0, UNITS, C)
        dm_all = part(mix, 1024, UNITS, C)
        pb_all = part(mix, 2048, UNITS, C)
        pk_all = part(mix, 3072, UNITS, C)
        vtok = part(mix, 4096, UNITS, C)
        ktok = part(mix, 5120, UNITS, C)
        btok = part(mix, 6144, UNITS, C)
        kdec_f = part(mix, 7168, GRP, NPR)
        m_st = part(mix, 8192, GRP, C)
        samp_s = part(mix, 0, 32, C)
        samp_t = part(mix, 2048, 32, C)
        prow = part(mix, 4096, 3, P)
        strow = part(mix, 4480, 8, P)
        last = part(mix, 4096, 6, P)
        g_lt = part(mix, 0, UNITS, C)
        g_at = part(mix, 1024, UNITS, C)
        g_kd = part(mix, 2048, 2, H_B, HD_B)
        g_bv = part(mix, 4096, 2, H_B, HD_B)
        g_s = part(mix, 6144, H_B, HD_B)
        g_w = part(mix, 7168, H_B, HD_B)
        g_vn = part(big, 0, H_B, HD_B)
        g_eg = part(big, 1024, NT, T)
        g_tmp = part(big, 1024 + NT * T, 6, T)
        g_row = part(big, 1024 + (NT + 6) * T, 8, T)
        inv = sb("inv", 4, UNITS, C)
        t_all, x_all, ltb, tt_all = (inv[:, n] for n in range(4))
        inv_f = inv[:, :, :, :].rearrange("p a b c -> p (a b c)")
        e2 = part(inv_f, 0, 2, T)
        lw = part(inv_f, 528, T)
        gc_i = part(inv_f, 792, T)
        e_x = part(inv_f, 1056, T)
        e_g = part(inv_f, 1320, T)
        e_n = part(inv_f, 1584, T)
        kkn = part(inv_f, 1848, T)
        b_f = part(inv_f, 2112, T)
        kd_f = part(inv_f, 2376, T)
        rkk = part(inv_f, 2640, T)
        sq_t = part(inv_f, 2904, T)
        rs_t = part(inv_f, 3168, T)
        kb_t = part(inv_f, 3432, T)
        last_c = part(inv_f, 0, 498)
        convs = part(inv_f, 512, Q_TILES, NS)
        convt = part(inv_f, 704, Q_TILES, NS)
        rs2 = part(inv_f, 896, T)
        ws_a, us_a, mo_a = x_all[:, 0:GRP], x_all[:, GRP:2 * GRP], x_all[:, 2 * GRP:3 * GRP]
        gs_s = [part(inv_f, 1024 * n, NS, HD_B) for n in range(2)]
        gs_x = part(inv_f, 2048, NS, HD_B)
        sgt = part(inv_f, 3072, 2, P)
        rs = sb("rs", T)
        pcol = sb("pcol", 3 * P)
        ncol = sb("ncol", 3 * NT)
        modv = sb("modv", ADA_TILES, NROW)
        mod_a = sb("mod_a", 3 * NT, NROW)
        mod_g = sb("mod_g", 3 * NT, NROW)
        shp = sb("shp", A_TILES, NS)
        cvp = sb("cvp", Q_TILES, 3 * NS)
        sv = sb("sv", 6, NS, NT)
        svt = sb("svt", 6, C)
        ssm = sb("ssm", 2, C)
        eg_end = sb("eg_end", NT, NC)
        adt = sb("adt", 2)
        tks = sb("tks", 2, 4, H_B)
        abr = sb("abr", 2, T)
        beta_s = sb("beta_s", H_B, NS)
        qk_s = sb("qk_s", H_B, NS)
        sg = sb("sg", 4, NS)

        banks = [ctx.enter_context(nc.psum_tensor(f"bank{n}", [P, 512], F32)) for n in range(8)]

        bada = pcol[:, 0:72]
        npre, npost = pcol[:, 72:96], pcol[:, 96:120]
        mu = pcol[:, 128:154]
        w0, a0, k_k, k_a, r_k, ln_w, ln_b = (pcol[:, 154 + 8 * n:162 + 8 * n] for n in range(7))
        g_nw = pcol[:, 210:211]
        convw = pcol[:, 256:352].rearrange("p (i j) -> p i j", i=4)

        w_in_slot = [signal(f"w_in_slot{n}", 16) for n in range(RING)]
        lin_done = signal("lin_done")
        rows_in = signal("rows_in", 16)
        masks_in = signal("masks_in", 16)
        consts = signal("consts")
        tr_done = signal("tr_done")
        cols_ready = signal("cols_ready")
        mod_ready = signal("mod_ready")
        x_ready = signal("x_ready")
        sq_ready = signal("sq_ready")
        ss_done = signal("ss_done")
        rs_ready = signal("rs_ready")
        h_ready = signal("h_ready")
        gate_taken = signal("gate_taken")
        hid_ready = signal("hid_ready")
        out_taken = signal("out_taken")
        pads = signal("pads")
        shifted = signal("shifted")
        conv_ready = signal("conv_ready")
        conv_done = signal("conv_done")
        last_tr = signal("last_tr")
        last_cp = signal("last_cp")
        st_out = signal("st_out", 16)
        kksq = signal("kksq")
        kkrs = signal("kkrs")
        ew_ready = signal("ew_ready")
        kkss = signal("kkss")
        bonss = signal("bonss")
        g_ready = signal("g_ready")
        eg_ready = signal("eg_ready")
        rkk_ready = signal("rkk_ready")
        ops_ready = signal("ops_ready")
        prod_done = signal("prod_done")
        prod_act = signal("prod_act")
        prod_dve = signal("prod_dve")
        bon_taken = signal("bon_taken")
        inv_pe = signal("inv_pe")
        inv_x = signal("inv_x")
        inv_t = signal("inv_t")
        m_ready = signal("m_ready")
        seq_pe = signal("seq_pe")
        seq_act = signal("seq_act")
        seq_dve = signal("seq_dve")
        sv_ready = signal("sv_ready")
        sv_pe = signal("sv_pe")
        svt_ready = signal("svt_ready")
        samp_in = signal("samp_in", 16)
        samp_done = signal("samp_done")
        samp_out = signal("samp_out", 16)
        gs_in = [signal(f"gs_in{n}", 16) for n in range(2)]
        gs_out = [signal(f"gs_out{n}", 16) for n in range(2)]
        ys_done = signal("ys_done")
        post_pe = signal("post_pe")
        post_act = signal("post_act")
        post_dve = signal("post_dve")
        lora_in = signal("lora_in")
        merged = signal("merged")
        rows_ready = signal("rows_ready")
        gdn_pe = signal("gdn_pe")
        gdn_act = signal("gdn_act")
        gdn_dve = signal("gdn_dve")
        last_rd = signal("last_rd")
        gdn_rows_a = signal("gdn_rows_a")
        gdn_rows_d = signal("gdn_rows_d")
        gdn_ra = signal("gdn_ra")
        gdn_rd = signal("gdn_rd")
        act_chain = signal("act_chain")
        dve_chain = signal("dve_chain")
        pool_chain = signal("pool_chain")

        def end_of_part():
            nums = sorted(s.sem.num for s in signals)
            assert nums == list(range(nums[0], nums[-1] + 1))
            nc.all_engine_barrier()
            nc.gpsimd.sem_clear(range(nums[0], nums[-1] + 1))
            nc.all_engine_barrier()
            for s in signals:
                s.reset()

        def bc(ap, n):
            return ap.unsqueeze(2).to_broadcast([ap.shape[0], ap.shape[1], n])

        def bm(ap, n):
            return ap.unsqueeze(1).to_broadcast([ap.shape[0], n, ap.shape[1]])


        INV_PE, INV_ACT, INV_DVE = 2 + 4 * 5, 2 + 2 * 5, 1 + 3 * 5

        def inv_tiles(run):
            return g_lt if run == 2 else lt_all

        def batch(bt):
            return slice(8 * bt, 8 * bt + 8)

        def invert(pe, run):
            p0, a0_, d0 = run * INV_PE, run * INV_ACT, run * INV_DVE

            def products(bank, bt, lhs, rhs):
                for u in range(8):
                    for hf in HALVES:
                        r = ident64[hf, :] if rhs is None else rhs[hf, 8 * bt + u, :]
                        i = pe.matmul(banks[bank][hf, u * C:(u + 1) * C], lhs[hf, 8 * bt + u, :], r, start=True, stop=True)
                return i

            pe.wait_ge(inv_t.sem, inv_t.at(d0 + 1))
            for bt in range(2):
                products(4 + bt, bt, tt_all, None).then_inc(inv_pe.sem, inv_pe.one())
            for n in range(1, 6):
                for bt in range(2):
                    if n == 1:
                        pe.wait_ge(inv_t.sem, inv_t.at(d0 + 2))
                        pe.wait_ge(inv_x.sem, inv_x.at(a0_ + 1 + bt))
                    else:
                        pe.wait_ge(inv_t.sem, inv_t.at(d0 + 2 + 3 * (n - 2) + 2 + bt))
                    products(bt, bt, ltb, t_all).then_inc(inv_pe.sem, inv_pe.one())
                for bt in range(2):
                    pe.wait_ge(inv_x.sem, inv_x.at(a0_ + 2 * n + 1 + bt))
                    i = products(2 + bt, bt, x_all, tt_all)
                    if n < 5:
                        i = products(4 + bt, bt, tt_all, x_all)
                    i.then_inc(inv_pe.sem, inv_pe.one())
            pe.wait_ge(inv_t.sem, inv_t.at(d0 + INV_DVE))

        def invert_act(act, run):
            p0 = run * INV_PE
            for n in range(6):
                for bt in range(2):
                    dst, bank, at = (t_all, 4 + bt, 1 + bt) if n == 0 else (x_all, bt, 2 + 4 * (n - 1) + 1 + bt)
                    act.wait_ge(inv_pe.sem, inv_pe.at(p0 + at))
                    act.copy(dst[:, batch(bt), :], banks[bank][:, :].rearrange("p (u t) -> p u t", u=8)).then_inc(inv_x.sem, inv_x.one())
                    act.wait_ge(inv_x.sem, inv_x.all())

        def invert_dve(dve, run):
            p0, lt = run * INV_PE, inv_tiles(run)
            dve.tensor_tensor(ltb, lt, bm(level[:, 0, :], UNITS), ALU.mult).then_inc(dve_chain.sem, dve_chain.one())
            dve.wait_ge(dve_chain.sem, dve_chain.all())
            dve.tensor_tensor(tt_all, bm(ident64[:, :], UNITS), ltb, ALU.subtract).then_inc(inv_t.sem, inv_t.one())
            dve.wait_ge(inv_t.sem, inv_t.all())
            dve.tensor_tensor(ltb, lt, bm(level[:, 1, :], UNITS), ALU.mult).then_inc(inv_t.sem, inv_t.one())
            dve.wait_ge(inv_t.sem, inv_t.all())
            for n in range(1, 6):
                if n < 5:
                    dve.wait_ge(inv_pe.sem, inv_pe.at(p0 + 2 + 4 * (n - 1) + 2))
                    dve.tensor_tensor(ltb, lt, bm(level[:, n + 1, :], UNITS), ALU.mult).then_inc(inv_t.sem, inv_t.one())
                    dve.wait_ge(inv_t.sem, inv_t.all())
                for bt in range(2):
                    dve.wait_ge(inv_pe.sem, inv_pe.at(p0 + 2 + 4 * (n - 1) + 3 + bt))
                    us = batch(bt)
                    bank = [banks[2 * g + 2 + bt][:, :].rearrange("p (u t) -> p u t", u=8) for g in range(2)]
                    i = dve.tensor_tensor(tt_all[:, us, :], tt_all[:, us, :], bank[0], ALU.subtract)
                    if n < 5:
                        i = dve.tensor_tensor(t_all[:, us, :], t_all[:, us, :], bank[1], ALU.subtract)
                    i.then_inc(inv_t.sem, inv_t.one())
                    dve.wait_ge(inv_t.sem, inv_t.all())

        LAST = ((0, 26), (26, 104), (130, 104), (234, 72), (306, 96), (402, 96))
        GD_SEQ = H_B + 1 + 2 * NC
        GP_SAMP = 1 + 2 * H_B + 4 * NC + 1
        GP_POST = GP_SAMP + 3 * H_B

        with nc.Block() as block:
            @block.sync
            def _(sp):
                sp.dma_start(ring[:, 0, :].rearrange("p (a f) -> p a f", a=2),
                                          I["x_prompt"][0].rearrange("(a p) f -> p a f", p=P)).then_inc(rows_in.sem, rows_in.one())
                sp.dma_start(ring[0:8, 1, 0:P], I["c_prompt"].rearrange("b (j f) -> (b j) f", f=P)).then_inc(rows_in.sem, rows_in.one())
                sp.dma_start(ring[8:72, 1, 0:P], I["c_sample"].rearrange("b (j f) -> (b j) f", f=P)).then_inc(rows_in.sem, rows_in.one())
                sp.dma_start(ring[0:64, 1, P:2 * P],
                                          I["x_sample"].rearrange("b a (j f) -> (b a j) f", f=P)).then_inc(rows_in.sem, rows_in.one())

            @block.gpsimd
            def _(pool):
                for buf, value in ((ident, 0.0), (mean_all, 1.0 / D), (ones_all, 1.0), (ones_half, 0.0),
                                   (strict, 1.0), (incl, 1.0), (delta, 0.0)):
                    pool.memset(buf[:, :], value).then_inc(pool_chain.sem, pool_chain.one())
                    pool.wait_ge(pool_chain.sem, pool_chain.all())
                pool.memset(carry[:, :], 1.0).then_inc(pool_chain.sem, pool_chain.one())
                pool.wait_ge(pool_chain.sem, pool_chain.all())
                pool.memset(carry[:, 0:NPR].rearrange("p (c t) -> p c t", t=C)[:, :, 0:1], 0.0).then_inc(pool_chain.sem, pool_chain.one())
                pool.wait_ge(pool_chain.sem, pool_chain.all())
                pool.memset(carry[:, NPR:T], 0.0).then_inc(pool_chain.sem, pool_chain.one())
                pool.wait_ge(pool_chain.sem, pool_chain.all())
                pool.memset(level[:, :, :], 0.0).then_inc(pool_chain.sem, pool_chain.one())
                pool.wait_ge(pool_chain.sem, pool_chain.all())
                for n, value in enumerate((RMS_EPS, L2A_EPS, GN_EPS, 1.0)):
                    pool.memset(epsc[:, n:n + 1], value).then_inc(pool_chain.sem, pool_chain.one())
                    pool.wait_ge(pool_chain.sem, pool_chain.all())
                for half in HALVES:
                    pool.memset(ones_half[half, half], 1.0).then_inc(pool_chain.sem, pool_chain.one())
                    pool.wait_ge(pool_chain.sem, pool_chain.all())

                def select(v, pattern, base, mult, op, fill):
                    pool.affine_select(out=v, in_=v, pattern=pattern, base=base, channel_multiplier=mult,
                                       compare_op=op, fill=fill).then_inc(pool_chain.sem, pool_chain.one())
                    pool.wait_ge(pool_chain.sem, pool_chain.all())

                select(ident[:, :], [[-1, P]], 0, 1, ALU.not_equal, 1.0)
                select(delta[0:NS, :], [[-1, NS]], 0, 1, ALU.not_equal, 1.0)
                select(strict[0:64, :], [[1, 64]], 0, -1, ALU.is_gt, 0.0)
                select(incl[0:64, :], [[1, 64]], 0, -1, ALU.is_ge, 0.0)
                for n in range(6):
                    b = 1 << n
                    v = level[0:64, n, :].rearrange("p (a h t) -> p a h t", h=2, t=b)[:, :, 1, :]
                    pool.memset(v, 1.0).then_inc(pool_chain.sem, pool_chain.one())
                    pool.wait_ge(pool_chain.sem, pool_chain.all())
                    select(v, [[-2 * b, 32 // b], [0, b]], 0, 1, ALU.is_ge, 0.0)
                    select(v, [[2 * b, 32 // b], [0, b]], b - 1, -1, ALU.is_ge, 0.0)
                pool.memset(epsc[:, 3:4], 1.0).then_inc(consts.sem, consts.one())

            @block.tensor
            def _(pe):
                pe.wait_ge(rows_in.sem, rows_in.at(4))
                pe.wait_ge(consts.sem, consts.next(pe))
                for a in range(2):
                    for j in range(NT):
                        n = a * NT + j
                        tr = pe.transpose(banks[n // 4][:, (n % 4) * P:(n % 4 + 1) * P],
                                          ring[:, 0, a * D + j * P:a * D + (j + 1) * P], ident[:, :])
                pe.transpose(banks[4][:, 0:72], ring[0:72, 1, 0:P], ident[0:72, 0:72])
                tr = pe.transpose(banks[5][:, 0:64], ring[0:64, 1, P:2 * P], ident[0:64, 0:64])
                tr.then_inc(tr_done.sem, tr_done.one())

            @block.scalar
            def _(act):
                act.wait_ge(consts.sem, consts.next(act))
                for buf in (strict, incl):
                    act.dma_start(buf[64:128, :], buf[0:64, :]).then_inc(masks_in.sem, masks_in.one())
                act.dma_start(level[64:128, :, :], level[0:64, :, :]).then_inc(masks_in.sem, masks_in.one())
                act.wait_ge(masks_in.sem, masks_in.next(act, 3))
                act.wait_ge(tr_done.sem, tr_done.next(act))
                for n in range(4):
                    a, j = n // 2, 4 * (n % 2)
                    act.copy(xT[:, j:j + 4, a * P:(a + 1) * P], banks[n][:, :].rearrange("p (j t) -> p j t", j=4))
                act.copy(xT[:, :, NPR:T], banks[5][:, 0:64].rearrange("p (b j) -> p j b", j=NT))
                act.activation(c9[:, :, :], banks[4][:, 0:72].rearrange("p (r j) -> p j r", j=NT), ACT.Silu)

            @block.vector
            def _(dve):
                dve.wait_ge(consts.sem, consts.next(dve))
                dve.tensor_tensor(ident64[:, :], ident[:, 0:64], ident[:, 64:128], ALU.add)

        end_of_part()

        with nc.Fori(0, DEPTH) as l:
            plan = weight_plan()
            where, done_by, blocks = {}, {}, 0
            for n, key in enumerate(plan):
                where[key] = n
                blocks += BLOCKS[key[0]]
                done_by[n] = blocks

            with nc.Block() as block:
                @block.sync
                def _(sp):
                    def k_tiles(w, c0, n):
                        return w[l, :, c0:c0 + n].rearrange("(k p) n -> p k n", p=P)

                    for n, (kind, t) in enumerate(plan):
                        slot = ring[:, n % RING, :]
                        full = slot.rearrange("p (k n) -> p k n", k=NT)
                        into = w_in_slot[n % RING]
                        if n >= RING:
                            sp.wait_ge(lin_done.sem, lin_done.at(done_by[n - RING]))
                        if kind == "ada":
                            sp.dma_start(full, k_tiles(I["w_ada"], 256 * t, 256)).then_inc(into.sem, into.one())
                        elif kind in ("up0", "up1"):
                            w = I["ffn_up"][l, int(kind[2])]
                            for g in range(2):
                                c0 = g * D_FF + t * P
                                sp.dma_start(
                                    slot.rearrange("p (g k n) -> p g k n", g=2, k=NT)[:, g],
                                    w[:, c0:c0 + P].rearrange("(k p) n -> p k n", p=P)).then_inc(into.sem, into.one())
                        elif kind in ("down0", "down1"):
                            w = I["ffn_down"][l, int(kind[4])]
                            o, kh = t // 2, t % 2
                            sp.dma_start(
                                slot[:, 0:FT // 2 * P].rearrange("p (k n) -> p k n", n=P),
                                w[kh * D_FF // 2:(kh + 1) * D_FF // 2, o * P:(o + 1) * P]
                                .rearrange("(k p) n -> p k n", p=P)).then_inc(into.sem, into.one())
                        elif kind == "in":
                            sp.dma_start(full, k_tiles(I["w_in"], 256 * t, 256)).then_inc(into.sem, into.one())
                        elif kind == "ab":
                            sp.dma_start(slot[:, 0:NT * 16].rearrange("p (k n) -> p k n", k=NT),
                                                   k_tiles(I["w_in"], AB_COL, 16)).then_inc(into.sem, into.one())
                        elif kind == "zg":
                            sp.dma_start(full, k_tiles(I["w_in"], Z_COL + 256 * t, 256)).then_inc(into.sem, into.one())
                        elif kind == "lora":
                            sp.dma_start(slot[0:64, 0:D], I["rwkv_w2"][l]).then_inc(into.sem, into.one())
                            sp.dma_start(slot[64:128, 0:D], I["rwkv_a2"][l]).then_inc(into.sem, into.one())
                            sp.dma_start(slot[:, D:2 * D], I["rwkv_g2"][l]).then_inc(into.sem, into.one())
                        elif kind == "out":
                            sp.dma_start(full, k_tiles(I["w_out"], 256 * t, 256)).then_inc(into.sem, into.one())

                @block.tensor
                def _(pe):
                    def mm(out, lhsT, rhs, start=True, stop=True):
                        return pe.matmul(out, lhsT, rhs, start=start, stop=stop)

                    def slot_of(kind, t):
                        n = where[(kind, t)]
                        s = w_in_slot[n % RING]
                        upto = sum(3 if k == "lora" else 2 if k[:2] == "up" else 1
                                   for m, (k, _) in enumerate(plan[:n + 1]) if m % RING == n % RING)
                        pe.wait_ge(s.sem, s.at(upto))
                        return ring[:, n % RING, :]

                    pe.wait_ge(rows_in.sem, rows_in.at(17))
                    for g, rows in enumerate((120, 83, 96)):
                        pe.transpose(banks[6][:, g * P:g * P + rows], prow[0:rows, g, :], ident[0:rows, 0:rows])
                    for n in range(2):
                        pe.transpose(banks[7][:, n * 104:(n + 1) * 104], strow[0:104, n, :], ident[0:104, 0:104])
                    for n in range(6):
                        out = banks[7][:, 208 + n * 96:304 + n * 96] if n < 3 else banks[3][:, (n - 3) * 96:(n - 2) * 96]
                        tr = pe.transpose(out, strow[0:96, 2 + n, :], ident[0:96, 0:96])
                    tr.then_inc(tr_done.sem, tr_done.one())

                    for t in range(ADA_TILES // 2):
                        w = slot_of("ada", t).rearrange("p (k n) -> p k n", k=NT)
                        for o in range(2):
                            m = 2 * t + o
                            out = banks[4 + m // 36][:, (m % 36) * NROW:(m % 36 + 1) * NROW]
                            for k in range(NT):
                                i = mm(out, w[:, k, o * P:(o + 1) * P], c9[:, k, :], k == 0, k == NT - 1)
                            i.then_inc(lin_done.sem, lin_done.one())

                    def mean_square():
                        pe.wait_ge(sq_ready.sem, sq_ready.next(pe))
                        for k in range(NT):
                            i = mm(banks[7][:, 0:T], mean_all[:, :], h[:, k, :], k == 0, k == NT - 1)
                        i.then_inc(ss_done.sem, ss_done.one())

                    def mean_square_tiles(buf):
                        for k in range(NT):
                            pe.wait_ge(sq_ready.sem, sq_ready.next(pe))
                            i = mm(banks[7][:, 0:T], mean_all[:, :], buf[:, k, :], k == 0, k == NT - 1)
                        i.then_inc(ss_done.sem, ss_done.one())

                    def ffn(i_ffn):
                        mean_square()
                        pe.wait_ge(h_ready.sem, h_ready.next(pe))
                        for t in range(FT):
                            w = slot_of(f"up{i_ffn}", t).rearrange("p (g k n) -> p g k n", g=2, k=NT)
                            for g in range(2):
                                if t >= 2:
                                    read = gate_taken if g == 0 else hid_ready
                                    pe.wait_ge(read.sem, read.at(i_ffn * FT + t - 1))
                                for k in range(NT):
                                    i = mm(banks[2 * g + t % 2][:, 0:T], w[:, g, k, :], h[:, k, :], k == 0, k == NT - 1)
                                i.then_inc(lin_done.sem, lin_done.one())
                        pe.wait_ge(hid_ready.sem, hid_ready.at((i_ffn + 1) * FT))
                        base = 0 if i_ffn == 0 else out_base[1]
                        for o in range(NT):
                            if o >= 4:
                                pe.wait_ge(out_taken.sem, out_taken.at(base + o - 3))
                            for kh in range(2):
                                w = slot_of(f"down{i_ffn}", 2 * o + kh)[:, 0:FT // 2 * P].rearrange("p (k n) -> p k n", n=P)
                                for k in range(FT // 2):
                                    kk = kh * FT // 2 + k
                                    i = mm(banks[o % 4][:, 0:T], w[:, k, :], hid[:, kk, :], kk == 0, kk == FT - 1)
                                i.then_inc(lin_done.sem, lin_done.one())
                        mean_square_tiles(h)

                    pe.wait_ge(cols_ready.sem, cols_ready.next(pe))
                    out_base = (0, NT + A_TILES + Q_TILES + 2 + 3 * NT + NT)
                    ffn(0)

                    mean_square()
                    pe.wait_ge(h_ready.sem, h_ready.next(pe))
                    pe.wait_ge(pads.sem, pads.next(pe))
                    n_out = 0
                    base = NT
                    for kind, count in (("in", AB_COL // 256), ("ab", 1), ("zg", (IN_COLS - Z_COL) // 256)):
                        for t in range(count):
                            s = slot_of(kind, t)
                            for o in range(2):
                                pe.wait_ge(out_taken.sem, out_taken.at(base + n_out - 3))
                                if kind == "ab":
                                    w = s[:, 0:NT * 16].rearrange("p (k n) -> p k n", k=NT)
                                    out, cols = banks[n_out % 4][0:8, 0:T], slice(8 * o, 8 * o + 8)
                                else:
                                    w = s.rearrange("p (k n) -> p k n", k=NT)
                                    out, cols = banks[n_out % 4][:, 0:T], slice(o * P, (o + 1) * P)
                                for k in range(NT):
                                    i = mm(out, w[:, k, cols], h[:, k, :], k == 0, k == NT - 1)
                                i.then_inc(lin_done.sem, lin_done.one())
                                n_out += 1

                    pe.wait_ge(last_cp.sem, last_cp.next(pe, 2))
                    for n, (at, count) in enumerate(LAST):
                        i = pe.transpose(banks[4 + n // 4][0:count, (n % 4) * P:(n % 4 + 1) * P],
                                         last_c[:, at:at + count], ident[:, :])
                    i.then_inc(last_tr.sem, last_tr.one())
                    pe.wait_ge(last_rd.sem, last_rd.next(pe))

                    lora = slot_of("lora", 0)
                    pe.wait_ge(lora_in.sem, lora_in.next(pe))
                    for q in range(NT // GRP):
                        for jj in range(GRP):
                            j = GRP * q + jj
                            mm(banks[0][:, 0:T], lora[0:64, j * P:(j + 1) * P], pa[0:64, 24, 1:T + 1]).then_inc(lin_done.sem, lin_done.one())
                            mm(banks[1][:, 0:T], lora[64:128, j * P:(j + 1) * P], pa[64:128, 24, 1:T + 1]).then_inc(lin_done.sem, lin_done.one())
                            pe.wait_ge(kksq.sem, kksq.next(pe))
                            mm(banks[2][:, 0:T], ones_half[:, :], sq_t).then_inc(kkss.sem, kkss.one())
                            pe.wait_ge(rkk_ready.sem, rkk_ready.next(pe))
                            mm(banks[3][:, 0:T], ones_half[:, :], rkk).then_inc(bonss.sem, bonss.one())
                            pe.wait_ge(ops_ready.sem, ops_ready.next(pe))
                            if j:
                                pe.wait_ge(prod_act.sem, prod_act.at(j))
                                pe.wait_ge(prod_dve.sem, prod_dve.at(j))
                            for c in range(NC):
                                t0, u0 = c * C, c * C
                                for hf in HALVES:
                                    kt = kdec_f[hf, jj, t0:t0 + C]
                                    rt = pa[hf, j, 1 + t0:1 + t0 + C]
                                    mm(banks[4][hf, u0:u0 + C], b_f[hf, t0:t0 + C], kt)
                                    mm(banks[4][hf, 256 + u0:256 + u0 + C], b_f[hf, t0:t0 + C], rt)
                                    mm(banks[5][hf, u0:u0 + C], kd_f[hf, t0:t0 + C], kt)
                                    mm(banks[5][hf, 256 + u0:256 + u0 + C], kd_f[hf, t0:t0 + C], rt)
                                    mm(banks[6][hf, u0:u0 + C], pa[hf, 16 + j, 1 + t0:1 + t0 + C], ident64[hf, :])
                                    mm(banks[6][hf, 256 + u0:256 + u0 + C], kd_f[hf, t0:t0 + C], ident64[hf, :])
                                    i = mm(banks[7][hf, u0:u0 + C], b_f[hf, t0:t0 + C], ident64[hf, :])
                            i.then_inc(prod_done.sem, prod_done.one())
                        pe.wait_ge(prod_act.sem, prod_act.at(GRP * (q + 1)))
                        pe.wait_ge(prod_dve.sem, prod_dve.at(GRP * (q + 1)))
                        invert(pe, q)
                        for c in range(NC):
                            t0 = c * C
                            pe.wait_ge(seq_dve.sem, seq_dve.next(pe))
                            for jj in range(GRP):
                                u = jj * NC + c
                                for hf in HALVES:
                                    out = banks[0][hf, jj * C:(jj + 1) * C]
                                    mm(out, kdec_f[hf, jj, t0:t0 + C], m_st[hf, jj, :], True, False)
                                    i = mm(out, dm_all[hf, u, :], vtok[hf, u, :], False, True)
                            i.then_inc(seq_pe.sem, seq_pe.one())
                            pe.wait_ge(seq_act.sem, seq_act.next(pe))
                            for jj in range(GRP):
                                for hf in HALVES:
                                    i = mm(banks[1][hf, jj * C:(jj + 1) * C], tt_all[hf, jj * NC + c, :], ws_a[hf, jj, :])
                            i.then_inc(seq_pe.sem, seq_pe.one())
                            pe.wait_ge(seq_act.sem, seq_act.next(pe))
                            for jj in range(GRP):
                                u, j = jj * NC + c, GRP * q + jj
                                for hf in HALVES:
                                    out = banks[2][hf, jj * C:(jj + 1) * C]
                                    mm(out, m_st[hf, jj, :], pa[hf, j, 1 + t0:1 + t0 + C], True, False)
                                    mm(out, us_a[hf, jj, :], pb_all[hf, u, :], False, False)
                                    i = mm(out, vtok[hf, u, :], pk_all[hf, u, :], False, True)
                            i.then_inc(seq_pe.sem, seq_pe.one())
                            for jj in range(GRP):
                                u = jj * NC + c
                                for hf in HALVES:
                                    out = banks[3][hf, jj * C:(jj + 1) * C]
                                    mm(out, btok[hf, u, :], us_a[hf, jj, :], True, False)
                                    i = mm(out, ktok[hf, u, :], vtok[hf, u, :], False, True)
                            i.then_inc(seq_pe.sem, seq_pe.one())
                        pe.wait_ge(seq_dve.sem, seq_dve.next(pe))
                        for jj in range(GRP):
                            for hf in HALVES:
                                i = mm(banks[0][hf, jj * C:(jj + 1) * C], m_st[hf, jj, :], ident64[hf, :])
                        i.then_inc(seq_pe.sem, seq_pe.one())
                        pe.wait_ge(seq_act.sem, seq_act.next(pe))

                    for n in range(6):
                        for hf in HALVES:
                            i = mm(banks[4][hf, n * C:(n + 1) * C],
                                   sv[hf, n, :, :].rearrange("p b j -> p (b j)"), ident64[hf, :])
                    i.then_inc(sv_pe.sem, sv_pe.one())
                    pe.wait_ge(samp_done.sem, samp_done.next(pe, 2))
                    for hf in HALVES:
                        i = mm(banks[5][hf, 0:64], ssm[hf, 1, :], ident64[hf, :])
                    i.then_inc(sv_pe.sem, sv_pe.one())
                    pe.wait_ge(ys_done.sem, ys_done.next(pe))

                    for j in range(NT):
                        if j:
                            pe.wait_ge(post_dve.sem, post_dve.next(pe))
                        mm(banks[0][:, 0:T], ones_half[:, :], h[:, j, :]).then_inc(post_pe.sem, post_pe.one())
                        mm(banks[2][:, 0:T], lora[:, D + j * P:D + (j + 1) * P], pa[:, 25, 1:T + 1]).then_inc(lin_done.sem, lin_done.one())
                        pe.wait_ge(post_act.sem, post_act.at(2 * j + 1))
                        mm(banks[1][:, 0:T], ones_half[:, :], sq_t).then_inc(post_pe.sem, post_pe.one())
                        pe.wait_ge(post_dve.sem, post_dve.next(pe))
                    pe.wait_ge(post_dve.sem, post_dve.next(pe))

                    pe.wait_ge(rows_ready.sem, rows_ready.next(pe))
                    for a in range(2):
                        for n, r in enumerate((0, 1, 2, 7)):
                            i = pe.transpose(banks[7][:, (a * 4 + n) * H_B:(a * 4 + n + 1) * H_B],
                                             g_row[0:H_B, r, a * P:(a + 1) * P], ident[0:H_B, 0:H_B])
                    i.then_inc(gdn_pe.sem, gdn_pe.one())
                    for n in range(H_B):
                        pe.wait_ge(gdn_act.sem, gdn_act.next(pe))
                        if n:
                            pe.wait_ge(gdn_dve.sem, gdn_dve.next(pe))
                        mm(banks[0][:, 0:T], ones_all[:, :], g_tmp[:, 0, :])
                        mm(banks[1][:, 0:T], ones_all[:, :], g_tmp[:, 1, :])
                        head = ident[0:H_B, n:n + 1].to_broadcast([H_B, P])
                        mm(banks[2][:, 0:T], head, g_row[0:H_B, 0, :])
                        mm(banks[3][:, 0:T], head, g_row[0:H_B, 1, :]).then_inc(gdn_pe.sem, gdn_pe.one())
                        pe.wait_ge(gdn_rd.sem, gdn_rd.next(pe))
                        for c in range(NC):
                            hf, cp = HALVES[c % 2], c // 2
                            k_c = qk[:, 8 + n, 3 + c * C:3 + (c + 1) * C]
                            mm(banks[4][hf, cp * C:(cp + 1) * C], k_c, g_tmp[:, 2, c * C:(c + 1) * C])
                            mm(banks[4][hf, 128 + cp * C:128 + (cp + 1) * C], k_c, qk[:, n, 3 + c * C:3 + (c + 1) * C])
                        for cp in range(2):
                            pe.transpose(banks[5][:, cp * P:(cp + 1) * P], qk[:, 8 + n, 3 + cp * P:3 + (cp + 1) * P], ident[:, :])
                            i = pe.transpose(banks[5][:, 256 + cp * P:256 + (cp + 1) * P],
                                             qk[:, 16 + n, 3 + cp * P:3 + (cp + 1) * P], ident[:, :])
                        i.then_inc(gdn_pe.sem, gdn_pe.one())
                    pe.wait_ge(gdn_dve.sem, gdn_dve.next(pe))
                    invert(pe, 2)
                    for c in range(NC):
                        hf, cp = HALVES[c % 2], c // 2
                        pe.wait_ge(gdn_dve.sem, gdn_dve.next(pe))
                        for n in range(H_B):
                            i = mm(banks[n // 4][hf, (n % 4) * P:(n % 4 + 1) * P], qk[:, 8 + n, 3 + c * C:3 + (c + 1) * C], g_s[:, n, :])
                        i.then_inc(gdn_pe.sem, gdn_pe.one())
                        pe.wait_ge(gdn_dve.sem, gdn_dve.next(pe))
                        for n in range(H_B):
                            i = mm(banks[2 + n // 4][hf, (n % 4) * P:(n % 4 + 1) * P], tt_all[hf, 2 * n + cp, :], g_w[hf, n, :])
                        i.then_inc(gdn_pe.sem, gdn_pe.one())
                        pe.wait_ge(gdn_act.sem, gdn_act.next(pe))
                        for n in range(H_B):
                            out = banks[4][:, n * C:(n + 1) * C]
                            mm(out, g_s[:, n, :], qk[:, n, 3 + c * C:3 + (c + 1) * C], True, False)
                            i = mm(out, g_vn[hf, n, :], g_at[hf, 2 * n + cp, :], False, True)
                        i.then_inc(gdn_pe.sem, gdn_pe.one())
                        for n in range(H_B):
                            i = mm(banks[5 + n // 4][:, (n % 4) * P:(n % 4 + 1) * P], g_kd[hf, cp, n, :], g_vn[hf, n, :])
                        i.then_inc(gdn_pe.sem, gdn_pe.one())
                    pe.wait_ge(gdn_dve.sem, gdn_dve.next(pe))
                    mm(banks[7][:, 0:64], ones_all[:, :], qk_s[:, :, :].rearrange("p n b -> p (n b)")).then_inc(gdn_pe.sem, gdn_pe.one())
                    pe.wait_ge(gdn_dve.sem, gdn_dve.next(pe))
                    for n in range(H_B):
                        pe.wait_ge(gs_in[n % 2].sem, gs_in[n % 2].next(pe))
                        for b in range(NS):
                            i = mm(banks[0][:, 2 * b:2 * b + 2], gs_s[n % 2][:, b, :], qk[:, n:n + 9:8, 259 + b])
                        i.then_inc(gdn_pe.sem, gdn_pe.one())
                        pe.wait_ge(gdn_dve.sem, gdn_dve.next(pe))
                        pe.transpose(banks[1][0:NS, 0:P], sg[:, 1, :], ident[:, :])
                        pe.transpose(banks[1][0:NS, P:2 * P], qk[:, 8 + n, 259:267], ident[:, :]).then_inc(gdn_pe.sem, gdn_pe.one())
                        pe.wait_ge(gdn_dve.sem, gdn_dve.next(pe))
                        mm(banks[2][:, :], sgt[0:NS, 1, :], gs_x[0:NS, 0:4, :].rearrange("p b v -> p (b v)"))
                        mm(banks[3][:, :], sgt[0:NS, 1, :], gs_x[0:NS, 4:8, :].rearrange("p b v -> p (b v)")).then_inc(gdn_pe.sem, gdn_pe.one())
                        pe.wait_ge(gdn_dve.sem, gdn_dve.next(pe))
                    for n in range(H_B):
                        pe.wait_ge(gdn_act.sem, gdn_act.next(pe))
                        mm(banks[4 + n % 2][:, 0:T], ones_all[:, :], g_tmp[:, n % 2, :]).then_inc(gdn_pe.sem, gdn_pe.one())

                    pe.wait_ge(merged.sem, merged.at(NT))
                    base = NT + n_out
                    for o in range(NT):
                        w = slot_of("out", o // 2).rearrange("p (k n) -> p k n", k=NT)
                        if o >= 4:
                            pe.wait_ge(out_taken.sem, out_taken.at(base + o - 3))
                        for k in range(NT):
                            i = mm(banks[o % 4][:, 0:T], w[:, k, (o % 2) * P:(o % 2 + 1) * P], h[:, k, :], k == 0, k == NT - 1)
                        i.then_inc(lin_done.sem, lin_done.one())
                    mean_square_tiles(sq_out)
                    ffn(1)

                @block.scalar
                def _(act):
                    def row_load(dst, src):
                        act.dma_start(dst, src).then_inc(rows_in.sem, rows_in.one())

                    def tiles(ap):
                        return ap.rearrange("(j f) -> j f", f=P)

                    row_load(prow[0:72, 0, :], tiles(I["b_ada"][l]))
                    row_load(prow[72:96, 0, :], I["norm_pre"][l].rearrange("s (j f) -> (s j) f", f=P))
                    row_load(prow[96:120, 0, :], I["norm_post"][l].rearrange("s (j f) -> (s j) f", f=P))
                    row_load(prow[0:26, 1, :], tiles(I["rwkv_mu"][l]))
                    for n, name in enumerate(("w0", "a0", "k_k", "k_a")):
                        row_load(prow[26 + 8 * n:34 + 8 * n, 1, :], tiles(I["rwkv_" + name][l]))
                    row_load(prow[58:66, 1, :], I["rwkv_r_k"][l].rearrange("(j g) d -> j (g d)", g=2))
                    for n, name in enumerate(("ln_w", "ln_b")):
                        row_load(prow[66 + 8 * n:74 + 8 * n, 1, :], tiles(I["rwkv_" + name][l]))
                    row_load(prow[82:83, 1, :], tiles(I["gdn_norm_w"][l]))
                    row_load(prow[0:96, 2, :], I["gdn_conv"][l].rearrange("i (j f) -> (i j) f", f=P))
                    row_load(adt[0:8, 0:1], I["gdn_a_log"][l].rearrange("(h a) -> h a", a=1))
                    row_load(adt[0:8, 1:2], I["gdn_dt_bias"][l].rearrange("(h a) -> h a", a=1))
                    row_load(strow[0:104, 0:2, :],
                             I["state_rwkv_shift"][l].rearrange("(n b) (j f) -> (b j) n f", n=2, f=P))
                    row_load(strow[0:96, 2:8, :],
                             I["state_gdn_conv"][l].rearrange("b i (j f) -> (b i j) f", f=P).rearrange("(n q) f -> q n f", n=6))
                    act.dma_start(O["sample_gdn_conv"][l, :, 0:2, :], I["state_gdn_conv"][l, :, 1:3, :]).then_inc(st_out.sem, st_out.one())

                    def rsqrt(out, ss, scale, eps):
                        act.activation(out, ss, ACT.Ln, bias=epsc[:, eps:eps + 1], scale=scale).then_inc(act_chain.sem, act_chain.one())
                        act.wait_ge(act_chain.sem, act_chain.all())
                        return act.activation(out, out, ACT.Exp, scale=-0.5)

                    def normalise(square_x):
                        if square_x:
                            act.wait_ge(x_ready.sem, x_ready.next(act))
                            act.activation(h[:, :, :], xT[:, :, :], ACT.Square).then_inc(sq_ready.sem, sq_ready.one())
                            act.wait_ge(sq_ready.sem, sq_ready.all())
                        act.wait_ge(ss_done.sem, ss_done.next(act))
                        rsqrt(rs[:, :], banks[7][:, 0:T], 1.0, 0).then_inc(rs_ready.sem, rs_ready.one())
                        act.wait_ge(rs_ready.sem, rs_ready.all())

                    def ffn(i_ffn):
                        normalise(True)
                        n0 = done_by[where[(f"up{i_ffn}", 0)]] - 2
                        for t in range(FT):
                            act.wait_ge(lin_done.sem, lin_done.at(n0 + 2 * t + 1))
                            if t >= 2:
                                act.wait_ge(hid_ready.sem, hid_ready.at(i_ffn * FT + t - 1))
                            act.activation(silu_g[:, t % 2, :], banks[t % 2][:, 0:T], ACT.Silu).then_inc(gate_taken.sem, gate_taken.one())
                            act.wait_ge(gate_taken.sem, gate_taken.all())
                        for o in range(NT):
                            act.wait_ge(lin_done.sem, lin_done.at(done_by[where[(f"down{i_ffn}", 2 * o + 1)]]))
                            act.copy(y[:, o, :], banks[o % 4][:, 0:T]).then_inc(out_taken.sem, out_taken.one())
                            act.wait_ge(out_taken.sem, out_taken.all())
                            act.activation(h[:, o, :], y[:, o, :], ACT.Square).then_inc(sq_ready.sem, sq_ready.one())
                            act.wait_ge(sq_ready.sem, sq_ready.all())
                        normalise(False)

                    ffn(0)
                    normalise(True)
                    n0 = done_by[where[("in", 0)]] - 2
                    for n in range(A_TILES + Q_TILES + 2 + 3 * NT):
                        act.wait_ge(lin_done.sem, lin_done.at(n0 + n + 1))
                        src = banks[n % 4][:, 0:T]
                        if n == 0:
                            act.wait_ge(pads.sem, pads.at(1))
                        if n < A_TILES:
                            i = act.copy(pa[:, n, 1:T + 1], src)
                        elif n < A_TILES + Q_TILES:
                            i = act.copy(qk[:, n - A_TILES, 3:T + 3], src)
                        elif n < A_TILES + Q_TILES + 2:
                            i = act.copy(abr[0:8, n - A_TILES - Q_TILES, :], banks[n % 4][0:8, 0:T])
                        else:
                            m = n - A_TILES - Q_TILES - 2
                            if m < NT:
                                i = act.activation(zs[:, m, :], src, ACT.Silu)
                            else:
                                i = act.activation(gates[:, m - NT, :], src, ACT.Sigmoid)
                        i.then_inc(out_taken.sem, out_taken.one())
                        act.wait_ge(out_taken.sem, out_taken.all())
                    act.wait_ge(last_tr.sem, last_tr.next(act))
                    for n, (_, count) in enumerate(LAST):
                        i = act.copy(last[0:count, n, :], banks[4 + n // 4][0:count, (n % 4) * P:(n % 4 + 1) * P])
                    i.then_inc(last_rd.sem, last_rd.one())
                    act.wait_ge(last_rd.sem, last_rd.all())
                    LO = ((O["prompt_rwkv_shift"][l].rearrange("b (j f) -> (b j) f", f=P), 26, 0),
                          (O["sample_rwkv_shift"][l, 0:4].rearrange("b (j f) -> (b j) f", f=P), 104, 1),
                          (O["sample_rwkv_shift"][l, 4:8].rearrange("b (j f) -> (b j) f", f=P), 104, 2),
                          (O["prompt_gdn_conv"][l, 0].rearrange("i (j f) -> (i j) f", f=P), 72, 3))
                    for dst, rows, n in LO:
                        act.dma_start(dst, last[0:rows, n, :]).then_inc(st_out.sem, st_out.one())
                    for n in range(2):
                        for b in range(4):
                            act.dma_start(
                                O["sample_gdn_conv"][l, 4 * n + b, 2].rearrange("(j f) -> j f", f=P),
                                last[24 * b:24 * b + 24, 4 + n, :]).then_inc(st_out.sem, st_out.one())
                    for n in range(Q_TILES):
                        act.wait_ge(conv_ready.sem, conv_ready.next(act))
                        act.activation(qk[:, n, 3:T + 3], (rs[:, :], rs2)[n % 2], ACT.Silu).then_inc(conv_done.sem, conv_done.one())
                        act.wait_ge(conv_done.sem, conv_done.all())
                    act.wait_ge(st_out.sem, st_out.all())
                    act.wait_ge(shifted.sem, shifted.next(act, 4))
                    act.activation(pa[0:64, 24, 1:T + 1], pa[0:64, 24, 1:T + 1], ACT.Tanh)
                    act.activation(pa[:, 25, 1:T + 1], pa[:, 25, 1:T + 1], ACT.Sigmoid).then_inc(lora_in.sem, lora_in.one())
                    act.wait_ge(lora_in.sem, lora_in.all())

                    n0 = done_by[where[("lora", 0)]] - 3 * NT
                    for q in range(NT // GRP):
                        for jj in range(GRP):
                            j = GRP * q + jj
                            act.activation(sq_t, pa[:, 8 + j, 1:T + 1], ACT.Square, scale=k_k[:, j:j + 1]).then_inc(kksq.sem, kksq.one())
                            act.wait_ge(kksq.sem, kksq.all())
                            act.wait_ge(lin_done.sem, lin_done.at(n0 + 2 * j + 2))
                            act.activation(e2[:, 0, :], banks[0][:, 0:T], ACT.Exp, bias=ncol[:, j:j + 1], scale=-1.0)
                            act.activation(e2[:, 1, :], banks[1][:, 0:T], ACT.Exp,
                                          bias=ncol[:, NT + j:NT + j + 1], scale=-1.0).then_inc(ew_ready.sem, ew_ready.one())
                            act.wait_ge(ew_ready.sem, ew_ready.all())
                            act.wait_ge(kkss.sem, kkss.next(act))
                            rsqrt(rs_t, banks[2][:, 0:T], 1.0, 1).then_inc(kkrs.sem, kkrs.one())
                            act.wait_ge(kkrs.sem, kkrs.all())
                            act.wait_ge(g_ready.sem, g_ready.next(act))
                            act.activation(e_x, e_x, ACT.Exp)
                            act.activation(e_g, gc_i, ACT.Exp)
                            act.activation(e_n, gc_i, ACT.Exp, scale=-1.0).then_inc(eg_ready.sem, eg_ready.one())
                            act.wait_ge(eg_ready.sem, eg_ready.all())
                            act.wait_ge(prod_done.sem, prod_done.next(act))
                            us = slice(jj * NC, (jj + 1) * NC)
                            for dst, bank, at in ((vtok, 6, 0), (ktok, 6, 256), (btok, 7, 0)):
                                i = act.copy(dst[:, us, :], banks[bank][:, at:at + 256].rearrange("p (u d) -> p u d", u=NC))
                            i.then_inc(prod_act.sem, prod_act.one())
                            act.wait_ge(prod_act.sem, prod_act.all())
                        invert_act(act, q)
                        for c in range(NC):
                            act.wait_ge(seq_pe.sem, seq_pe.at((4 * NC + 1) * q + 4 * c + 1))
                            act.copy(ws_a, banks[0][:, 0:256].rearrange("p (u d) -> p u d", u=GRP)).then_inc(seq_act.sem, seq_act.one())
                            act.wait_ge(seq_act.sem, seq_act.all())
                            act.wait_ge(seq_pe.sem, seq_pe.at((4 * NC + 1) * q + 4 * c + 2))
                            act.mul(us_a, banks[1][:, 0:256].rearrange("p (u d) -> p u d", u=GRP), -1.0).then_inc(seq_act.sem, seq_act.one())
                            act.wait_ge(seq_act.sem, seq_act.all())
                        act.wait_ge(seq_pe.sem, seq_pe.at((4 * NC + 1) * (q + 1)))
                        act.copy(mo_a, banks[0][:, 0:256].rearrange("p (u d) -> p u d", u=GRP)).then_inc(seq_act.sem, seq_act.one())
                        act.wait_ge(seq_act.sem, seq_act.all())
                        for g in range(2):
                            act.dma_start(
                                O["prompt_rwkv_wkv"][l, 0, 2 * GRP * q:2 * GRP * (q + 1)]
                                .rearrange("(j g) v k -> g v j k", g=2)[g], mo_a[64 * g:64 * g + 64, :, :]).then_inc(st_out.sem, st_out.one())
                        act.wait_ge(st_out.sem, st_out.all())

                    def state_ap(ap, g, vh):
                        return ap.rearrange("b (j g) v k -> g (b j) (v k)", g=2)[g][:, vh * 2048:(vh + 1) * 2048]

                    for vh in range(2):
                        for g in range(2):
                            act.dma_start(
                                samp_s[64 * g:64 * g + 64, :, :].rearrange("p v k -> p (v k)"),
                                state_ap(I["state_rwkv_wkv"][l], g, vh)).then_inc(samp_in.sem, samp_in.one())
                        if vh == 0:
                            act.wait_ge(sv_pe.sem, sv_pe.next(act))
                            act.copy(svt[:, :, :], banks[4][:, 0:6 * C].rearrange("p (n d) -> p n d", n=6)).then_inc(svt_ready.sem, svt_ready.one())
                            act.wait_ge(svt_ready.sem, svt_ready.all())
                        act.wait_ge(samp_done.sem, samp_done.next(act))
                        for g in range(2):
                            act.dma_start(
                                state_ap(O["sample_rwkv_wkv"][l], g, vh),
                                samp_s[64 * g:64 * g + 64, :, :].rearrange("p v k -> p (v k)")).then_inc(samp_out.sem, samp_out.one())
                        act.wait_ge(samp_out.sem, samp_out.next(act, 2))
                    act.wait_ge(sv_pe.sem, sv_pe.next(act))
                    act.copy(h[:, :, NPR:T], banks[5][:, 0:64].rearrange("p (b j) -> p j b", j=NT)).then_inc(ys_done.sem, ys_done.one())
                    act.wait_ge(ys_done.sem, ys_done.all())

                    for j in range(NT):
                        act.wait_ge(post_dve.sem, post_dve.at(2 * j + 1))
                        act.activation(sq_t, h[:, j, :], ACT.Square).then_inc(post_act.sem, post_act.one())
                        act.wait_ge(post_act.sem, post_act.all())
                        act.wait_ge(post_pe.sem, post_pe.at(2 * j + 2))
                        rsqrt(rs_t, banks[1][:, 0:T], 1.0 / HD_A, 2).then_inc(post_act.sem, post_act.one())
                        act.wait_ge(post_act.sem, post_act.all())

                    act.wait_ge(post_dve.sem, post_dve.at(2 * NT))
                    r3, r4 = g_row[0:8, 3, :], g_row[0:8, 4, :]
                    act.activation(r3, abr[0:8, 0, :], ACT.Abs, bias=adt[0:8, 1:2]).then_inc(act_chain.sem, act_chain.one())
                    act.wait_ge(act_chain.sem, act_chain.all())
                    act.activation(r3, r3, ACT.Exp, scale=-1.0).then_inc(act_chain.sem, act_chain.one())
                    act.wait_ge(act_chain.sem, act_chain.all())
                    act.activation(r3, r3, ACT.Ln, bias=epsc[0:8, 3:4])
                    act.activation(r4, abr[0:8, 1, :], ACT.Exp, scale=-1.0)
                    act.activation(adt[0:8, 0:1], adt[0:8, 0:1], ACT.Exp).then_inc(gdn_rows_a.sem, gdn_rows_a.one())
                    act.wait_ge(gdn_rows_a.sem, gdn_rows_a.all())
                    act.wait_ge(gdn_rows_d.sem, gdn_rows_d.next(act))
                    act.activation(g_row[0:8, 2, 0:NPR], g_row[0:8, 2, 0:NPR], ACT.Exp)
                    act.activation(g_row[0:8, 6, :], g_row[0:8, 0, :], ACT.Exp).then_inc(gdn_rows_a.sem, gdn_rows_a.one())
                    act.wait_ge(gdn_rows_a.sem, gdn_rows_a.all())
                    for n in range(H_B):
                        if n:
                            act.wait_ge(gdn_dve.sem, gdn_dve.at(n))
                        act.activation(g_tmp[:, 0, :], qk[:, n, 3:T + 3], ACT.Square)
                        act.activation(g_tmp[:, 1, :], qk[:, 8 + n, 3:T + 3], ACT.Square).then_inc(gdn_act.sem, gdn_act.one())
                        act.wait_ge(gdn_act.sem, gdn_act.all())
                        act.wait_ge(gdn_pe.sem, gdn_pe.at(1 + 2 * n + 1))
                        rsqrt(g_tmp[:, 0, :], banks[0][:, 0:T], 1.0, 0)
                        rsqrt(g_tmp[:, 1, :], banks[1][:, 0:T], 1.0, 0)
                        act.activation(g_eg[:, n, :], banks[2][:, 0:T], ACT.Exp).then_inc(gdn_ra.sem, gdn_ra.one())
                        act.wait_ge(gdn_ra.sem, gdn_ra.all())
                        act.wait_ge(gdn_rd.sem, gdn_rd.next(act))
                        act.activation(g_tmp[:, 3, 0:P], g_tmp[:, 3, 0:P], ACT.Exp).then_inc(gdn_ra.sem, gdn_ra.one())
                        act.wait_ge(gdn_ra.sem, gdn_ra.all())
                    invert_act(act, 2)
                    for c in range(NC):
                        hf = HALVES[c % 2]
                        act.wait_ge(gdn_pe.sem, gdn_pe.at(1 + 2 * H_B + 4 * c + 2))
                        act.copy(g_vn[hf, 0:4, :], banks[2][hf, :].rearrange("p (n v) -> p n v", n=4))
                        act.copy(g_vn[hf, 4:8, :], banks[3][hf, :].rearrange("p (n v) -> p n v", n=4)).then_inc(gdn_act.sem, gdn_act.one())
                        act.wait_ge(gdn_act.sem, gdn_act.all())
                    act.wait_ge(gdn_dve.sem, gdn_dve.at(GD_SEQ))
                    act.dma_start(O["prompt_gdn_ssm"][l, 0].rearrange("h k v -> k h v"), g_s[:, :, :]).then_inc(st_out.sem, st_out.one())
                    def sample_state(ap, n):
                        return ap[:, n].rearrange("b k v -> k b v")

                    def load_state(n):
                        act.dma_start(gs_s[n % 2], sample_state(I["state_gdn_ssm"][l], n)).then_inc(gs_in[n % 2].sem, gs_in[n % 2].one())

                    load_state(0)
                    load_state(1)
                    for n in range(H_B):
                        act.wait_ge(gdn_dve.sem, gdn_dve.at(GD_SEQ + 1 + 3 * (n + 1)))
                        act.dma_start(sample_state(O["sample_gdn_ssm"][l], n), gs_s[n % 2]).then_inc(gs_out[n % 2].sem, gs_out[n % 2].one())
                        if n + 2 < H_B:
                            act.wait_ge(gs_out[n % 2].sem, gs_out[n % 2].next(act))
                            load_state(n + 2)
                    for n in range(H_B):
                        if n >= 2:
                            act.wait_ge(gdn_pe.sem, gdn_pe.at(GP_POST + n - 1))
                        act.activation(g_tmp[:, n % 2, :], y[:, n, :], ACT.Square).then_inc(gdn_act.sem, gdn_act.one())
                        act.wait_ge(gdn_act.sem, gdn_act.all())
                        act.wait_ge(gdn_pe.sem, gdn_pe.at(GP_POST + n + 1))
                        if n >= 2:
                            act.wait_ge(merged.sem, merged.at(n - 1))
                        rsqrt(g_tmp[:, 2 + n % 2, :], banks[4 + n % 2][:, 0:T], 1.0 / HD_B, 0).then_inc(gdn_ra.sem, gdn_ra.one())
                        act.wait_ge(gdn_ra.sem, gdn_ra.all())

                    n0 = done_by[where[("out", 0)]] - 2
                    for o in range(NT):
                        act.wait_ge(lin_done.sem, lin_done.at(n0 + o + 1))
                        act.copy(y[:, o, :], banks[o % 4][:, 0:T]).then_inc(out_taken.sem, out_taken.one())
                        act.wait_ge(out_taken.sem, out_taken.all())
                        act.activation(sq_out[:, o, :], y[:, o, :], ACT.Square).then_inc(sq_ready.sem, sq_ready.one())
                        act.wait_ge(sq_ready.sem, sq_ready.all())
                    normalise(False)
                    ffn(1)
                    act.wait_ge(st_out.sem, st_out.all())
                    for s in gs_out:
                        act.wait_ge(s.sem, s.all())

                @block.vector
                def _(dve):
                    def tt(out, a, b, op=ALU.mult):
                        return dve.tensor_tensor(out, a, b, op)

                    def stt(out, a, s, b, op0, op1):
                        return dve.scalar_tensor_tensor(out, a, s, b, op0, op1)

                    dve.wait_ge(tr_done.sem, tr_done.next(dve))
                    for g, rows in enumerate((120, 83, 96)):
                        i = dve.tensor_copy(pcol[:, g * P:g * P + rows], banks[6][:, g * P:g * P + rows])
                    dve.tensor_copy(shp[:, :, :], banks[7][:, 0:208].rearrange("p (b j) -> p j b", b=NS))
                    dve.tensor_copy(cvp[:, :, 0:12], banks[7][:, 208:496].rearrange("p (r j) -> p j r", r=12))
                    i = dve.tensor_copy(cvp[:, :, 12:24], banks[3][:, 0:288].rearrange("p (r j) -> p j r", r=12))
                    i.then_inc(cols_ready.sem, cols_ready.one())
                    dve.wait_ge(cols_ready.sem, cols_ready.all())
                    dve.tensor_scalar(ncol[:, 0:16], pcol[:, 154:170], -1.0, None, ALU.mult)
                    dve.tensor_scalar(ncol[:, 16:24], k_a, -1.0, 1.0, ALU.mult, ALU.add)

                    dve.wait_ge(lin_done.sem, lin_done.at(ADA_TILES))
                    for g in range(2):
                        i = tt(modv[:, 36 * g:36 * g + 36, :], banks[4 + g][:, 0:36 * NROW].rearrange("p (m r) -> p m r", r=NROW),
                               bc(bada[:, 36 * g:36 * g + 36], NROW), ALU.add)
                    i.then_inc(dve_chain.sem, dve_chain.one())
                    dve.wait_ge(dve_chain.sem, dve_chain.all())
                    for s in range(3):
                        m = 3 * NT * s
                        sub = slice(NT * s, NT * (s + 1))
                        stt(mod_a[:, sub, :], modv[:, m + NT:m + 2 * NT, :], 1.0, bc(npre[:, sub], NROW), ALU.add, ALU.mult)
                        i = stt(mod_g[:, sub, :], modv[:, m + 2 * NT:m + 3 * NT, :], 1.0 if s == 1 else FFN_RES,
                                bc(npost[:, sub], NROW), ALU.mult, ALU.mult)
                    i.then_inc(x_ready.sem, x_ready.one())
                    dve.wait_ge(x_ready.sem, x_ready.all())

                    def sub_in(s):
                        dve.wait_ge(rs_ready.sem, rs_ready.next(dve))
                        tt(h[:, :, :], xT[:, :, :], bm(rs[:, :], NT)).then_inc(dve_chain.sem, dve_chain.one())
                        dve.wait_ge(dve_chain.sem, dve_chain.all())
                        for j in range(NT):
                            dve.tensor_scalar(h[:, j, 0:NPR], h[:, j, 0:NPR], mod_a[:, NT * s + j, 0:1],
                                              modv[:, 3 * NT * s + j, 0:1], ALU.mult, ALU.add)
                        hs = h[:, :, NPR:T]
                        tt(hs, hs, mod_a[:, NT * s:NT * (s + 1), 1:NROW]).then_inc(dve_chain.sem, dve_chain.one())
                        dve.wait_ge(dve_chain.sem, dve_chain.all())
                        tt(hs, hs, modv[:, 3 * NT * s:3 * NT * s + NT, 1:NROW], ALU.add).then_inc(h_ready.sem, h_ready.one())
                        dve.wait_ge(h_ready.sem, h_ready.all())

                    def sub_out(s):
                        dve.wait_ge(rs_ready.sem, rs_ready.next(dve))
                        tt(y[:, :, :], y[:, :, :], bm(rs[:, :], NT)).then_inc(dve_chain.sem, dve_chain.one())
                        dve.wait_ge(dve_chain.sem, dve_chain.all())
                        for j in range(NT):
                            stt(xT[:, j, 0:NPR], y[:, j, 0:NPR], mod_g[:, NT * s + j, 0:1], xT[:, j, 0:NPR], ALU.mult, ALU.add)
                        ys, xs = y[:, :, NPR:T], xT[:, :, NPR:T]
                        tt(ys, ys, mod_g[:, NT * s:NT * (s + 1), 1:NROW]).then_inc(dve_chain.sem, dve_chain.one())
                        dve.wait_ge(dve_chain.sem, dve_chain.all())
                        tt(xs, xs, ys, ALU.add).then_inc(x_ready.sem, x_ready.one())
                        dve.wait_ge(x_ready.sem, x_ready.all())

                    def ffn(i_ffn):
                        sub_in(2 * i_ffn)
                        n0 = done_by[where[(f"up{i_ffn}", 0)]] - 2
                        for t in range(FT):
                            dve.wait_ge(gate_taken.sem, gate_taken.at(i_ffn * FT + t + 1))
                            dve.wait_ge(lin_done.sem, lin_done.at(n0 + 2 * t + 2))
                            tt(hid[:, t, :], silu_g[:, t % 2, :], banks[2 + t % 2][:, 0:T]).then_inc(hid_ready.sem, hid_ready.one())
                            dve.wait_ge(hid_ready.sem, hid_ready.all())
                        sub_out(2 * i_ffn)

                    ffn(0)
                    sub_in(1)
                    dve.memset(pa[:, :, 0:1], 0.0)
                    dve.memset(qk[:, :, 0:3], 0.0).then_inc(pads.sem, pads.one())
                    dve.wait_ge(pads.sem, pads.all())

                    dve.wait_ge(out_taken.sem, out_taken.at(NT + A_TILES))
                    dve.tensor_copy(last_c[:, 0:26], pa[:, :, NPR])
                    dve.tensor_copy(last_c[:, 26:234].rearrange("p (b j) -> p b j", b=NS),
                                   pa[:, :, NPR + 1:T + 1].rearrange("p j b -> p b j")).then_inc(last_cp.sem, last_cp.one())
                    dve.wait_ge(last_cp.sem, last_cp.all())
                    for t0, n in ((0, 8), (8, 8), (16, 8), (24, 2)):
                        ts = slice(t0, t0 + n)
                        tt(y[:, 0:n, 0:NPR], pa[:, ts, 0:NPR], pa[:, ts, 1:NPR + 1], ALU.subtract)
                        tt(y[:, 0:n, NPR:T], shp[:, ts, :], pa[:, ts, NPR + 1:T + 1], ALU.subtract).then_inc(dve_chain.sem, dve_chain.one())
                        dve.wait_ge(dve_chain.sem, dve_chain.all())
                        for j in range(n):
                            i = stt(pa[:, t0 + j, 1:T + 1], y[:, j, :], mu[:, t0 + j:t0 + j + 1], pa[:, t0 + j, 1:T + 1],
                                    ALU.mult, ALU.add)
                        i.then_inc(shifted.sem, shifted.one())
                        dve.wait_ge(shifted.sem, shifted.all())
                    dve.wait_ge(out_taken.sem, out_taken.at(NT + A_TILES + Q_TILES))
                    dve.tensor_copy(last_c[:, 234:306].rearrange("p (i j) -> p i j", i=3),
                                    qk[:, :, NPR:NPR + 3].rearrange("p j i -> p i j"))
                    dve.tensor_copy(last_c[:, 306:498].rearrange("p (b j) -> p b j", b=NS),
                                   qk[:, :, NPR + 3:T + 3].rearrange("p j b -> p b j")).then_inc(last_cp.sem, last_cp.one())
                    dve.wait_ge(last_cp.sem, last_cp.all())
                    tt(convs[:, :, :], qk[:, :, NPR + 3:T + 3], bc(convw[:, 3, :], NS)).then_inc(dve_chain.sem, dve_chain.one())
                    dve.wait_ge(dve_chain.sem, dve_chain.all())
                    cv = cvp[:, :, :].rearrange("p j (b i) -> p j b i", i=3)
                    for n in range(3):
                        tt(convt[:, :, :], cv[:, :, :, n], bc(convw[:, n, :], NS)).then_inc(dve_chain.sem, dve_chain.one())
                        dve.wait_ge(dve_chain.sem, dve_chain.all())
                        tt(convs[:, :, :], convs[:, :, :], convt[:, :, :], ALU.add).then_inc(dve_chain.sem, dve_chain.one())
                        dve.wait_ge(dve_chain.sem, dve_chain.all())
                    for n in range(Q_TILES):
                        acc = (rs[:, :], rs2)[n % 2]
                        if n >= 2:
                            dve.wait_ge(conv_done.sem, conv_done.at(n - 1))
                        dve.tensor_scalar(acc[:, 0:NPR], qk[:, n, 0:NPR], convw[:, 0, n:n + 1], None, ALU.mult).then_inc(dve_chain.sem, dve_chain.one())
                        dve.wait_ge(dve_chain.sem, dve_chain.all())
                        for k in range(1, 4):
                            stt(acc[:, 0:NPR], qk[:, n, k:k + NPR], convw[:, k, n:n + 1], acc[:, 0:NPR], ALU.mult, ALU.add).then_inc(dve_chain.sem, dve_chain.one())
                            dve.wait_ge(dve_chain.sem, dve_chain.all())
                        dve.tensor_copy(acc[:, NPR:T], convs[:, n, :]).then_inc(conv_ready.sem, conv_ready.one())
                        dve.wait_ge(conv_ready.sem, conv_ready.all())
                    dve.wait_ge(last_tr.sem, last_tr.next(dve))

                    for q in range(NT // GRP):
                        for jj in range(GRP):
                            j = GRP * q + jj
                            r, k, v = (pa[:, 8 * n + j, 1:T + 1] for n in range(3))
                            dve.wait_ge(ew_ready.sem, ew_ready.next(dve))
                            dve.tensor_scalar(e2[:, :, :], e2[:, :, :], 1.0, None, ALU.add).then_inc(dve_chain.sem, dve_chain.one())
                            dve.wait_ge(dve_chain.sem, dve_chain.all())
                            dve.reciprocal(e2[:, :, :], e2[:, :, :]).then_inc(dve_chain.sem, dve_chain.one())
                            dve.wait_ge(dve_chain.sem, dve_chain.all())
                            dve.tensor_scalar(lw, e2[:, 0, :], -EXP_MHALF, None, ALU.mult).then_inc(dve_chain.sem, dve_chain.one())
                            dve.wait_ge(dve_chain.sem, dve_chain.all())
                            dve.tensor_tensor_scan(gc_i, carry[:, :], lw, 0.0, ALU.mult, ALU.add).then_inc(dve_chain.sem, dve_chain.one())
                            dve.wait_ge(dve_chain.sem, dve_chain.all())
                            tt(e_x, gc_i, lw, ALU.subtract).then_inc(g_ready.sem, g_ready.one())
                            dve.wait_ge(g_ready.sem, g_ready.all())
                            dve.wait_ge(kkrs.sem, kkrs.next(dve))
                            dve.tensor_scalar(rkk, e2[:, 1, :], k_a[:, j:j + 1], ncol[:, 16 + j:17 + j], ALU.mult, ALU.add)
                            stt(kkn, k, k_k[:, j:j + 1], rs_t, ALU.mult, ALU.mult).then_inc(dve_chain.sem, dve_chain.one())
                            dve.wait_ge(dve_chain.sem, dve_chain.all())
                            tt(kb_t, kkn, e2[:, 1, :])
                            tt(k, rkk, k).then_inc(dve_chain.sem, dve_chain.one())
                            dve.wait_ge(dve_chain.sem, dve_chain.all())
                            stt(rkk, r, r_k[:, j:j + 1], k, ALU.mult, ALU.mult).then_inc(rkk_ready.sem, rkk_ready.one())
                            dve.wait_ge(rkk_ready.sem, rkk_ready.all())
                            dve.wait_ge(eg_ready.sem, eg_ready.next(dve))
                            tt(kdec_f[:, jj, :], kkn[:, 0:NPR], e_x[:, 0:NPR])
                            tt(b_f[:, 0:NPR], kb_t[:, 0:NPR], e_n[:, 0:NPR])
                            tt(kd_f[:, 0:NPR], k[:, 0:NPR], e_n[:, 0:NPR])
                            dve.tensor_copy(eg_end[:, j, :], e_g[:, 0:NPR].rearrange("p (c t) -> p c t", t=C)[:, :, C - 1])
                            for n, src in enumerate((e_g, kkn, kb_t, k, v, r)):
                                dve.tensor_copy(sv[:, n, :, j], src[:, NPR:T])
                            tt(r[:, 0:NPR], r[:, 0:NPR], e_g[:, 0:NPR]).then_inc(ops_ready.sem, ops_ready.one())
                            dve.wait_ge(ops_ready.sem, ops_ready.all())
                            dve.wait_ge(bonss.sem, bonss.next(dve))
                            tt(y[:, j, :], v, banks[3][:, 0:T])
                            dve.wait_ge(prod_done.sem, prod_done.next(dve))
                            us = slice(jj * NC, (jj + 1) * NC)
                            for dst, bank, at, mask in ((lt_all, 4, 0, strict), (pb_all, 4, 256, incl),
                                                        (dm_all, 5, 0, strict), (pk_all, 5, 256, incl)):
                                i = tt(dst[:, us, :], banks[bank][:, at:at + 256].rearrange("p (u t) -> p u t", u=NC),
                                       bm(mask[:, :], NC))
                            i.then_inc(prod_dve.sem, prod_dve.one())
                            dve.wait_ge(prod_dve.sem, prod_dve.all())
                        invert_dve(dve, q)
                        dve.memset(m_st, 0.0).then_inc(seq_dve.sem, seq_dve.one())
                        dve.wait_ge(seq_dve.sem, seq_dve.all())
                        for c in range(NC):
                            dve.wait_ge(seq_pe.sem, seq_pe.at((4 * NC + 1) * q + 4 * c + 3))
                            dve.tensor_copy(h[:, GRP * q:GRP * (q + 1), c * C:(c + 1) * C],
                                            banks[2][:, 0:256].rearrange("p (u t) -> p u t", u=GRP))
                            dve.wait_ge(seq_pe.sem, seq_pe.at((4 * NC + 1) * q + 4 * c + 4))
                            tt(m_st, m_st, banks[3][:, 0:256].rearrange("p (u t) -> p u t", u=GRP), ALU.add).then_inc(dve_chain.sem, dve_chain.one())
                            dve.wait_ge(dve_chain.sem, dve_chain.all())
                            tt(m_st, m_st, bc(eg_end[:, GRP * q:GRP * (q + 1), c], C)).then_inc(seq_dve.sem, seq_dve.one())
                            dve.wait_ge(seq_dve.sem, seq_dve.all())
                        if q + 1 < NT // GRP:
                            dve.wait_ge(seq_pe.sem, seq_pe.at((4 * NC + 1) * (q + 1)))

                    dve.wait_ge(svt_ready.sem, svt_ready.next(dve))
                    w_s, kk_s, b_s, k_s, v_s, r_s = (svt[:, n, :] for n in range(6))
                    for vh in range(2):
                        dve.wait_ge(samp_in.sem, samp_in.at(2 * vh + 2))
                        vs = slice(32 * vh, 32 * vh + 32)
                        tt(samp_t, samp_s, bm(kk_s, 32)).then_inc(dve_chain.sem, dve_chain.one())
                        dve.wait_ge(dve_chain.sem, dve_chain.all())
                        dve.tensor_reduce(ssm[:, 0, vs], samp_t, AX_X, ALU.add).then_inc(dve_chain.sem, dve_chain.one())
                        dve.wait_ge(dve_chain.sem, dve_chain.all())
                        tt(samp_s, samp_s, bm(w_s, 32)).then_inc(dve_chain.sem, dve_chain.one())
                        dve.wait_ge(dve_chain.sem, dve_chain.all())
                        tt(samp_t, bc(ssm[:, 0, vs], C), bm(b_s, 32)).then_inc(dve_chain.sem, dve_chain.one())
                        dve.wait_ge(dve_chain.sem, dve_chain.all())
                        tt(samp_s, samp_s, samp_t, ALU.subtract).then_inc(dve_chain.sem, dve_chain.one())
                        dve.wait_ge(dve_chain.sem, dve_chain.all())
                        tt(samp_t, bc(v_s[:, vs], C), bm(k_s, 32)).then_inc(dve_chain.sem, dve_chain.one())
                        dve.wait_ge(dve_chain.sem, dve_chain.all())
                        tt(samp_s, samp_s, samp_t, ALU.add).then_inc(dve_chain.sem, dve_chain.one())
                        dve.wait_ge(dve_chain.sem, dve_chain.all())
                        tt(samp_t, samp_s, bm(r_s, 32)).then_inc(dve_chain.sem, dve_chain.one())
                        dve.wait_ge(dve_chain.sem, dve_chain.all())
                        dve.tensor_reduce(ssm[:, 1, vs], samp_t, AX_X, ALU.add).then_inc(samp_done.sem, samp_done.one())
                        dve.wait_ge(samp_done.sem, samp_done.all())
                    dve.wait_ge(ys_done.sem, ys_done.next(dve))

                    for j in range(NT):
                        hj = h[:, j, :]
                        dve.wait_ge(post_pe.sem, post_pe.at(2 * j + 1))
                        stt(hj, banks[0][:, 0:T], -1.0 / HD_A, hj, ALU.mult, ALU.add).then_inc(post_dve.sem, post_dve.one())
                        dve.wait_ge(post_dve.sem, post_dve.all())
                        dve.wait_ge(post_act.sem, post_act.at(2 * j + 2))
                        tt(hj, hj, rs_t).then_inc(dve_chain.sem, dve_chain.one())
                        dve.wait_ge(dve_chain.sem, dve_chain.all())
                        dve.tensor_scalar(hj, hj, ln_w[:, j:j + 1], ln_b[:, j:j + 1], ALU.mult, ALU.add).then_inc(dve_chain.sem, dve_chain.one())
                        dve.wait_ge(dve_chain.sem, dve_chain.all())
                        tt(hj, hj, y[:, j, :], ALU.add).then_inc(dve_chain.sem, dve_chain.one())
                        dve.wait_ge(dve_chain.sem, dve_chain.all())
                        dve.wait_ge(lin_done.sem, lin_done.at(done_by[where[("lora", 0)]] - NT + j + 1))
                        tt(hj, hj, banks[2][:, 0:T]).then_inc(dve_chain.sem, dve_chain.one())
                        dve.wait_ge(dve_chain.sem, dve_chain.all())
                        tt(hj, hj, gates[:, j, :]).then_inc(post_dve.sem, post_dve.one())
                        dve.wait_ge(post_dve.sem, post_dve.all())

                    dve.wait_ge(gdn_rows_a.sem, gdn_rows_a.next(dve))
                    row = [g_row[0:8, n, :] for n in range(8)]
                    dve.tensor_scalar(row[4], row[4], 1.0, None, ALU.add)
                    dve.tensor_scalar(row[5], abr[0:8, 0, :], adt[0:8, 1:2], 0.0, ALU.add, ALU.max).then_inc(dve_chain.sem, dve_chain.one())
                    dve.wait_ge(dve_chain.sem, dve_chain.all())
                    dve.reciprocal(row[1], row[4])
                    tt(row[5], row[5], row[3], ALU.add).then_inc(dve_chain.sem, dve_chain.one())
                    dve.wait_ge(dve_chain.sem, dve_chain.all())
                    dve.tensor_scalar(row[5], row[5], adt[0:8, 0:1], -1.0, ALU.mult, ALU.mult).then_inc(dve_chain.sem, dve_chain.one())
                    dve.wait_ge(dve_chain.sem, dve_chain.all())
                    dve.tensor_tensor_scan(row[0], carry[0:8, :], row[5], 0.0, ALU.mult, ALU.add).then_inc(dve_chain.sem, dve_chain.one())
                    dve.wait_ge(dve_chain.sem, dve_chain.all())
                    gcv = row[0][:, 0:NPR].rearrange("p (c t) -> p c t", t=C)
                    tt(row[2][:, 0:NPR].rearrange("p (c t) -> p c t", t=C),
                      gcv[:, :, C - 1:C].to_broadcast([8, NC, C]), gcv, ALU.subtract).then_inc(gdn_rows_d.sem, gdn_rows_d.one())
                    dve.wait_ge(gdn_rows_d.sem, gdn_rows_d.all())
                    dve.wait_ge(gdn_rows_a.sem, gdn_rows_a.next(dve))
                    stt(row[7], row[6], -1.0, row[1], ALU.mult, ALU.mult).then_inc(rows_ready.sem, rows_ready.one())
                    dve.wait_ge(rows_ready.sem, rows_ready.all())
                    dve.wait_ge(gdn_pe.sem, gdn_pe.at(1))
                    dve.tensor_copy(tks[:, :, :, :].rearrange("p a n h -> p (a n h)"), banks[7][:, 0:64]).then_inc(dve_chain.sem, dve_chain.one())
                    dve.wait_ge(dve_chain.sem, dve_chain.all())
                    for n in range(H_B):
                        dve.wait_ge(gdn_ra.sem, gdn_ra.at(2 * n + 1))
                        qn, kn = qk[:, n, 3:T + 3], qk[:, 8 + n, 3:T + 3]
                        stt(qn, qn, HD_B ** -0.5, g_tmp[:, 0, :], ALU.mult, ALU.mult)
                        tt(kn, kn, g_tmp[:, 1, :]).then_inc(dve_chain.sem, dve_chain.one())
                        dve.wait_ge(dve_chain.sem, dve_chain.all())
                        tt(g_tmp[:, 2, 0:NPR], kn[:, 0:NPR], banks[3][:, 0:NPR])
                        dve.tensor_copy(beta_s[:, n, :], banks[3][:, NPR:T])
                        tt(qk_s[:, n, :], qn[:, NPR:T], kn[:, NPR:T])
                        for c in range(NC):
                            hf, cp = HALVES[c % 2], c // 2
                            i = dve.tensor_scalar(g_tmp[hf, 3, cp * C:(cp + 1) * C], banks[2][hf, c * C:(c + 1) * C],
                                                  tks[hf, cp, 0, n:n + 1], 0.0, ALU.subtract, ALU.min)
                        i.then_inc(gdn_rd.sem, gdn_rd.one())
                        dve.wait_ge(gdn_rd.sem, gdn_rd.all())
                        dve.wait_ge(gdn_ra.sem, gdn_ra.at(2 * n + 2))
                        dd = g_tmp[:, 3, 0:P].rearrange("p (c t) -> p c t", c=2)
                        ds = g_tmp[:, 4, 0:P].rearrange("p (c t) -> p c t", c=2)
                        di = g_tmp[:, 5, 0:P].rearrange("p (c t) -> p c t", c=2)
                        tt(ds, dd, bm(strict[:, :], 2))
                        tt(di, dd, bm(incl[:, :], 2)).then_inc(dve_chain.sem, dve_chain.one())
                        dve.wait_ge(dve_chain.sem, dve_chain.all())
                        dve.wait_ge(gdn_pe.sem, gdn_pe.at(1 + 2 * n + 2))
                        tt(g_lt[:, 2 * n:2 * n + 2, :], banks[4][:, 0:P].rearrange("p (c t) -> p c t", c=2), ds)
                        tt(g_at[:, 2 * n:2 * n + 2, :], banks[4][:, P:2 * P].rearrange("p (c t) -> p c t", c=2), di)
                        for cp in range(2):
                            dve.tensor_scalar(g_kd[:, cp, n, :], banks[5][:, cp * P:(cp + 1) * P],
                                              tks[:, cp, 2, n:n + 1], None, ALU.mult)
                            dve.tensor_scalar(g_bv[:, cp, n, :], banks[5][:, 256 + cp * P:256 + (cp + 1) * P],
                                              tks[:, cp, 1, n:n + 1], None, ALU.mult)
                        tt(qn[:, 0:NPR], qn[:, 0:NPR], g_eg[:, n, 0:NPR]).then_inc(gdn_dve.sem, gdn_dve.one())
                        dve.wait_ge(gdn_dve.sem, gdn_dve.all())
                    invert_dve(dve, 2)
                    dve.memset(g_s[:, :, :], 0.0).then_inc(gdn_dve.sem, gdn_dve.one())
                    dve.wait_ge(gdn_dve.sem, gdn_dve.all())
                    for c in range(NC):
                        hf, cp = HALVES[c % 2], c // 2
                        dve.wait_ge(gdn_pe.sem, gdn_pe.at(1 + 2 * H_B + 4 * c + 1))
                        for n in range(H_B):
                            i = stt(g_w[hf, n, :], banks[n // 4][hf, (n % 4) * P:(n % 4 + 1) * P],
                                    tks[hf, cp, 3, n:n + 1], g_bv[hf, cp, n, :], ALU.mult, ALU.add)
                        i.then_inc(gdn_dve.sem, gdn_dve.one())
                        dve.wait_ge(gdn_dve.sem, gdn_dve.all())
                        dve.wait_ge(gdn_pe.sem, gdn_pe.at(1 + 2 * H_B + 4 * c + 3))
                        dve.tensor_copy(y[:, :, c * C:(c + 1) * C], banks[4][:, :].rearrange("p (n t) -> p n t", n=H_B))
                        dve.wait_ge(gdn_pe.sem, gdn_pe.at(1 + 2 * H_B + 4 * c + 4))
                        for n in range(H_B):
                            i = stt(g_s[:, n, :], g_s[:, n, :], g_eg[:, n, c * C + C - 1:(c + 1) * C],
                                    banks[5 + n // 4][:, (n % 4) * P:(n % 4 + 1) * P], ALU.mult, ALU.add)
                        i.then_inc(gdn_dve.sem, gdn_dve.one())
                        dve.wait_ge(gdn_dve.sem, gdn_dve.all())
                    assert gdn_dve.posted == GD_SEQ
                    dve.wait_ge(gdn_pe.sem, gdn_pe.at(GP_SAMP))
                    dve.tensor_copy(qk_s[:, :, :].rearrange("p n b -> p (n b)"), banks[7][:, 0:64]).then_inc(gdn_dve.sem, gdn_dve.one())
                    dve.wait_ge(gdn_dve.sem, gdn_dve.all())
                    for n in range(H_B):
                        s = gs_s[n % 2]
                        dve.wait_ge(gdn_pe.sem, gdn_pe.at(GP_SAMP + 3 * n + 1))
                        both = banks[0][:, 0:2 * NS].rearrange("p (b g) -> p g b", g=2)
                        eg, vn = g_eg[:, n, NPR:T], sg[:, 1, :]
                        tt(sg[:, 2, :], both[:, 0, :], eg)
                        tt(sg[:, 0, :], both[:, 1, :], eg).then_inc(dve_chain.sem, dve_chain.one())
                        dve.wait_ge(dve_chain.sem, dve_chain.all())
                        tt(vn, qk[:, 16 + n, NPR + 3:T + 3], sg[:, 0, :], ALU.subtract).then_inc(dve_chain.sem, dve_chain.one())
                        dve.wait_ge(dve_chain.sem, dve_chain.all())
                        tt(vn, vn, beta_s[:, n, :]).then_inc(dve_chain.sem, dve_chain.one())
                        dve.wait_ge(dve_chain.sem, dve_chain.all())
                        tt(sg[:, 3, :], vn, qk_s[:, n, :]).then_inc(dve_chain.sem, dve_chain.one())
                        dve.wait_ge(dve_chain.sem, dve_chain.all())
                        tt(y[:, n, NPR:T], sg[:, 2, :], sg[:, 3, :], ALU.add).then_inc(gdn_dve.sem, gdn_dve.one())
                        dve.wait_ge(gdn_dve.sem, gdn_dve.all())
                        dve.wait_ge(gdn_pe.sem, gdn_pe.at(GP_SAMP + 3 * n + 2))
                        dve.tensor_copy(sgt[0:NS, :, :], banks[1][0:NS, 0:2 * P].rearrange("p (a f) -> p a f", a=2)).then_inc(dve_chain.sem, dve_chain.one())
                        dve.wait_ge(dve_chain.sem, dve_chain.all())
                        tt(gs_x[0:NS, :, :], bm(sgt[0:NS, 0, :], NS), bc(delta[0:NS, :], P)).then_inc(gdn_dve.sem, gdn_dve.one())
                        dve.wait_ge(gdn_dve.sem, gdn_dve.all())
                        tt(s, s, bc(eg, P)).then_inc(dve_chain.sem, dve_chain.one())
                        dve.wait_ge(dve_chain.sem, dve_chain.all())
                        dve.wait_ge(gdn_pe.sem, gdn_pe.at(GP_SAMP + 3 * n + 3))
                        for g in range(2):
                            i = tt(s[:, 4 * g:4 * g + 4, :], s[:, 4 * g:4 * g + 4, :],
                                   banks[2 + g][:, :].rearrange("p (b v) -> p b v", b=4), ALU.add)
                        i.then_inc(gdn_dve.sem, gdn_dve.one())
                        dve.wait_ge(gdn_dve.sem, gdn_dve.all())
                    for n in range(H_B):
                        dve.wait_ge(gdn_ra.sem, gdn_ra.at(2 * H_B + n + 1))
                        yn = y[:, n, :]
                        tt(yn, yn, g_tmp[:, 2 + n % 2, :]).then_inc(dve_chain.sem, dve_chain.one())
                        dve.wait_ge(dve_chain.sem, dve_chain.all())
                        stt(yn, yn, g_nw, zs[:, n, :], ALU.mult, ALU.mult).then_inc(dve_chain.sem, dve_chain.one())
                        dve.wait_ge(dve_chain.sem, dve_chain.all())
                        tt(yn, yn, gates[:, NT + n, :]).then_inc(dve_chain.sem, dve_chain.one())
                        dve.wait_ge(dve_chain.sem, dve_chain.all())
                        tt(h[:, n, :], h[:, n, :], yn, ALU.add).then_inc(merged.sem, merged.one())
                        dve.wait_ge(merged.sem, merged.all())
                    sub_out(1)
                    ffn(1)

            end_of_part()

        with nc.Block() as block:
            @block.tensor
            def _(pe):
                for a in range(2):
                    for j in range(NT):
                        n = a * NT + j
                        pe.transpose(banks[n // 4][:, (n % 4) * P:(n % 4 + 1) * P], xT[:, j, a * P:(a + 1) * P], ident[:, :])
                for j in range(NT):
                    i = pe.transpose(banks[4 + j // 4][0:NS, (j % 4) * P:(j % 4 + 1) * P], xT[:, j, NPR:T], ident[:, :])
                i.then_inc(tr_done.sem, tr_done.one())

            @block.scalar
            def _(act):
                act.wait_ge(tr_done.sem, tr_done.next(act))
                flat = y[:, :, :].rearrange("p j t -> p (j t)")
                for n in range(4):
                    i = act.copy(flat[:, n * 512:(n + 1) * 512], banks[n][:, :])
                i.then_inc(act_chain.sem, act_chain.one())
                hf = h[:, :, :].rearrange("p j t -> p (j t)")
                for n in range(2):
                    i = act.copy(hf[0:NS, n * 512:(n + 1) * 512], banks[4 + n][0:NS, :])
                i.then_inc(act_chain.sem, act_chain.one())
                act.wait_ge(act_chain.sem, act_chain.next(act, 2))
                act.dma_start(O["y_prompt"][0].rearrange("(a p) f -> p a f", p=P),
                                          flat[:, 0:2 * D].rearrange("p (a f) -> p a f", a=2)).then_inc(st_out.sem, st_out.one())
                act.dma_start(O["y_sample"].rearrange("b a f -> (b a) f"), hf[0:NS, 0:D]).then_inc(st_out.sem, st_out.one())
                act.wait_ge(st_out.sem, st_out.next(act, 2))


_INS = ["x_prompt", "x_sample", "c_prompt", "c_sample", "state_rwkv_shift", "state_rwkv_wkv", "state_gdn_conv",
        "state_gdn_ssm", "w_ada", "b_ada", "norm_pre", "norm_post", "ffn_up", "ffn_down", "w_in", "w_out", "rwkv_mu",
        "rwkv_w0", "rwkv_w2", "rwkv_a0", "rwkv_a2", "rwkv_g2", "rwkv_k_k", "rwkv_k_a", "rwkv_r_k", "rwkv_ln_w",
        "rwkv_ln_b", "gdn_conv", "gdn_a_log", "gdn_dt_bias", "gdn_norm_w"]
_OUTS = [("y_prompt", (1, NPR, D)), ("y_sample", (NS, 1, D)),
         ("prompt_rwkv_shift", (DEPTH, 1, A_COLS)), ("prompt_rwkv_wkv", (DEPTH, 1, H_A, HD_A, HD_A)),
         ("prompt_gdn_conv", (DEPTH, 1, 3, Q_COLS)), ("prompt_gdn_ssm", (DEPTH, 1, H_B, HD_B, HD_B)),
         ("sample_rwkv_shift", (DEPTH, NS, A_COLS)), ("sample_rwkv_wkv", (DEPTH, NS, H_A, HD_A, HD_A)),
         ("sample_gdn_conv", (DEPTH, NS, 3, Q_COLS)), ("sample_gdn_ssm", (DEPTH, NS, H_B, HD_B, HD_B))]


def kernel(**inputs):
    import numpy as _np
    import concourse.bacc as _bacc
    from concourse.bass_utils import run_bass_kernel_spmd as _run

    nc = _bacc.Bacc("TRN2", target_bir_lowering=False, num_devices=1)
    arrays, ins, outs = {}, {}, {}
    for name in _INS:
        a = _np.ascontiguousarray(inputs[name])
        arrays[f"in_{name}"] = a
        ins[name] = nc.dram_tensor(f"in_{name}", a.shape, F32, kind="ExternalInput").ap()
    for name, shape in _OUTS:
        outs[name] = nc.dram_tensor(f"out_{name}", shape, F32, kind="ExternalOutput").ap()
    build(nc, ins, outs)
    r = _run(nc, [arrays], core_ids=[0])
    return tuple(r.results[0][f"out_{name}"] for name, _ in _OUTS)
```

```python
from contextlib import ExitStack

import concourse.bass as bass
from concourse import mybir

F32, F32R = mybir.dt.float32, mybir.dt.float32r
ALU = mybir.AluOpType
ACT = mybir.ActivationFunctionType
AX_X = mybir.AxisListType.X

P = 128
DEPTH, D = 2, 1024
NT = D // P
NPR, NS = 256, 8
T = NPR + NS
C = 64
NC = NPR // C
NROW = NS + 1
H_A, HD_A = 16, 64
H_B, HD_B = 8, 128
A_COLS = 3 * D + 64 + 64 + 128
A_TILES = A_COLS // P
Q_COLS = 3 * D
Q_TILES = Q_COLS // P
AB_COL = A_COLS + Q_COLS
Z_COL = AB_COL + 2 * H_B
IN_COLS = Z_COL + D + 2 * D
D_FF = 2816
FT = D_FF // P
PROJ = A_TILES + Q_TILES + 2 + 3 * NT
ADA_TILES = 9 * NT
FFN_RES = 0.5
RMS_EPS, L2A_EPS, L2B_EPS, GN_EPS = 1e-6, 1e-12, 1e-6, 6.4e-4
EXP_MHALF = 0.6065306597126334
RING = 5
TILE = NT * P
HI = 3
DOWN = ((0, 8), (8, 8), (16, 6))
ADA = (24, 34, 44, 72)
GRP = 4
UNITS = GRP * NC
HALVES = (slice(0, 64), slice(64, 128))
LN_EXP, SILU_TANH = "natural_log_exp_and_others", "silu_and_others"


class Signal:

    def __init__(self, sem, step=1):
        self.sem, self.step = sem, step
        self.reset()

    def reset(self):
        self.posted, self.taken = 0, {}

    def one(self):
        self.posted += 1
        return self.step

    def all(self):
        return self.at(self.posted)

    def next(self, eng, n=1):
        self.taken[id(eng)] = self.taken.get(id(eng), 0) + n
        return self.at(self.taken[id(eng)])

    def at(self, n):
        assert n > 0
        return self.step * n


def weight_plan():
    plan = [("ada", n) for n in range(ADA[0])]
    plan += [("up0", n) for n in range(2 * FT)] + [("down0", n) for n in range(3 * NT)]
    plan += [("ada", n) for n in range(ADA[0], ADA[2])]
    plan += [("in", n) for n in range(AB_COL // P)] + [("ab", 0), ("ab", 1)]
    plan += [("zg", n) for n in range((IN_COLS - Z_COL) // P)]
    plan += [("ada", n) for n in range(ADA[2], ADA[3])]
    plan += [("out", n) for n in range(NT)]
    plan += [("up1", n) for n in range(2 * FT)] + [("down1", n) for n in range(3 * NT)]
    return plan


def build(nc, I, O):
    ctx = ExitStack()
    with ctx:
        ctx.enter_context(nc.allow_non_contiguous_dma(reason="two [8] vectors a layer"))

        def sb(name, *free):
            return ctx.enter_context(nc.sbuf_tensor(name, [P, *free], F32))

        def sb_both(name, *free):
            with nc.sbuf_tensor(name, [P, *free], F32) as as_f32:
                pass
            return as_f32, ctx.enter_context(nc.sbuf_tensor(name + "_r", [P, *free], F32R))

        signals = []

        def signal(name, step=1):
            s = Signal(ctx.enter_context(nc.semaphore(name)), step)
            signals.append(s)
            return s

        ident = sb("ident", P)
        ident64 = sb("ident64", 64)
        mean_all = sb("mean_all", P)
        ones_all = sb("ones_all", P)
        ones_half = sb("ones_half", P)
        strict = sb("strict", 64)
        incl = sb("incl", 64)
        level = sb("level", 6, 64)
        carry = sb("carry", T)
        delta = sb("delta", NS)
        epsc = sb("epsc", 4)
        xT = sb("xT", NT, T)
        h, h_r = sb_both("h", NT, T)
        y = sb("y", NT, T)
        c9 = sb("c9", NT, NROW)
        ring, ring_r = sb_both("ring", RING, TILE)
        w_hi32, w_hi = sb_both("w_hi", HI, TILE)
        lora = w_hi32[:, 0:2, :].rearrange("p a n -> p (a n)")
        BIG_A, BIG_Q = A_TILES * (T + 1), Q_TILES * (T + 3)
        BIG_Z = NT * T
        big, big_r = sb_both("big", BIG_A + BIG_Q + 3 * BIG_Z)

        def part(buf, at, *shape):
            n = 1
            for s in shape:
                n *= s
            v = buf[:, at:at + n]
            if len(shape) == 2:
                return v.rearrange("p (a b) -> p a b", a=shape[0])
            if len(shape) == 3:
                return v.rearrange("p (a b c) -> p a b c", a=shape[0], b=shape[1])
            return v

        pa = part(big, 0, A_TILES, T + 1)
        qk = part(big, BIG_A, Q_TILES, T + 3)
        zs = part(big, BIG_A + BIG_Q, NT, T)
        gates = part(big, BIG_A + BIG_Q + BIG_Z, 2 * NT, T)
        hid_hi = part(big_r, 0, FT, T)
        hid_lo = part(big_r, FT * T, FT, T)
        sq_out = part(big, 0, NT, T)
        silu_g = part(big, 2 * FT * T, 2, T)
        h_lo = h_r[:, :, :]
        hi_ffn = part(big_r, (2 * FT + 2) * T, NT, T)
        hi_out = part(big_r, BIG_A, NT, T)
        mix = sb("mix", 8448)
        lt_all = part(mix, 0, UNITS, C)
        dm_all = part(mix, 1024, UNITS, C)
        pb_all = part(mix, 2048, UNITS, C)
        pk_all = part(mix, 3072, UNITS, C)
        vtok = part(mix, 4096, UNITS, C)
        ktok = part(mix, 5120, UNITS, C)
        btok = part(mix, 6144, UNITS, C)
        kdec_f = part(mix, 7168, GRP, NPR)
        m_st = part(mix, 8192, GRP, C)
        samp_both = [part(mix, 2048 * n, 32, C) for n in range(2)]
        samp_t = part(mix, 4096, 32, C)
        prow = part(mix, 4096, 3, P)
        strow = part(mix, 4480, 8, P)
        last = part(mix, 4096, 6, P)
        g_lt = part(mix, 0, UNITS, C)
        g_at = part(mix, 1024, UNITS, C)
        g_kd = part(mix, 2048, 2, H_B, HD_B)
        g_bv = part(mix, 4096, 2, H_B, HD_B)
        g_s = part(mix, 6144, H_B, HD_B)
        g_w = part(mix, 7168, H_B, HD_B)
        g_vn = part(big, 0, H_B, HD_B)
        g_eg = part(big, 1024, NT, T)
        g_tmp = part(big, 1024 + NT * T, 6, T)
        g_row = part(big, 1024 + (NT + 6) * T, 8, T)
        inv, inv_r = sb_both("inv", 4, UNITS, C)
        t_all, x_all, ltb, tt_all = (inv[:, n] for n in range(4))
        inv_f = inv[:, :, :, :].rearrange("p a b c -> p (a b c)")
        e2 = part(inv_f, 0, 2, T)
        lw = part(inv_f, 528, T)
        gc_i = part(inv_f, 792, T)
        e_x = part(inv_f, 1056, T)
        e_g = part(inv_f, 1320, T)
        e_n = part(inv_f, 1584, T)
        kkn = part(inv_f, 1848, T)
        b_f = part(inv_f, 2112, T)
        kd_f = part(inv_f, 2376, T)
        rkk = part(inv_f, 2640, T)
        sq_t = part(inv_f, 2904, T)
        rs_t = part(inv_f, 3168, T)
        kb_t = part(inv_f, 3432, T)
        gn_squares, gn_factors = (sq_t, kb_t), (rs_t, rkk)
        last_c = part(inv_f, 0, 498)
        hi_in = part(inv_r[:, :, :, :].rearrange("p a b c -> p (a b c)"), 1984, NT, T)
        convs = part(inv_f, 512, Q_TILES, NS)
        convt = part(inv_f, 704, Q_TILES, NS)
        rs2 = part(inv_f, 896, T)
        ws_a, us_a, mo_a = x_all[:, 0:GRP], x_all[:, GRP:2 * GRP], x_all[:, 2 * GRP:3 * GRP]
        gs_s = [part(inv_f, 1024 * n, NS, HD_B) for n in range(2)]
        gs_x = part(inv_f, 2048, NS, HD_B)
        sgt = part(inv_f, 3072, 2, P)
        rs = sb("rs", T)
        pcol = sb("pcol", 3 * P)
        ncol = sb("ncol", 3 * NT)
        modv = sb("modv", ADA_TILES, NROW)
        mod_a = sb("mod_a", 3 * NT, NROW)
        mod_g = sb("mod_g", 3 * NT, NROW)
        shp = sb("shp", A_TILES, NS)
        cvp = sb("cvp", Q_TILES, 3 * NS)
        sv = sb("sv", 6, NS, NT)
        svt = sb("svt", 6, C)
        ssm = sb("ssm", 2, C)
        eg_end = sb("eg_end", NT, NC)
        adt = sb("adt", 2)
        tks = sb("tks", 2, 4, H_B)
        abr = sb("abr", 2, T)
        beta_s = sb("beta_s", H_B, NS)
        qk_s = sb("qk_s", H_B, NS)
        sg = sb("sg", 4, NS)

        banks = [ctx.enter_context(nc.psum_tensor(f"bank{n}", [P, 512], F32)) for n in range(8)]

        bada = pcol[:, 0:72]
        npre, npost = pcol[:, 72:96], pcol[:, 96:120]
        mu = pcol[:, 128:154]
        w0, a0, k_k, k_a, r_k, ln_w, ln_b = (pcol[:, 154 + 8 * n:162 + 8 * n] for n in range(7))
        g_nw = pcol[:, 210:211]
        convw = pcol[:, 256:352].rearrange("p (i j) -> p i j", i=4)

        w_in_slot = [signal(f"w_in_slot{n}", 16) for n in range(RING)]
        lin_done = signal("lin_done")
        hi_ready = signal("hi_ready")
        lo_ready = signal("lo_ready")
        lora_w = signal("lora_w", 16)
        lora_done = signal("lora_done")
        rows_in = signal("rows_in", 16)
        masks_in = signal("masks_in", 16)
        consts = signal("consts")
        tr_done = signal("tr_done")
        cols_ready = signal("cols_ready")
        mod_ready = signal("mod_ready")
        x_ready = signal("x_ready")
        sq_ready = signal("sq_ready")
        ss_done = signal("ss_done")
        rs_ready = signal("rs_ready")
        h_ready = signal("h_ready")
        gate_taken = signal("gate_taken")
        hid_ready = signal("hid_ready")
        out_taken = signal("out_taken")
        pads = signal("pads")
        shifted = signal("shifted")
        conv_ready = signal("conv_ready")
        conv_done = signal("conv_done")
        last_tr = signal("last_tr")
        last_cp = signal("last_cp")
        st_out = signal("st_out", 16)
        kksq = signal("kksq")
        kkrs = signal("kkrs")
        ew_ready = signal("ew_ready")
        kkss = signal("kkss")
        bonss = signal("bonss")
        g_ready = signal("g_ready")
        eg_ready = signal("eg_ready")
        rkk_ready = signal("rkk_ready")
        ops_ready = signal("ops_ready")
        prod_done = signal("prod_done")
        prod_act = signal("prod_act")
        prod_dve = signal("prod_dve")
        bon_taken = signal("bon_taken")
        inv_pe = signal("inv_pe")
        inv_x = signal("inv_x")
        inv_t = signal("inv_t")
        m_ready = signal("m_ready")
        seq_pe = signal("seq_pe")
        seq_act = signal("seq_act")
        seq_dve = signal("seq_dve")
        sv_ready = signal("sv_ready")
        sv_pe = signal("sv_pe")
        svt_ready = signal("svt_ready")
        samp_in = [signal(f"samp_in{n}", 16) for n in range(2)]
        samp_done = signal("samp_done")
        samp_out = signal("samp_out", 16)
        gs_in = [signal(f"gs_in{n}", 16) for n in range(2)]
        gs_out = [signal(f"gs_out{n}", 16) for n in range(2)]
        ys_done = signal("ys_done")
        gn_mean, gn_cent, gn_sq, gn_sum, gn_rs, gn_out = (
            signal("gn_" + n) for n in ("mean", "cent", "sq", "sum", "rs", "out"))
        lora_in = signal("lora_in")
        gate_in = signal("gate_in")
        merged = signal("merged")
        rows_ready = signal("rows_ready")
        gdn_pe = signal("gdn_pe")
        gdn_act = signal("gdn_act")
        gdn_dve = signal("gdn_dve")
        last_rd = signal("last_rd")
        unit_sq = signal("unit_sq")
        unit_ss = signal("unit_ss")
        unit_rs = signal("unit_rs")
        unit_done = signal("unit_done")
        gc_done = signal("gc_done")
        gdn_rows_a = signal("gdn_rows_a")
        gdn_rows_d = signal("gdn_rows_d")
        gdn_ra = signal("gdn_ra")
        gdn_rd = signal("gdn_rd")
        act_chain = signal("act_chain")
        dve_chain = signal("dve_chain")
        pool_chain = signal("pool_chain")

        def end_of_part():
            nums = sorted(s.sem.num for s in signals)
            assert nums == list(range(nums[0], nums[-1] + 1))
            nc.all_engine_barrier()
            nc.gpsimd.sem_clear(range(nums[0], nums[-1] + 1))
            nc.all_engine_barrier()
            for s in signals:
                s.reset()

        def bc(ap, n):
            return ap.unsqueeze(2).to_broadcast([ap.shape[0], ap.shape[1], n])

        def bm(ap, n):
            return ap.unsqueeze(1).to_broadcast([ap.shape[0], n, ap.shape[1]])


        INV_PE, INV_ACT, INV_DVE = 2 + 4 * 5, 2 + 2 * 5, 1 + 3 * 5

        def inv_tiles(run):
            return g_lt if run == 2 else lt_all

        def batch(bt):
            return slice(8 * bt, 8 * bt + 8)

        def invert(pe, run):
            p0, a0_, d0 = run * INV_PE, run * INV_ACT, run * INV_DVE

            def products(bank, bt, lhs, rhs):
                for u in range(8):
                    for hf in HALVES:
                        r = ident64[hf, :] if rhs is None else rhs[hf, 8 * bt + u, :]
                        i = pe.matmul(banks[bank][hf, u * C:(u + 1) * C], lhs[hf, 8 * bt + u, :], r, start=True, stop=True)
                return i

            pe.wait_ge(inv_t.sem, inv_t.at(d0 + 1))
            for bt in range(2):
                products(4 + bt, bt, tt_all, None).then_inc(inv_pe.sem, inv_pe.one())
            for n in range(1, 6):
                for bt in range(2):
                    if n == 1:
                        pe.wait_ge(inv_t.sem, inv_t.at(d0 + 2))
                        pe.wait_ge(inv_x.sem, inv_x.at(a0_ + 1 + bt))
                    else:
                        pe.wait_ge(inv_t.sem, inv_t.at(d0 + 2 + 3 * (n - 2) + 2 + bt))
                    products(bt, bt, ltb, t_all).then_inc(inv_pe.sem, inv_pe.one())
                for bt in range(2):
                    pe.wait_ge(inv_x.sem, inv_x.at(a0_ + 2 * n + 1 + bt))
                    i = products(2 + bt, bt, x_all, tt_all)
                    if n < 5:
                        i = products(4 + bt, bt, tt_all, x_all)
                    i.then_inc(inv_pe.sem, inv_pe.one())
            pe.wait_ge(inv_t.sem, inv_t.at(d0 + INV_DVE))

        def invert_act(act, run):
            p0 = run * INV_PE
            for n in range(6):
                for bt in range(2):
                    dst, bank, at = (t_all, 4 + bt, 1 + bt) if n == 0 else (x_all, bt, 2 + 4 * (n - 1) + 1 + bt)
                    act.wait_ge(inv_pe.sem, inv_pe.at(p0 + at))
                    act.copy(dst[:, batch(bt), :], banks[bank][:, :].rearrange("p (u t) -> p u t", u=8)).then_inc(inv_x.sem, inv_x.one())
                    act.wait_ge(inv_x.sem, inv_x.all())

        def invert_dve(dve, run):
            p0, lt = run * INV_PE, inv_tiles(run)
            dve.tensor_tensor(ltb, lt, bm(level[:, 0, :], UNITS), ALU.mult).then_inc(dve_chain.sem, dve_chain.one())
            dve.wait_ge(dve_chain.sem, dve_chain.all())
            dve.tensor_tensor(tt_all, bm(ident64[:, :], UNITS), ltb, ALU.subtract).then_inc(inv_t.sem, inv_t.one())
            dve.wait_ge(inv_t.sem, inv_t.all())
            dve.tensor_tensor(ltb, lt, bm(level[:, 1, :], UNITS), ALU.mult).then_inc(inv_t.sem, inv_t.one())
            dve.wait_ge(inv_t.sem, inv_t.all())
            for n in range(1, 6):
                if n < 5:
                    dve.wait_ge(inv_pe.sem, inv_pe.at(p0 + 2 + 4 * (n - 1) + 2))
                    dve.tensor_tensor(ltb, lt, bm(level[:, n + 1, :], UNITS), ALU.mult).then_inc(inv_t.sem, inv_t.one())
                    dve.wait_ge(inv_t.sem, inv_t.all())
                for bt in range(2):
                    dve.wait_ge(inv_pe.sem, inv_pe.at(p0 + 2 + 4 * (n - 1) + 3 + bt))
                    us = batch(bt)
                    bank = [banks[2 * g + 2 + bt][:, :].rearrange("p (u t) -> p u t", u=8) for g in range(2)]
                    i = dve.tensor_tensor(tt_all[:, us, :], tt_all[:, us, :], bank[0], ALU.subtract)
                    if n < 5:
                        i = dve.tensor_tensor(t_all[:, us, :], t_all[:, us, :], bank[1], ALU.subtract)
                    i.then_inc(inv_t.sem, inv_t.one())
                    dve.wait_ge(inv_t.sem, inv_t.all())

        LAST = ((0, 26), (26, 104), (130, 104), (234, 72), (306, 96), (402, 96))
        GD_SEQ = H_B + 1 + 2 * NC
        GP_SAMP = 1 + H_B + 4 * NC + 1
        GP_POST = GP_SAMP + 3 * H_B

        with nc.Block() as block:
            @block.sync
            def _(sp):
                sp.dma_start(ring[:, 0:2, :],
                                          I["x_prompt"][0].rearrange("(a p) f -> p a f", p=P)).then_inc(rows_in.sem, rows_in.one())
                sp.dma_start(ring[0:8, 2, 0:P], I["c_prompt"].rearrange("b (j f) -> (b j) f", f=P)).then_inc(rows_in.sem, rows_in.one())
                sp.dma_start(ring[8:72, 2, 0:P], I["c_sample"].rearrange("b (j f) -> (b j) f", f=P)).then_inc(rows_in.sem, rows_in.one())
                sp.dma_start(ring[0:64, 2, P:2 * P],
                                          I["x_sample"].rearrange("b a (j f) -> (b a j) f", f=P)).then_inc(rows_in.sem, rows_in.one())

            @block.gpsimd
            def _(pool):
                for buf, value in ((ident, 0.0), (mean_all, 1.0 / D), (ones_all, 1.0), (ones_half, 0.0),
                                   (strict, 1.0), (incl, 1.0), (delta, 0.0)):
                    pool.memset(buf[:, :], value).then_inc(pool_chain.sem, pool_chain.one())
                    pool.wait_ge(pool_chain.sem, pool_chain.all())
                pool.memset(carry[:, :], 1.0).then_inc(pool_chain.sem, pool_chain.one())
                pool.wait_ge(pool_chain.sem, pool_chain.all())
                pool.memset(carry[:, 0:NPR].rearrange("p (c t) -> p c t", t=C)[:, :, 0:1], 0.0).then_inc(pool_chain.sem, pool_chain.one())
                pool.wait_ge(pool_chain.sem, pool_chain.all())
                pool.memset(carry[:, NPR:T], 0.0).then_inc(pool_chain.sem, pool_chain.one())
                pool.wait_ge(pool_chain.sem, pool_chain.all())
                pool.memset(level[:, :, :], 0.0).then_inc(pool_chain.sem, pool_chain.one())
                pool.wait_ge(pool_chain.sem, pool_chain.all())
                for n, value in enumerate((RMS_EPS, L2A_EPS, GN_EPS, 1.0)):
                    pool.memset(epsc[:, n:n + 1], value).then_inc(pool_chain.sem, pool_chain.one())
                    pool.wait_ge(pool_chain.sem, pool_chain.all())
                for half in HALVES:
                    pool.memset(ones_half[half, half], 1.0).then_inc(pool_chain.sem, pool_chain.one())
                    pool.wait_ge(pool_chain.sem, pool_chain.all())

                def select(v, pattern, base, mult, op, fill):
                    pool.affine_select(out=v, in_=v, pattern=pattern, base=base, channel_multiplier=mult,
                                       compare_op=op, fill=fill).then_inc(pool_chain.sem, pool_chain.one())
                    pool.wait_ge(pool_chain.sem, pool_chain.all())

                select(ident[:, :], [[-1, P]], 0, 1, ALU.not_equal, 1.0)
                select(delta[0:NS, :], [[-1, NS]], 0, 1, ALU.not_equal, 1.0)
                select(strict[0:64, :], [[1, 64]], 0, -1, ALU.is_gt, 0.0)
                select(incl[0:64, :], [[1, 64]], 0, -1, ALU.is_ge, 0.0)
                for n in range(6):
                    b = 1 << n
                    v = level[0:64, n, :].rearrange("p (a h t) -> p a h t", h=2, t=b)[:, :, 1, :]
                    pool.memset(v, 1.0).then_inc(pool_chain.sem, pool_chain.one())
                    pool.wait_ge(pool_chain.sem, pool_chain.all())
                    select(v, [[-2 * b, 32 // b], [0, b]], 0, 1, ALU.is_ge, 0.0)
                    select(v, [[2 * b, 32 // b], [0, b]], b - 1, -1, ALU.is_ge, 0.0)
                pool.memset(epsc[:, 3:4], 1.0).then_inc(consts.sem, consts.one())

            @block.tensor
            def _(pe):
                pe.wait_ge(rows_in.sem, rows_in.at(4))
                pe.wait_ge(consts.sem, consts.next(pe))
                for a in range(2):
                    for j in range(NT):
                        n = a * NT + j
                        tr = pe.transpose(banks[n // 4][:, (n % 4) * P:(n % 4 + 1) * P],
                                          ring[:, a, j * P:(j + 1) * P], ident[:, :])
                pe.transpose(banks[4][:, 0:72], ring[0:72, 2, 0:P], ident[0:72, 0:72])
                tr = pe.transpose(banks[5][:, 0:64], ring[0:64, 2, P:2 * P], ident[0:64, 0:64])
                tr.then_inc(tr_done.sem, tr_done.one())

            @block.scalar
            def _(act):
                act.wait_ge(consts.sem, consts.next(act))
                for buf in (strict, incl):
                    act.dma_start(buf[64:128, :], buf[0:64, :]).then_inc(masks_in.sem, masks_in.one())
                act.dma_start(level[64:128, :, :], level[0:64, :, :]).then_inc(masks_in.sem, masks_in.one())
                act.wait_ge(masks_in.sem, masks_in.next(act, 3))
                act.wait_ge(tr_done.sem, tr_done.next(act))
                for n in range(4):
                    a, j = n // 2, 4 * (n % 2)
                    act.copy(xT[:, j:j + 4, a * P:(a + 1) * P], banks[n][:, :].rearrange("p (j t) -> p j t", j=4))
                act.copy(xT[:, :, NPR:T], banks[5][:, 0:64].rearrange("p (b j) -> p j b", j=NT))
                act.activation(c9[:, :, :], banks[4][:, 0:72].rearrange("p (r j) -> p j r", j=NT), ACT.Silu)

            @block.vector
            def _(dve):
                dve.wait_ge(consts.sem, consts.next(dve))
                dve.tensor_tensor(ident64[:, :], ident[:, 0:64], ident[:, 64:128], ALU.add)

        end_of_part()

        with nc.Fori(0, DEPTH) as l:
            plan = weight_plan()
            where = {key: n for n, key in enumerate(plan)}
            splits = [key for key in plan if key[0] != "ada"]
            split_no = {key: m for m, key in enumerate(splits)}
            run_ends = (split_no[("in", 0)], split_no[("out", 0)], len(splits))

            def tile_size(kind, t):
                return (DOWN[t % 3][1] if kind[:4] == "down" else NT), (8 if kind == "ab" else P)

            def loaded(eng, n):
                eng.wait_ge(w_in_slot[n % RING].sem, w_in_slot[n % RING].at(n // RING + 1))

            def high(act, m):
                kind, t = splits[m]
                n, (kt, cols) = where[(kind, t)], tile_size(kind, t)
                loaded(act, n)
                if m >= HI:
                    act.wait_ge(lin_done.sem, lin_done.at(where[splits[m - HI]] + 1))
                size = kt * cols
                act.copy(w_hi[:, m % HI, 0:size], ring[:, n % RING, 0:size]).then_inc(hi_ready.sem, hi_ready.one())

            def low(dve, m):
                kind, t = splits[m]
                n, (kt, cols) = where[(kind, t)], tile_size(kind, t)
                size = kt * cols
                dve.wait_ge(hi_ready.sem, hi_ready.at(m + 1))
                w = ring[:, n % RING, 0:size]
                dve.tensor_tensor(ring_r[:, n % RING, 0:size], w, w_hi[:, m % HI, 0:size].bitcast(F32), ALU.subtract).then_inc(lo_ready.sem, lo_ready.one())

            def conv_turn(n):
                first = A_TILES + NT
                return first + (PROJ - first) * n // Q_TILES

            def ahead(eng, part_of, key):
                m = split_no[key] + 2
                if m < len(splits) and m not in run_ends and m - 1 not in run_ends:
                    part_of(eng, m)

            with nc.Block() as block:
                @block.sync
                def _(sp):
                    def k_tiles(w, c0, n):
                        return w[l, :, c0:c0 + n].rearrange("(k p) n -> p k n", p=P)

                    def load(n):
                        kind, t = plan[n]
                        kt, cols = tile_size(kind, t)
                        into = w_in_slot[n % RING]
                        if n >= RING:
                            sp.wait_ge(lin_done.sem, lin_done.at(n - RING + 1))
                        if kind == "ada":
                            src = k_tiles(I["w_ada"], P * t, P)
                        elif kind in ("up0", "up1"):
                            src = k_tiles(I["ffn_up"][:, int(kind[2])], (t % 2) * D_FF + t // 2 * P, P)
                        elif kind in ("down0", "down1"):
                            k0, o = DOWN[t % 3][0], t // 3
                            src = I["ffn_down"][l, int(kind[4])][k0 * P:(k0 + kt) * P, o * P:(o + 1) * P].rearrange(
                                "(k p) n -> p k n", p=P)
                        elif kind == "out":
                            src = k_tiles(I["w_out"], P * t, P)
                        else:
                            src = k_tiles(I["w_in"], {"in": 0, "ab": AB_COL, "zg": Z_COL}[kind] + cols * t, cols)
                        sp.dma_start(ring[:, n % RING, 0:kt * cols].rearrange("p (k n) -> p k n", k=kt), src).then_inc(into.sem, into.one())

                    first_c = where[("ada", ADA[2])]
                    for n in range(first_c):
                        load(n)
                    sp.wait_ge(lin_done.sem, lin_done.at(first_c))
                    sp.dma_start(lora[0:64, 0:D], I["rwkv_w2"][l]).then_inc(lora_w.sem, lora_w.one())
                    sp.dma_start(lora[64:128, 0:D], I["rwkv_a2"][l]).then_inc(lora_w.sem, lora_w.one())
                    sp.dma_start(lora[:, D:2 * D], I["rwkv_g2"][l]).then_inc(lora_w.sem, lora_w.one())
                    for n in range(first_c, len(plan)):
                        load(n)

                @block.tensor
                def _(pe):
                    def mm(out, lhsT, rhs, start=True, stop=True):
                        return pe.matmul(out, lhsT, rhs, start=start, stop=stop)

                    def linear(out, key, x_hi, x_lo, start=True, stop=True):
                        m, n = split_no[key], where[key]
                        kt, cols = tile_size(*key)
                        pe.wait_ge(lo_ready.sem, lo_ready.at(m + 1))
                        hi = w_hi[:, m % HI, 0:kt * cols].rearrange("p (k n) -> p k n", k=kt)
                        lo = ring_r[:, n % RING, 0:kt * cols].rearrange("p (k n) -> p k n", k=kt)
                        for k in range(kt):
                            mm(out, hi[:, k, :], x_hi[:, k, :], start and k == 0, False)
                            mm(out, hi[:, k, :], x_lo[:, k, :], False, False)
                            i = mm(out, lo[:, k, :], x_hi[:, k, :], False, stop and k == kt - 1)
                        i.then_inc(lin_done.sem, lin_done.one())

                    def conditioning(part, bank, at):
                        first = ADA[part - 1] if part else 0
                        blocks(first, ADA[part], bank, at)

                    def blocks(first, last, bank, at):
                        for m in range(first, last):
                            n = where[("ada", m)]
                            loaded(pe, n)
                            w = ring[:, n % RING, :].rearrange("p (k n) -> p k n", k=NT)
                            for half in HALVES:
                                out = banks[bank][half, at + (m - first) * NROW:at + (m - first + 1) * NROW]
                                for k in range(NT):
                                    i = mm(out, w[:, k, half], c9[:, k, :], k == 0, k == NT - 1)
                            i.then_inc(lin_done.sem, lin_done.one())

                    pe.wait_ge(rows_in.sem, rows_in.at(17))
                    for g, rows in enumerate((120, 83, 96)):
                        pe.transpose(banks[6][:, g * P:g * P + rows], prow[0:rows, g, :], ident[0:rows, 0:rows])
                    for n in range(2):
                        pe.transpose(banks[7][:, n * 104:(n + 1) * 104], strow[0:104, n, :], ident[0:104, 0:104])
                    for n in range(6):
                        out = banks[7][:, 208 + n * 96:304 + n * 96] if n < 3 else banks[3][:, (n - 3) * 96:(n - 2) * 96]
                        tr = pe.transpose(out, strow[0:96, 2 + n, :], ident[0:96, 0:96])
                    tr.then_inc(tr_done.sem, tr_done.one())

                    def mean_square():
                        pe.wait_ge(sq_ready.sem, sq_ready.next(pe))
                        for k in range(NT):
                            i = mm(banks[7][:, 0:T], mean_all[:, :], h[:, k, :], k == 0, k == NT - 1)
                        i.then_inc(ss_done.sem, ss_done.one())

                    def mean_square_tiles(buf):
                        for k in range(NT):
                            pe.wait_ge(sq_ready.sem, sq_ready.next(pe))
                            i = mm(banks[7][:, 0:T], mean_all[:, :], buf[:, k, :], k == 0, k == NT - 1)
                        i.then_inc(ss_done.sem, ss_done.one())

                    def ffn(i_ffn):
                        pe.wait_ge(h_ready.sem, h_ready.next(pe))
                        for t in range(FT):
                            for g in range(2):
                                if t >= 2:
                                    read = gate_taken if g == 0 else hid_ready
                                    pe.wait_ge(read.sem, read.at(i_ffn * FT + t - 1))
                                linear(banks[2 * g + t % 2][:, 0:T], (f"up{i_ffn}", 2 * t + g), hi_ffn, h_lo)
                        pe.wait_ge(hid_ready.sem, hid_ready.at((i_ffn + 1) * FT))
                        base = 0 if i_ffn == 0 else out_base[1]
                        for o in range(NT):
                            if o >= 4:
                                pe.wait_ge(out_taken.sem, out_taken.at(base + o - 3))
                            for n, (k0, kt) in enumerate(DOWN):
                                linear(banks[o % 4][:, 0:T], (f"down{i_ffn}", 3 * o + n), hid_hi[:, k0:k0 + kt],
                                       hid_lo[:, k0:k0 + kt], n == 0, n == 2)
                        mean_square_tiles(h)

                    pe.wait_ge(cols_ready.sem, cols_ready.next(pe))
                    out_base = (0, NT + PROJ + NT)
                    mean_square()
                    conditioning(0, 4, 0)
                    ffn(0)

                    conditioning(1, 5, 0)
                    mean_square()
                    conditioning(2, 5, (ADA[1] - ADA[0]) * NROW)
                    pe.wait_ge(h_ready.sem, h_ready.next(pe))
                    pe.wait_ge(pads.sem, pads.next(pe))
                    n_out = 0
                    base = NT
                    for kind, count in (("in", AB_COL // P), ("ab", 2), ("zg", (IN_COLS - Z_COL) // P)):
                        for t in range(count):
                            pe.wait_ge(out_taken.sem, out_taken.at(base + n_out - 3))
                            rows = tile_size(kind, t)[1]
                            linear(banks[n_out % 4][0:rows, 0:T], (kind, t), hi_in, h_lo)
                            n_out += 1

                    pe.wait_ge(last_cp.sem, last_cp.next(pe, 2))
                    for n, (at, count) in enumerate(LAST):
                        i = pe.transpose(banks[4 + n // 4][0:count, (n % 4) * P:(n % 4 + 1) * P],
                                         last_c[:, at:at + count], ident[:, :])
                    i.then_inc(last_tr.sem, last_tr.one())
                    pe.wait_ge(last_rd.sem, last_rd.next(pe))

                    pe.wait_ge(lora_w.sem, lora_w.next(pe, 3))
                    pe.wait_ge(lora_in.sem, lora_in.next(pe))

                    def loras(j):
                        mm(banks[0][:, 0:T], lora[0:64, j * P:(j + 1) * P], pa[0:64, 24, 1:T + 1]).then_inc(lora_done.sem, lora_done.one())
                        mm(banks[1][:, 0:T], lora[64:128, j * P:(j + 1) * P], pa[64:128, 24, 1:T + 1]).then_inc(lora_done.sem, lora_done.one())
                        pe.wait_ge(kksq.sem, kksq.next(pe))
                        mm(banks[2][:, 0:T], ones_half[:, :], sq_t).then_inc(kkss.sem, kkss.one())

                    for q in range(NT // GRP):
                        loras(GRP * q)
                        for jj in range(GRP):
                            j = GRP * q + jj
                            pe.wait_ge(rkk_ready.sem, rkk_ready.next(pe))
                            mm(banks[3][:, 0:T], ones_half[:, :], rkk).then_inc(bonss.sem, bonss.one())
                            if jj + 1 < GRP:
                                loras(j + 1)
                            if j:
                                pe.wait_ge(prod_act.sem, prod_act.at(j))
                                pe.wait_ge(prod_dve.sem, prod_dve.at(j))
                            if j < NT - 1:
                                per = (ADA[3] - ADA[2]) // (NT - 1)
                                blocks(ADA[2] + per * j, ADA[2] + per * (j + 1), 7, 256 + per * j * NROW)
                            pe.wait_ge(ops_ready.sem, ops_ready.next(pe))
                            for c in range(NC):
                                t0, u0 = c * C, c * C
                                for hf in HALVES:
                                    kt = kdec_f[hf, jj, t0:t0 + C]
                                    rt = pa[hf, j, 1 + t0:1 + t0 + C]
                                    mm(banks[4][hf, u0:u0 + C], b_f[hf, t0:t0 + C], kt)
                                    mm(banks[4][hf, 256 + u0:256 + u0 + C], b_f[hf, t0:t0 + C], rt)
                                    mm(banks[5][hf, u0:u0 + C], kd_f[hf, t0:t0 + C], kt)
                                    mm(banks[5][hf, 256 + u0:256 + u0 + C], kd_f[hf, t0:t0 + C], rt)
                                    mm(banks[6][hf, u0:u0 + C], pa[hf, 16 + j, 1 + t0:1 + t0 + C], ident64[hf, :])
                                    mm(banks[6][hf, 256 + u0:256 + u0 + C], kd_f[hf, t0:t0 + C], ident64[hf, :])
                                    i = mm(banks[7][hf, u0:u0 + C], b_f[hf, t0:t0 + C], ident64[hf, :])
                            i.then_inc(prod_done.sem, prod_done.one())
                        pe.wait_ge(prod_act.sem, prod_act.at(GRP * (q + 1)))
                        pe.wait_ge(prod_dve.sem, prod_dve.at(GRP * (q + 1)))
                        invert(pe, q)
                        for c in range(NC):
                            t0 = c * C
                            pe.wait_ge(seq_dve.sem, seq_dve.next(pe))
                            for jj in range(GRP):
                                u = jj * NC + c
                                for hf in HALVES:
                                    out = banks[0][hf, jj * C:(jj + 1) * C]
                                    mm(out, kdec_f[hf, jj, t0:t0 + C], m_st[hf, jj, :], True, False)
                                    i = mm(out, dm_all[hf, u, :], vtok[hf, u, :], False, True)
                            i.then_inc(seq_pe.sem, seq_pe.one())
                            pe.wait_ge(seq_act.sem, seq_act.next(pe))
                            for jj in range(GRP):
                                for hf in HALVES:
                                    i = mm(banks[1][hf, jj * C:(jj + 1) * C], tt_all[hf, jj * NC + c, :], ws_a[hf, jj, :])
                            i.then_inc(seq_pe.sem, seq_pe.one())
                            pe.wait_ge(seq_act.sem, seq_act.next(pe))
                            for jj in range(GRP):
                                u, j = jj * NC + c, GRP * q + jj
                                for hf in HALVES:
                                    out = banks[2][hf, jj * C:(jj + 1) * C]
                                    mm(out, m_st[hf, jj, :], pa[hf, j, 1 + t0:1 + t0 + C], True, False)
                                    mm(out, us_a[hf, jj, :], pb_all[hf, u, :], False, False)
                                    i = mm(out, vtok[hf, u, :], pk_all[hf, u, :], False, True)
                            i.then_inc(seq_pe.sem, seq_pe.one())
                            for jj in range(GRP):
                                u = jj * NC + c
                                for hf in HALVES:
                                    out = banks[3][hf, jj * C:(jj + 1) * C]
                                    mm(out, btok[hf, u, :], us_a[hf, jj, :], True, False)
                                    i = mm(out, ktok[hf, u, :], vtok[hf, u, :], False, True)
                            i.then_inc(seq_pe.sem, seq_pe.one())
                        pe.wait_ge(seq_dve.sem, seq_dve.next(pe))
                        for jj in range(GRP):
                            for hf in HALVES:
                                i = mm(banks[0][hf, jj * C:(jj + 1) * C], m_st[hf, jj, :], ident64[hf, :])
                        i.then_inc(seq_pe.sem, seq_pe.one())
                        pe.wait_ge(seq_act.sem, seq_act.next(pe))

                    for n in range(6):
                        for hf in HALVES:
                            i = mm(banks[4][hf, n * C:(n + 1) * C],
                                   sv[hf, n, :, :].rearrange("p b j -> p (b j)"), ident64[hf, :])
                    i.then_inc(sv_pe.sem, sv_pe.one())
                    pe.wait_ge(samp_done.sem, samp_done.next(pe, 2))
                    for hf in HALVES:
                        i = mm(banks[5][hf, 0:64], ssm[hf, 1, :], ident64[hf, :])
                    i.then_inc(sv_pe.sem, sv_pe.one())
                    pe.wait_ge(ys_done.sem, ys_done.next(pe))

                    pe.wait_ge(gate_in.sem, gate_in.next(pe))
                    def means(j):
                        if j >= 2:
                            pe.wait_ge(gn_cent.sem, gn_cent.at(j - 1))
                        mm(banks[3 * (j % 2)][:, 0:T], ones_half[:, :], h[:, j, :]).then_inc(gn_mean.sem, gn_mean.one())
                        if j >= 2:
                            pe.wait_ge(gn_out.sem, gn_out.at(j - 1))
                        mm(banks[2 + 3 * (j % 2)][:, 0:T], lora[:, D + j * P:D + (j + 1) * P], pa[:, 25, 1:T + 1]).then_inc(lora_done.sem, lora_done.one())

                    means(0)
                    for j in range(NT):
                        if j + 1 < NT:
                            means(j + 1)
                        pe.wait_ge(gn_sq.sem, gn_sq.next(pe))
                        if j >= 2:
                            pe.wait_ge(gn_rs.sem, gn_rs.at(j - 1))
                        mm(banks[1 + 3 * (j % 2)][:, 0:T], ones_half[:, :], gn_squares[j % 2]).then_inc(gn_sum.sem, gn_sum.one())
                    pe.wait_ge(gn_out.sem, gn_out.at(NT))

                    pe.wait_ge(rows_ready.sem, rows_ready.next(pe))
                    for a in range(2):
                        for n, r in enumerate((0, 1, 2, 7)):
                            i = pe.transpose(banks[7][:, (a * 4 + n) * H_B:(a * 4 + n + 1) * H_B],
                                             g_row[0:H_B, r, a * P:(a + 1) * P], ident[0:H_B, 0:H_B])
                    i.then_inc(gdn_pe.sem, gdn_pe.one())
                    for u in range(2 * H_B):
                        pe.wait_ge(unit_sq.sem, unit_sq.next(pe))
                        if u >= 2:
                            pe.wait_ge(unit_rs.sem, unit_rs.at(u - 1))
                        mm(banks[u % 2][:, 0:T], ones_all[:, :], g_tmp[:, u % 2, :]).then_inc(unit_ss.sem, unit_ss.one())

                    def spread(n):
                        head = ident[0:H_B, n:n + 1].to_broadcast([H_B, P])
                        mm(banks[2][:, 0:T], head, g_row[0:H_B, 0, :])
                        mm(banks[3][:, 0:T], head, g_row[0:H_B, 1, :]).then_inc(gc_done.sem, gc_done.one())

                    spread(0)
                    for n in range(H_B):
                        pe.wait_ge(gdn_rd.sem, gdn_rd.next(pe))
                        pe.wait_ge(gdn_ra.sem, gdn_ra.at(2 * n + 1))
                        if n + 1 < H_B:
                            spread(n + 1)
                        if n:
                            pe.wait_ge(gdn_dve.sem, gdn_dve.next(pe))
                        kb = g_tmp[:, 2 * ((n + 1) % 2), :]
                        for c in range(NC):
                            hf, cp = HALVES[c % 2], c // 2
                            k_c = qk[:, 8 + n, 3 + c * C:3 + (c + 1) * C]
                            mm(banks[4][hf, cp * C:(cp + 1) * C], k_c, kb[:, c * C:(c + 1) * C])
                            mm(banks[4][hf, 128 + cp * C:128 + (cp + 1) * C], k_c, qk[:, n, 3 + c * C:3 + (c + 1) * C])
                        for cp in range(2):
                            pe.transpose(banks[5][:, cp * P:(cp + 1) * P], qk[:, 8 + n, 3 + cp * P:3 + (cp + 1) * P], ident[:, :])
                            i = pe.transpose(banks[5][:, 256 + cp * P:256 + (cp + 1) * P],
                                             qk[:, 16 + n, 3 + cp * P:3 + (cp + 1) * P], ident[:, :])
                        i.then_inc(gdn_pe.sem, gdn_pe.one())
                    pe.wait_ge(gdn_dve.sem, gdn_dve.next(pe))
                    invert(pe, 2)
                    for c in range(NC):
                        hf, cp = HALVES[c % 2], c // 2
                        pe.wait_ge(gdn_dve.sem, gdn_dve.next(pe))
                        for n in range(H_B):
                            i = mm(banks[n // 4][hf, (n % 4) * P:(n % 4 + 1) * P], qk[:, 8 + n, 3 + c * C:3 + (c + 1) * C], g_s[:, n, :])
                        i.then_inc(gdn_pe.sem, gdn_pe.one())
                        pe.wait_ge(gdn_dve.sem, gdn_dve.next(pe))
                        for n in range(H_B):
                            i = mm(banks[2 + n // 4][hf, (n % 4) * P:(n % 4 + 1) * P], tt_all[hf, 2 * n + cp, :], g_w[hf, n, :])
                        i.then_inc(gdn_pe.sem, gdn_pe.one())
                        pe.wait_ge(gdn_act.sem, gdn_act.next(pe))
                        for n in range(H_B):
                            for half in HALVES:
                                out = banks[4][half, n * C:(n + 1) * C]
                                mm(out, g_s[:, n, half], qk[:, n, 3 + c * C:3 + (c + 1) * C], True, False)
                                i = mm(out, g_vn[hf, n, half], g_at[hf, 2 * n + cp, :], False, True)
                        i.then_inc(gdn_pe.sem, gdn_pe.one())
                        for n in range(H_B):
                            i = mm(banks[5 + n // 4][:, (n % 4) * P:(n % 4 + 1) * P], g_kd[hf, cp, n, :], g_vn[hf, n, :])
                        i.then_inc(gdn_pe.sem, gdn_pe.one())
                    pe.wait_ge(gdn_dve.sem, gdn_dve.next(pe))
                    mm(banks[7][:, 0:64], ones_all[:, :], qk_s[:, :, :].rearrange("p n b -> p (n b)")).then_inc(gdn_pe.sem, gdn_pe.one())
                    pe.wait_ge(gdn_dve.sem, gdn_dve.next(pe))
                    for n in range(H_B):
                        pe.wait_ge(gs_in[n % 2].sem, gs_in[n % 2].next(pe))
                        for b in range(NS):
                            for half in HALVES:
                                i = mm(banks[0][half, 2 * b:2 * b + 2], gs_s[n % 2][:, b, half], qk[:, n:n + 9:8, 259 + b])
                        i.then_inc(gdn_pe.sem, gdn_pe.one())
                        pe.wait_ge(gdn_dve.sem, gdn_dve.next(pe))
                        pe.transpose(banks[1][0:NS, 0:P], sg[:, 1, :], ident[:, :])
                        pe.transpose(banks[1][0:NS, P:2 * P], qk[:, 8 + n, 259:267], ident[:, :]).then_inc(gdn_pe.sem, gdn_pe.one())
                        pe.wait_ge(gdn_dve.sem, gdn_dve.next(pe))
                        mm(banks[2][:, :], sgt[0:NS, 1, :], gs_x[0:NS, 0:4, :].rearrange("p b v -> p (b v)"))
                        mm(banks[3][:, :], sgt[0:NS, 1, :], gs_x[0:NS, 4:8, :].rearrange("p b v -> p (b v)")).then_inc(gdn_pe.sem, gdn_pe.one())
                        pe.wait_ge(gdn_dve.sem, gdn_dve.next(pe))
                    for n in range(H_B):
                        pe.wait_ge(gdn_act.sem, gdn_act.next(pe))
                        mm(banks[4 + n % 2][:, 0:T], ones_all[:, :], g_tmp[:, n % 2, :]).then_inc(gdn_pe.sem, gdn_pe.one())

                    pe.wait_ge(merged.sem, merged.at(NT))
                    base = NT + n_out
                    for o in range(NT):
                        if o >= 4:
                            pe.wait_ge(out_taken.sem, out_taken.at(base + o - 3))
                        linear(banks[o % 4][:, 0:T], ("out", o), hi_out, h_lo)
                    mean_square_tiles(sq_out)
                    mean_square()
                    ffn(1)

                @block.scalar
                def _(act):
                    def row_load(dst, src):
                        act.dma_start(dst, src).then_inc(rows_in.sem, rows_in.one())

                    def tiles(ap):
                        return ap.rearrange("(j f) -> j f", f=P)

                    row_load(prow[0:72, 0, :], tiles(I["b_ada"][l]))
                    row_load(prow[72:96, 0, :], I["norm_pre"][l].rearrange("s (j f) -> (s j) f", f=P))
                    row_load(prow[96:120, 0, :], I["norm_post"][l].rearrange("s (j f) -> (s j) f", f=P))
                    row_load(prow[0:26, 1, :], tiles(I["rwkv_mu"][l]))
                    for n, name in enumerate(("w0", "a0", "k_k", "k_a")):
                        row_load(prow[26 + 8 * n:34 + 8 * n, 1, :], tiles(I["rwkv_" + name][l]))
                    row_load(prow[58:66, 1, :], I["rwkv_r_k"][l].rearrange("(j g) d -> j (g d)", g=2))
                    for n, name in enumerate(("ln_w", "ln_b")):
                        row_load(prow[66 + 8 * n:74 + 8 * n, 1, :], tiles(I["rwkv_" + name][l]))
                    row_load(prow[82:83, 1, :], tiles(I["gdn_norm_w"][l]))
                    row_load(prow[0:96, 2, :], I["gdn_conv"][l].rearrange("i (j f) -> (i j) f", f=P))
                    row_load(adt[0:8, 0:1], I["gdn_a_log"][l].rearrange("(h a) -> h a", a=1))
                    row_load(adt[0:8, 1:2], I["gdn_dt_bias"][l].rearrange("(h a) -> h a", a=1))
                    row_load(strow[0:104, 0:2, :],
                             I["state_rwkv_shift"][l].rearrange("(n b) (j f) -> (b j) n f", n=2, f=P))
                    row_load(strow[0:96, 2:8, :],
                             I["state_gdn_conv"][l].rearrange("b i (j f) -> (b i j) f", f=P).rearrange("(n q) f -> q n f", n=6))
                    act.dma_start(O["sample_gdn_conv"][l, :, 0:2, :], I["state_gdn_conv"][l, :, 1:3, :]).then_inc(st_out.sem, st_out.one())

                    def rsqrt(out, ss, scale, eps):
                        act.activation(out, ss, ACT.Ln, bias=epsc[:, eps:eps + 1], scale=scale).then_inc(act_chain.sem, act_chain.one())
                        act.wait_ge(act_chain.sem, act_chain.all())
                        return act.activation(out, out, ACT.Exp, scale=-0.5)

                    def normalise(square_x):
                        act.preload_act_table_set(LN_EXP)
                        if square_x:
                            act.wait_ge(x_ready.sem, x_ready.next(act))
                            act.activation(h[:, :, :], xT[:, :, :], ACT.Square).then_inc(sq_ready.sem, sq_ready.one())
                            act.wait_ge(sq_ready.sem, sq_ready.all())
                        act.wait_ge(ss_done.sem, ss_done.next(act))
                        rsqrt(rs[:, :], banks[7][:, 0:T], 1.0, 0).then_inc(rs_ready.sem, rs_ready.one())
                        act.wait_ge(rs_ready.sem, rs_ready.all())

                    def ffn(i_ffn):
                        act.preload_act_table_set(SILU_TANH)
                        for t in range(FT):
                            for g in range(2):
                                ahead(act, high, (f"up{i_ffn}", 2 * t + g))
                            act.wait_ge(lin_done.sem, lin_done.at(where[(f"up{i_ffn}", 2 * t)] + 1))
                            if t >= 2:
                                act.wait_ge(hid_ready.sem, hid_ready.at(i_ffn * FT + t - 1))
                            act.activation(silu_g[:, t % 2, :], banks[t % 2][:, 0:T], ACT.Silu).then_inc(gate_taken.sem, gate_taken.one())
                            act.wait_ge(gate_taken.sem, gate_taken.all())
                        for o in range(NT):
                            for n in range(3):
                                ahead(act, high, (f"down{i_ffn}", 3 * o + n))
                            act.wait_ge(lin_done.sem, lin_done.at(where[(f"down{i_ffn}", 3 * o + 2)] + 1))
                            act.copy(y[:, o, :], banks[o % 4][:, 0:T]).then_inc(out_taken.sem, out_taken.one())
                            act.wait_ge(out_taken.sem, out_taken.all())
                            act.activation(h[:, o, :], y[:, o, :], ACT.Square).then_inc(sq_ready.sem, sq_ready.one())
                            act.wait_ge(sq_ready.sem, sq_ready.all())
                        normalise(False)

                    normalise(True)
                    for m in range(2):
                        high(act, m)
                    ffn(0)
                    normalise(True)
                    act.preload_act_table_set(SILU_TANH)
                    for m in range(2):
                        high(act, run_ends[0] + m)
                    n0 = where[("in", 0)]
                    for n in range(PROJ):
                        ahead(act, high, plan[n0 + n])
                        act.wait_ge(lin_done.sem, lin_done.at(n0 + n + 1))
                        src = banks[n % 4][:, 0:T]
                        if n == 0:
                            act.wait_ge(pads.sem, pads.at(1))
                        if n < A_TILES:
                            i = act.copy(pa[:, n, 1:T + 1], src)
                        elif n < A_TILES + Q_TILES:
                            i = act.copy(qk[:, n - A_TILES, 3:T + 3], src)
                        elif n < A_TILES + Q_TILES + 2:
                            i = act.copy(abr[0:8, n - A_TILES - Q_TILES, :], banks[n % 4][0:8, 0:T])
                        else:
                            m = n - A_TILES - Q_TILES - 2
                            if m < NT:
                                i = act.activation(zs[:, m, :], src, ACT.Silu)
                            else:
                                i = act.activation(gates[:, m - NT, :], src, ACT.Tanh, scale=0.5)
                        i.then_inc(out_taken.sem, out_taken.one())
                        act.wait_ge(out_taken.sem, out_taken.all())
                        for m in range(Q_TILES):
                            if n == min(conv_turn(m + 1) + 1, PROJ - 1):
                                act.wait_ge(conv_ready.sem, conv_ready.next(act))
                                act.activation(qk[:, m, 3:T + 3], (rs[:, :], rs2)[m % 2], ACT.Silu).then_inc(conv_done.sem, conv_done.one())
                                act.wait_ge(conv_done.sem, conv_done.all())
                    act.wait_ge(last_tr.sem, last_tr.next(act))
                    for n, (_, count) in enumerate(LAST):
                        i = act.copy(last[0:count, n, :], banks[4 + n // 4][0:count, (n % 4) * P:(n % 4 + 1) * P])
                    i.then_inc(last_rd.sem, last_rd.one())
                    act.wait_ge(last_rd.sem, last_rd.all())
                    LO = ((O["prompt_rwkv_shift"][l].rearrange("b (j f) -> (b j) f", f=P), 26, 0),
                          (O["sample_rwkv_shift"][l, 0:4].rearrange("b (j f) -> (b j) f", f=P), 104, 1),
                          (O["sample_rwkv_shift"][l, 4:8].rearrange("b (j f) -> (b j) f", f=P), 104, 2),
                          (O["prompt_gdn_conv"][l, 0].rearrange("i (j f) -> (i j) f", f=P), 72, 3))
                    for dst, rows, n in LO:
                        act.dma_start(dst, last[0:rows, n, :]).then_inc(st_out.sem, st_out.one())
                    for n in range(2):
                        for b in range(4):
                            act.dma_start(
                                O["sample_gdn_conv"][l, 4 * n + b, 2].rearrange("(j f) -> j f", f=P),
                                last[24 * b:24 * b + 24, 4 + n, :]).then_inc(st_out.sem, st_out.one())
                    act.wait_ge(st_out.sem, st_out.all())
                    act.wait_ge(shifted.sem, shifted.next(act, A_TILES // 2))
                    act.activation(pa[0:64, 24, 1:T + 1], pa[0:64, 24, 1:T + 1], ACT.Tanh)
                    act.activation(pa[:, 25, 1:T + 1], pa[:, 25, 1:T + 1], ACT.Tanh, scale=0.5).then_inc(lora_in.sem, lora_in.one())
                    act.wait_ge(lora_in.sem, lora_in.all())
                    act.preload_act_table_set(LN_EXP)

                    def rates(j):
                        act.activation(sq_t, pa[:, 8 + j, 1:T + 1], ACT.Square, scale=k_k[:, j:j + 1]).then_inc(kksq.sem, kksq.one())
                        act.wait_ge(kksq.sem, kksq.all())
                        act.wait_ge(lora_done.sem, lora_done.at(2 * j + 2))
                        if j:
                            act.wait_ge(rkk_ready.sem, rkk_ready.at(j))
                        act.activation(e2[:, 0, :], banks[0][:, 0:T], ACT.Exp, bias=ncol[:, j:j + 1], scale=-1.0)
                        act.activation(e2[:, 1, :], banks[1][:, 0:T], ACT.Exp,
                                       bias=ncol[:, NT + j:NT + j + 1], scale=-1.0).then_inc(act_chain.sem, act_chain.one())
                        act.wait_ge(act_chain.sem, act_chain.all())
                        act.activation(e2[:, :, :], e2[:, :, :], ACT.Ln, bias=epsc[:, 3:4]).then_inc(act_chain.sem, act_chain.one())
                        act.wait_ge(act_chain.sem, act_chain.all())
                        act.activation(e2[:, :, :], e2[:, :, :], ACT.Exp, scale=-1.0).then_inc(ew_ready.sem, ew_ready.one())
                        act.wait_ge(ew_ready.sem, ew_ready.all())
                        act.wait_ge(kkss.sem, kkss.next(act))
                        rsqrt(rs_t, banks[2][:, 0:T], 1.0, 1).then_inc(kkrs.sem, kkrs.one())
                        act.wait_ge(kkrs.sem, kkrs.all())

                    for q in range(NT // GRP):
                        rates(GRP * q)
                        for jj in range(GRP):
                            j = GRP * q + jj
                            act.wait_ge(g_ready.sem, g_ready.next(act))
                            act.activation(e_x, e_x, ACT.Exp)
                            act.activation(e_g, gc_i, ACT.Exp)
                            act.activation(e_n, gc_i, ACT.Exp, scale=-1.0).then_inc(eg_ready.sem, eg_ready.one())
                            act.wait_ge(eg_ready.sem, eg_ready.all())
                            if jj + 1 < GRP:
                                rates(j + 1)
                            act.wait_ge(prod_done.sem, prod_done.next(act))
                            us = slice(jj * NC, (jj + 1) * NC)
                            for dst, bank, at in ((vtok, 6, 0), (ktok, 6, 256), (btok, 7, 0)):
                                i = act.copy(dst[:, us, :], banks[bank][:, at:at + 256].rearrange("p (u d) -> p u d", u=NC))
                            i.then_inc(prod_act.sem, prod_act.one())
                            act.wait_ge(prod_act.sem, prod_act.all())
                        invert_act(act, q)
                        for c in range(NC):
                            act.wait_ge(seq_pe.sem, seq_pe.at((4 * NC + 1) * q + 4 * c + 1))
                            act.copy(ws_a, banks[0][:, 0:256].rearrange("p (u d) -> p u d", u=GRP)).then_inc(seq_act.sem, seq_act.one())
                            act.wait_ge(seq_act.sem, seq_act.all())
                            act.wait_ge(seq_pe.sem, seq_pe.at((4 * NC + 1) * q + 4 * c + 2))
                            act.mul(us_a, banks[1][:, 0:256].rearrange("p (u d) -> p u d", u=GRP), -1.0).then_inc(seq_act.sem, seq_act.one())
                            act.wait_ge(seq_act.sem, seq_act.all())
                        act.wait_ge(seq_pe.sem, seq_pe.at((4 * NC + 1) * (q + 1)))
                        act.copy(mo_a, banks[0][:, 0:256].rearrange("p (u d) -> p u d", u=GRP)).then_inc(seq_act.sem, seq_act.one())
                        act.wait_ge(seq_act.sem, seq_act.all())
                        for g in range(2):
                            act.dma_start(
                                O["prompt_rwkv_wkv"][l, 0, 2 * GRP * q:2 * GRP * (q + 1)]
                                .rearrange("(j g) v k -> g v j k", g=2)[g], mo_a[64 * g:64 * g + 64, :, :]).then_inc(st_out.sem, st_out.one())
                        act.wait_ge(st_out.sem, st_out.all())

                    def state_ap(ap, g, vh):
                        return ap.rearrange("b (j g) v k -> g (b j) (v k)", g=2)[g][:, vh * 2048:(vh + 1) * 2048]

                    for vh in range(2):
                        for g in range(2):
                            act.dma_start(
                                samp_both[vh][64 * g:64 * g + 64, :, :].rearrange("p v k -> p (v k)"),
                                state_ap(I["state_rwkv_wkv"][l], g, vh)).then_inc(samp_in[vh].sem, samp_in[vh].one())
                    act.wait_ge(sv_pe.sem, sv_pe.next(act))
                    act.copy(svt[:, :, :], banks[4][:, 0:6 * C].rearrange("p (n d) -> p n d", n=6)).then_inc(svt_ready.sem, svt_ready.one())
                    act.wait_ge(svt_ready.sem, svt_ready.all())
                    for vh in range(2):
                        act.wait_ge(samp_done.sem, samp_done.next(act))
                        for g in range(2):
                            act.dma_start(
                                state_ap(O["sample_rwkv_wkv"][l], g, vh),
                                samp_both[vh][64 * g:64 * g + 64, :, :].rearrange("p v k -> p (v k)")).then_inc(samp_out.sem, samp_out.one())
                    act.wait_ge(sv_pe.sem, sv_pe.next(act))
                    act.copy(h[:, :, NPR:T], banks[5][:, 0:64].rearrange("p (b j) -> p j b", j=NT)).then_inc(ys_done.sem, ys_done.one())
                    act.wait_ge(ys_done.sem, ys_done.all())

                    def square_centred(j):
                        act.wait_ge(gn_cent.sem, gn_cent.at(j + 1))
                        if j >= 2:
                            act.wait_ge(gn_sum.sem, gn_sum.at(j - 1))
                        act.activation(gn_squares[j % 2], h[:, j, :], ACT.Square).then_inc(gn_sq.sem, gn_sq.one())
                        act.wait_ge(gn_sq.sem, gn_sq.all())

                    square_centred(0)
                    for j in range(NT):
                        if j + 1 < NT:
                            square_centred(j + 1)
                        act.wait_ge(gn_sum.sem, gn_sum.at(j + 1))
                        if j >= 2:
                            act.wait_ge(gn_out.sem, gn_out.at(j - 1))
                        rsqrt(gn_factors[j % 2], banks[1 + 3 * (j % 2)][:, 0:T], 1.0 / HD_A, 2).then_inc(gn_rs.sem, gn_rs.one())
                        act.wait_ge(gn_rs.sem, gn_rs.all())

                    act.wait_ge(gn_out.sem, gn_out.at(NT))
                    r3, r4 = g_row[0:8, 3, :], g_row[0:8, 4, :]
                    act.activation(r3, abr[0:8, 0, :], ACT.Abs, bias=adt[0:8, 1:2]).then_inc(act_chain.sem, act_chain.one())
                    act.wait_ge(act_chain.sem, act_chain.all())
                    act.activation(r3, r3, ACT.Exp, scale=-1.0).then_inc(act_chain.sem, act_chain.one())
                    act.wait_ge(act_chain.sem, act_chain.all())
                    act.activation(r3, r3, ACT.Ln, bias=epsc[0:8, 3:4])
                    act.activation(r4, abr[0:8, 1, :], ACT.Exp, scale=-1.0)
                    act.activation(adt[0:8, 0:1], adt[0:8, 0:1], ACT.Exp).then_inc(gdn_rows_a.sem, gdn_rows_a.one())
                    act.wait_ge(gdn_rows_a.sem, gdn_rows_a.all())
                    act.wait_ge(gdn_rows_d.sem, gdn_rows_d.next(act))
                    act.activation(g_row[0:8, 2, 0:NPR], g_row[0:8, 2, 0:NPR], ACT.Exp)
                    act.activation(g_row[0:8, 6, :], g_row[0:8, 0, :], ACT.Exp).then_inc(gdn_rows_a.sem, gdn_rows_a.one())
                    act.wait_ge(gdn_rows_a.sem, gdn_rows_a.all())
                    act.wait_ge(samp_out.sem, samp_out.next(act, 4))
                    def square(u):
                        if u >= 2:
                            act.wait_ge(unit_ss.sem, unit_ss.at(u - 1))
                        act.activation(g_tmp[:, u % 2, :], qk[:, u, 3:T + 3], ACT.Square).then_inc(unit_sq.sem, unit_sq.one())
                        act.wait_ge(unit_sq.sem, unit_sq.all())

                    square(0)
                    for u in range(2 * H_B):
                        if u + 1 < 2 * H_B:
                            square(u + 1)
                        act.wait_ge(unit_ss.sem, unit_ss.at(u + 1))
                        if u >= 2:
                            act.wait_ge(unit_done.sem, unit_done.at(u - 1))
                        rsqrt(g_tmp[:, 2 + u % 2, :], banks[u % 2][:, 0:T], 1.0, 0).then_inc(unit_rs.sem, unit_rs.one())
                        act.wait_ge(unit_rs.sem, unit_rs.all())
                    for n in range(H_B):
                        act.wait_ge(gc_done.sem, gc_done.at(n + 1))
                        act.activation(g_eg[:, n, :], banks[2][:, 0:T], ACT.Exp).then_inc(gdn_ra.sem, gdn_ra.one())
                        act.wait_ge(gdn_ra.sem, gdn_ra.all())
                        act.wait_ge(gdn_rd.sem, gdn_rd.next(act))
                        dd = g_tmp[:, 1 + 2 * ((n + 1) % 2), 0:P]
                        act.activation(dd, dd, ACT.Exp).then_inc(gdn_ra.sem, gdn_ra.one())
                        act.wait_ge(gdn_ra.sem, gdn_ra.all())
                    invert_act(act, 2)
                    for c in range(NC):
                        hf = HALVES[c % 2]
                        act.wait_ge(gdn_pe.sem, gdn_pe.at(1 + H_B + 4 * c + 2))
                        act.copy(g_vn[hf, 0:4, :], banks[2][hf, :].rearrange("p (n v) -> p n v", n=4))
                        act.copy(g_vn[hf, 4:8, :], banks[3][hf, :].rearrange("p (n v) -> p n v", n=4)).then_inc(gdn_act.sem, gdn_act.one())
                        act.wait_ge(gdn_act.sem, gdn_act.all())
                    act.wait_ge(gdn_dve.sem, gdn_dve.at(GD_SEQ))
                    act.dma_start(O["prompt_gdn_ssm"][l, 0].rearrange("h k v -> k h v"), g_s[:, :, :]).then_inc(st_out.sem, st_out.one())
                    def sample_state(ap, n):
                        return ap[:, n].rearrange("b k v -> k b v")

                    def load_state(n):
                        act.dma_start(gs_s[n % 2], sample_state(I["state_gdn_ssm"][l], n)).then_inc(gs_in[n % 2].sem, gs_in[n % 2].one())

                    load_state(0)
                    load_state(1)
                    for n in range(H_B):
                        act.wait_ge(gdn_dve.sem, gdn_dve.at(GD_SEQ + 1 + 3 * (n + 1)))
                        act.dma_start(sample_state(O["sample_gdn_ssm"][l], n), gs_s[n % 2]).then_inc(gs_out[n % 2].sem, gs_out[n % 2].one())
                        if n + 2 < H_B:
                            act.wait_ge(gs_out[n % 2].sem, gs_out[n % 2].next(act))
                            load_state(n + 2)
                    act.wait_ge(lora_done.sem, lora_done.at(3 * NT))
                    for m in range(2):
                        high(act, run_ends[1] + m)
                    for n in range(H_B):
                        if n >= 2:
                            act.wait_ge(gdn_pe.sem, gdn_pe.at(GP_POST + n - 1))
                        act.activation(g_tmp[:, n % 2, :], y[:, n, :], ACT.Square).then_inc(gdn_act.sem, gdn_act.one())
                        act.wait_ge(gdn_act.sem, gdn_act.all())
                        act.wait_ge(gdn_pe.sem, gdn_pe.at(GP_POST + n + 1))
                        if n >= 2:
                            act.wait_ge(merged.sem, merged.at(n - 1))
                        rsqrt(g_tmp[:, 2 + n % 2, :], banks[4 + n % 2][:, 0:T], 1.0 / HD_B, 0).then_inc(gdn_ra.sem, gdn_ra.one())
                        act.wait_ge(gdn_ra.sem, gdn_ra.all())

                    for o in range(NT):
                        ahead(act, high, ("out", o))
                        act.wait_ge(lin_done.sem, lin_done.at(where[("out", o)] + 1))
                        act.mul(y[:, o, :], banks[o % 4][:, 0:T], 0.5).then_inc(out_taken.sem, out_taken.one())
                        act.wait_ge(out_taken.sem, out_taken.all())
                        act.activation(sq_out[:, o, :], y[:, o, :], ACT.Square).then_inc(sq_ready.sem, sq_ready.one())
                        act.wait_ge(sq_ready.sem, sq_ready.all())
                    normalise(False)
                    normalise(True)
                    ffn(1)
                    act.wait_ge(st_out.sem, st_out.all())
                    for s in gs_out:
                        act.wait_ge(s.sem, s.all())

                @block.vector
                def _(dve):
                    def tt(out, a, b, op=ALU.mult):
                        return dve.tensor_tensor(out, a, b, op)

                    def stt(out, a, s, b, op0, op1):
                        return dve.scalar_tensor_tensor(out, a, s, b, op0, op1)

                    dve.wait_ge(tr_done.sem, tr_done.next(dve))
                    for g, rows in enumerate((120, 83, 96)):
                        i = dve.tensor_copy(pcol[:, g * P:g * P + rows], banks[6][:, g * P:g * P + rows])
                    dve.tensor_copy(shp[:, :, :], banks[7][:, 0:208].rearrange("p (b j) -> p j b", b=NS))
                    dve.tensor_copy(cvp[:, :, 0:12], banks[7][:, 208:496].rearrange("p (r j) -> p j r", r=12))
                    i = dve.tensor_copy(cvp[:, :, 12:24], banks[3][:, 0:288].rearrange("p (r j) -> p j r", r=12))
                    i.then_inc(cols_ready.sem, cols_ready.one())
                    dve.wait_ge(cols_ready.sem, cols_ready.all())
                    dve.tensor_scalar(ncol[:, 0:16], pcol[:, 154:170], -1.0, None, ALU.mult)
                    dve.tensor_scalar(ncol[:, 16:24], k_a, -1.0, 1.0, ALU.mult, ALU.add)

                    dve.memset(pa[:, 24, 0:1], 0.0).then_inc(x_ready.sem, x_ready.one())
                    dve.wait_ge(x_ready.sem, x_ready.all())

                    def conditioning(first, last, bank, at):
                        dve.wait_ge(lin_done.sem, lin_done.at(where[("ada", last - 1)] + 1))
                        n = last - first
                        tt(modv[:, first:last, :], banks[bank][:, at:at + n * NROW].rearrange("p (m r) -> p m r", r=NROW),
                           bc(bada[:, first:last], NROW), ALU.add).then_inc(dve_chain.sem, dve_chain.one())
                        dve.wait_ge(dve_chain.sem, dve_chain.all())

                    def scales(s):
                        sub, m = slice(NT * s, NT * (s + 1)), 3 * NT * s
                        stt(mod_a[:, sub, :], modv[:, m + NT:m + 2 * NT, :], 1.0, bc(npre[:, sub], NROW), ALU.add, ALU.mult).then_inc(dve_chain.sem, dve_chain.one())
                        dve.wait_ge(dve_chain.sem, dve_chain.all())

                    def gate_of(s):
                        sub, m = slice(NT * s, NT * (s + 1)), 3 * NT * s
                        stt(mod_g[:, sub, :], modv[:, m + 2 * NT:m + 3 * NT, :], 1.0 if s == 1 else FFN_RES,
                            bc(npost[:, sub], NROW), ALU.mult, ALU.mult).then_inc(dve_chain.sem, dve_chain.one())
                        dve.wait_ge(dve_chain.sem, dve_chain.all())

                    def split_input(hi):
                        for half in (slice(0, NT // 2), slice(NT // 2, NT)):
                            dve.tensor_copy(hi[:, half, :], h[:, half, :]).then_inc(dve_chain.sem, dve_chain.one())
                            dve.wait_ge(dve_chain.sem, dve_chain.all())
                            i = tt(h_lo[:, half, :], h[:, half, :], hi[:, half, :].bitcast(F32), ALU.subtract)
                        i.then_inc(h_ready.sem, h_ready.one())
                        dve.wait_ge(h_ready.sem, h_ready.all())

                    def sub_in(s, hi):
                        dve.wait_ge(rs_ready.sem, rs_ready.next(dve))
                        tt(h[:, :, :], xT[:, :, :], bm(rs[:, :], NT)).then_inc(dve_chain.sem, dve_chain.one())
                        dve.wait_ge(dve_chain.sem, dve_chain.all())
                        for j in range(NT):
                            dve.tensor_scalar(h[:, j, 0:NPR], h[:, j, 0:NPR], mod_a[:, NT * s + j, 0:1],
                                              modv[:, 3 * NT * s + j, 0:1], ALU.mult, ALU.add)
                        hs = h[:, :, NPR:T]
                        tt(hs, hs, mod_a[:, NT * s:NT * (s + 1), 1:NROW]).then_inc(dve_chain.sem, dve_chain.one())
                        dve.wait_ge(dve_chain.sem, dve_chain.all())
                        tt(hs, hs, modv[:, 3 * NT * s:3 * NT * s + NT, 1:NROW], ALU.add).then_inc(dve_chain.sem, dve_chain.one())
                        dve.wait_ge(dve_chain.sem, dve_chain.all())
                        split_input(hi)

                    def sub_out(s):
                        dve.wait_ge(rs_ready.sem, rs_ready.next(dve))
                        tt(y[:, :, :], y[:, :, :], bm(rs[:, :], NT)).then_inc(dve_chain.sem, dve_chain.one())
                        dve.wait_ge(dve_chain.sem, dve_chain.all())
                        for j in range(NT):
                            stt(xT[:, j, 0:NPR], y[:, j, 0:NPR], mod_g[:, NT * s + j, 0:1], xT[:, j, 0:NPR], ALU.mult, ALU.add)
                        ys, xs = y[:, :, NPR:T], xT[:, :, NPR:T]
                        tt(ys, ys, mod_g[:, NT * s:NT * (s + 1), 1:NROW]).then_inc(dve_chain.sem, dve_chain.one())
                        dve.wait_ge(dve_chain.sem, dve_chain.all())
                        tt(xs, xs, ys, ALU.add).then_inc(x_ready.sem, x_ready.one())
                        dve.wait_ge(x_ready.sem, x_ready.all())

                    def ffn(i_ffn):
                        sub_in(2 * i_ffn, hi_ffn)
                        for t in range(FT):
                            for g in range(2):
                                ahead(dve, low, (f"up{i_ffn}", 2 * t + g))
                            dve.wait_ge(gate_taken.sem, gate_taken.at(i_ffn * FT + t + 1))
                            dve.wait_ge(lin_done.sem, lin_done.at(where[(f"up{i_ffn}", 2 * t + 1)] + 1))
                            hid = silu_g[:, t % 2, :]
                            tt(hid, hid, banks[2 + t % 2][:, 0:T]).then_inc(dve_chain.sem, dve_chain.one())
                            dve.wait_ge(dve_chain.sem, dve_chain.all())
                            dve.tensor_copy(hid_hi[:, t, :], hid).then_inc(dve_chain.sem, dve_chain.one())
                            dve.wait_ge(dve_chain.sem, dve_chain.all())
                            tt(hid_lo[:, t, :], hid, hid_hi[:, t, :].bitcast(F32), ALU.subtract).then_inc(hid_ready.sem, hid_ready.one())
                            dve.wait_ge(hid_ready.sem, hid_ready.all())
                        for n in range(3 * NT):
                            ahead(dve, low, (f"down{i_ffn}", n))
                        sub_out(2 * i_ffn)

                    for m in range(2):
                        low(dve, m)
                    conditioning(0, ADA[0], 4, 0)
                    scales(0)
                    gate_of(0)
                    ffn(0)
                    conditioning(ADA[0], ADA[2], 5, 0)
                    scales(1)
                    for m in range(2):
                        low(dve, run_ends[0] + m)
                    sub_in(1, hi_in)
                    dve.memset(pa[:, :, 0:1], 0.0)
                    dve.memset(qk[:, :, 0:3], 0.0).then_inc(pads.sem, pads.one())
                    dve.wait_ge(pads.sem, pads.all())

                    def lows(first, last):
                        for n in range(first, last):
                            ahead(dve, low, plan[where[("in", 0)] + n])

                    for t0 in range(0, A_TILES, 2):
                        lows(t0, t0 + 2)
                        ts = slice(t0, t0 + 2)
                        dve.wait_ge(out_taken.sem, out_taken.at(NT + t0 + 2))
                        dve.tensor_copy(last_c[:, ts], pa[:, ts, NPR])
                        i = dve.tensor_copy(last_c[:, 26:234].rearrange("p (b j) -> p b j", b=NS)[:, :, ts],
                                            pa[:, ts, NPR + 1:T + 1].rearrange("p j b -> p b j"))
                        if t0 + 2 == A_TILES:
                            i.then_inc(last_cp.sem, last_cp.one())
                            dve.wait_ge(last_cp.sem, last_cp.all())
                        tt(y[:, 0:2, 0:NPR], pa[:, ts, 0:NPR], pa[:, ts, 1:NPR + 1], ALU.subtract)
                        tt(y[:, 0:2, NPR:T], shp[:, ts, :], pa[:, ts, NPR + 1:T + 1], ALU.subtract).then_inc(dve_chain.sem, dve_chain.one())
                        dve.wait_ge(dve_chain.sem, dve_chain.all())
                        for j in range(2):
                            i = stt(pa[:, t0 + j, 1:T + 1], y[:, j, :], mu[:, t0 + j:t0 + j + 1], pa[:, t0 + j, 1:T + 1],
                                    ALU.mult, ALU.add)
                        i.then_inc(shifted.sem, shifted.one())
                        dve.wait_ge(shifted.sem, shifted.all())
                    cv = cvp[:, :, :].rearrange("p j (b i) -> p j b i", i=3)
                    lows(A_TILES, conv_turn(0))
                    for n in range(Q_TILES):
                        lows(conv_turn(n), conv_turn(n + 1))
                        if n % NT == 0:
                            js = slice(n, n + NT)
                            dve.wait_ge(out_taken.sem, out_taken.at(NT + A_TILES + n + NT))
                            dve.tensor_copy(last_c[:, 234:306].rearrange("p (i j) -> p i j", i=3)[:, :, js],
                                            qk[:, js, NPR:NPR + 3].rearrange("p j i -> p i j"))
                            i = dve.tensor_copy(last_c[:, 306:498].rearrange("p (b j) -> p b j", b=NS)[:, :, js],
                                                qk[:, js, NPR + 3:T + 3].rearrange("p j b -> p b j"))
                            if n + NT == Q_TILES:
                                i.then_inc(last_cp.sem, last_cp.one())
                                dve.wait_ge(last_cp.sem, last_cp.all())
                            tt(convs[:, js, :], qk[:, js, NPR + 3:T + 3], bc(convw[:, 3, js], NS)).then_inc(dve_chain.sem, dve_chain.one())
                            dve.wait_ge(dve_chain.sem, dve_chain.all())
                            for k in range(3):
                                tt(convt[:, js, :], cv[:, js, :, k], bc(convw[:, k, js], NS)).then_inc(dve_chain.sem, dve_chain.one())
                                dve.wait_ge(dve_chain.sem, dve_chain.all())
                                tt(convs[:, js, :], convs[:, js, :], convt[:, js, :], ALU.add).then_inc(dve_chain.sem, dve_chain.one())
                                dve.wait_ge(dve_chain.sem, dve_chain.all())
                        acc = (rs[:, :], rs2)[n % 2]
                        if n >= 2:
                            dve.wait_ge(conv_done.sem, conv_done.at(n - 1))
                        dve.tensor_scalar(acc[:, 0:NPR], qk[:, n, 0:NPR], convw[:, 0, n:n + 1], None, ALU.mult).then_inc(dve_chain.sem, dve_chain.one())
                        dve.wait_ge(dve_chain.sem, dve_chain.all())
                        for k in range(1, 4):
                            stt(acc[:, 0:NPR], qk[:, n, k:k + NPR], convw[:, k, n:n + 1], acc[:, 0:NPR], ALU.mult, ALU.add).then_inc(dve_chain.sem, dve_chain.one())
                            dve.wait_ge(dve_chain.sem, dve_chain.all())
                        dve.tensor_copy(acc[:, NPR:T], convs[:, n, :]).then_inc(conv_ready.sem, conv_ready.one())
                        dve.wait_ge(conv_ready.sem, conv_ready.all())
                    dve.wait_ge(last_tr.sem, last_tr.next(dve))

                    dve.wait_ge(lora_in.sem, lora_in.next(dve))
                    dve.tensor_scalar(pa[:, 25, 1:T + 1], pa[:, 25, 1:T + 1], 0.5, 0.5, ALU.mult, ALU.add).then_inc(gate_in.sem, gate_in.one())
                    dve.wait_ge(gate_in.sem, gate_in.all())
                    def decay(j):
                        r, k = pa[:, j, 1:T + 1], pa[:, 8 + j, 1:T + 1]
                        dve.wait_ge(ew_ready.sem, ew_ready.next(dve))
                        dve.tensor_scalar(lw, e2[:, 0, :], -EXP_MHALF, None, ALU.mult).then_inc(dve_chain.sem, dve_chain.one())
                        dve.wait_ge(dve_chain.sem, dve_chain.all())
                        dve.tensor_tensor_scan(gc_i, carry[:, :], lw, 0.0, ALU.mult, ALU.add).then_inc(dve_chain.sem, dve_chain.one())
                        dve.wait_ge(dve_chain.sem, dve_chain.all())
                        tt(e_x, gc_i, lw, ALU.subtract).then_inc(g_ready.sem, g_ready.one())
                        dve.wait_ge(g_ready.sem, g_ready.all())
                        dve.wait_ge(kkrs.sem, kkrs.next(dve))
                        dve.tensor_scalar(rkk, e2[:, 1, :], k_a[:, j:j + 1], ncol[:, 16 + j:17 + j], ALU.mult, ALU.add)
                        stt(kkn, k, k_k[:, j:j + 1], rs_t, ALU.mult, ALU.mult).then_inc(dve_chain.sem, dve_chain.one())
                        dve.wait_ge(dve_chain.sem, dve_chain.all())
                        tt(kb_t, kkn, e2[:, 1, :])
                        tt(k, rkk, k).then_inc(dve_chain.sem, dve_chain.one())
                        dve.wait_ge(dve_chain.sem, dve_chain.all())
                        stt(rkk, r, r_k[:, j:j + 1], k, ALU.mult, ALU.mult).then_inc(rkk_ready.sem, rkk_ready.one())
                        dve.wait_ge(rkk_ready.sem, rkk_ready.all())

                    for q in range(NT // GRP):
                        decay(GRP * q)
                        for jj in range(GRP):
                            j = GRP * q + jj
                            r, k, v = (pa[:, 8 * n + j, 1:T + 1] for n in range(3))
                            dve.wait_ge(eg_ready.sem, eg_ready.next(dve))
                            tt(kdec_f[:, jj, :], kkn[:, 0:NPR], e_x[:, 0:NPR])
                            tt(b_f[:, 0:NPR], kb_t[:, 0:NPR], e_n[:, 0:NPR])
                            tt(kd_f[:, 0:NPR], k[:, 0:NPR], e_n[:, 0:NPR])
                            dve.tensor_copy(eg_end[:, j, :], e_g[:, 0:NPR].rearrange("p (c t) -> p c t", t=C)[:, :, C - 1])
                            for n, src in enumerate((e_g, kkn, kb_t, k, v, r)):
                                dve.tensor_copy(sv[:, n, :, j], src[:, NPR:T])
                            tt(r[:, 0:NPR], r[:, 0:NPR], e_g[:, 0:NPR]).then_inc(ops_ready.sem, ops_ready.one())
                            dve.wait_ge(ops_ready.sem, ops_ready.all())
                            dve.wait_ge(bonss.sem, bonss.next(dve))
                            tt(y[:, j, :], v, banks[3][:, 0:T]).then_inc(dve_chain.sem, dve_chain.one())
                            dve.wait_ge(dve_chain.sem, dve_chain.all())
                            if jj + 1 < GRP:
                                decay(j + 1)
                            dve.wait_ge(prod_done.sem, prod_done.next(dve))
                            us = slice(jj * NC, (jj + 1) * NC)
                            for dst, bank, at, mask in ((lt_all, 4, 0, strict), (pb_all, 4, 256, incl),
                                                        (dm_all, 5, 0, strict), (pk_all, 5, 256, incl)):
                                i = tt(dst[:, us, :], banks[bank][:, at:at + 256].rearrange("p (u t) -> p u t", u=NC),
                                       bm(mask[:, :], NC))
                            i.then_inc(prod_dve.sem, prod_dve.one())
                            dve.wait_ge(prod_dve.sem, prod_dve.all())
                        if q:
                            dve.wait_ge(prod_act.sem, prod_act.at(NT))
                            conditioning(ADA[2], ADA[3], 7, 256)
                            gate_of(1)
                            scales(2)
                            gate_of(2)
                        invert_dve(dve, q)
                        dve.memset(m_st, 0.0).then_inc(seq_dve.sem, seq_dve.one())
                        dve.wait_ge(seq_dve.sem, seq_dve.all())
                        for c in range(NC):
                            dve.wait_ge(seq_pe.sem, seq_pe.at((4 * NC + 1) * q + 4 * c + 3))
                            dve.tensor_copy(h[:, GRP * q:GRP * (q + 1), c * C:(c + 1) * C],
                                            banks[2][:, 0:256].rearrange("p (u t) -> p u t", u=GRP))
                            dve.wait_ge(seq_pe.sem, seq_pe.at((4 * NC + 1) * q + 4 * c + 4))
                            tt(m_st, m_st, banks[3][:, 0:256].rearrange("p (u t) -> p u t", u=GRP), ALU.add).then_inc(dve_chain.sem, dve_chain.one())
                            dve.wait_ge(dve_chain.sem, dve_chain.all())
                            tt(m_st, m_st, bc(eg_end[:, GRP * q:GRP * (q + 1), c], C)).then_inc(seq_dve.sem, seq_dve.one())
                            dve.wait_ge(seq_dve.sem, seq_dve.all())
                        if q + 1 < NT // GRP:
                            dve.wait_ge(seq_pe.sem, seq_pe.at((4 * NC + 1) * (q + 1)))

                    dve.wait_ge(svt_ready.sem, svt_ready.next(dve))
                    w_s, kk_s, b_s, k_s, v_s, r_s = (svt[:, n, :] for n in range(6))
                    for vh in range(2):
                        dve.wait_ge(samp_in[vh].sem, samp_in[vh].next(dve, 2))
                        samp_s = samp_both[vh]
                        vs = slice(32 * vh, 32 * vh + 32)
                        tt(samp_t, samp_s, bm(kk_s, 32)).then_inc(dve_chain.sem, dve_chain.one())
                        dve.wait_ge(dve_chain.sem, dve_chain.all())
                        dve.tensor_reduce(ssm[:, 0, vs], samp_t, AX_X, ALU.add).then_inc(dve_chain.sem, dve_chain.one())
                        dve.wait_ge(dve_chain.sem, dve_chain.all())
                        tt(samp_s, samp_s, bm(w_s, 32)).then_inc(dve_chain.sem, dve_chain.one())
                        dve.wait_ge(dve_chain.sem, dve_chain.all())
                        tt(samp_t, bc(ssm[:, 0, vs], C), bm(b_s, 32)).then_inc(dve_chain.sem, dve_chain.one())
                        dve.wait_ge(dve_chain.sem, dve_chain.all())
                        tt(samp_s, samp_s, samp_t, ALU.subtract).then_inc(dve_chain.sem, dve_chain.one())
                        dve.wait_ge(dve_chain.sem, dve_chain.all())
                        tt(samp_t, bc(v_s[:, vs], C), bm(k_s, 32)).then_inc(dve_chain.sem, dve_chain.one())
                        dve.wait_ge(dve_chain.sem, dve_chain.all())
                        tt(samp_s, samp_s, samp_t, ALU.add).then_inc(dve_chain.sem, dve_chain.one())
                        dve.wait_ge(dve_chain.sem, dve_chain.all())
                        tt(samp_t, samp_s, bm(r_s, 32)).then_inc(dve_chain.sem, dve_chain.one())
                        dve.wait_ge(dve_chain.sem, dve_chain.all())
                        dve.tensor_reduce(ssm[:, 1, vs], samp_t, AX_X, ALU.add).then_inc(samp_done.sem, samp_done.one())
                        dve.wait_ge(samp_done.sem, samp_done.all())
                    dve.wait_ge(ys_done.sem, ys_done.next(dve))

                    def centre(j):
                        dve.wait_ge(gn_mean.sem, gn_mean.at(j + 1))
                        stt(h[:, j, :], banks[3 * (j % 2)][:, 0:T], -1.0 / HD_A, h[:, j, :], ALU.mult, ALU.add).then_inc(gn_cent.sem, gn_cent.one())
                        dve.wait_ge(gn_cent.sem, gn_cent.all())

                    centre(0)
                    for j in range(NT):
                        if j + 1 < NT:
                            centre(j + 1)
                        hj = h[:, j, :]
                        dve.wait_ge(gn_rs.sem, gn_rs.at(j + 1))
                        tt(hj, hj, gn_factors[j % 2]).then_inc(dve_chain.sem, dve_chain.one())
                        dve.wait_ge(dve_chain.sem, dve_chain.all())
                        dve.tensor_scalar(hj, hj, ln_w[:, j:j + 1], ln_b[:, j:j + 1], ALU.mult, ALU.add).then_inc(dve_chain.sem, dve_chain.one())
                        dve.wait_ge(dve_chain.sem, dve_chain.all())
                        tt(hj, hj, y[:, j, :], ALU.add).then_inc(dve_chain.sem, dve_chain.one())
                        dve.wait_ge(dve_chain.sem, dve_chain.all())
                        dve.wait_ge(lora_done.sem, lora_done.at(2 * NT + j + 1))
                        tt(hj, hj, banks[2 + 3 * (j % 2)][:, 0:T]).then_inc(dve_chain.sem, dve_chain.one())
                        dve.wait_ge(dve_chain.sem, dve_chain.all())
                        stt(hj, gates[:, j, :], 1.0, hj, ALU.add, ALU.mult).then_inc(gn_out.sem, gn_out.one())
                        dve.wait_ge(gn_out.sem, gn_out.all())

                    dve.wait_ge(gdn_rows_a.sem, gdn_rows_a.next(dve))
                    row = [g_row[0:8, n, :] for n in range(8)]
                    dve.tensor_scalar(row[4], row[4], 1.0, None, ALU.add)
                    dve.tensor_scalar(row[5], abr[0:8, 0, :], adt[0:8, 1:2], 0.0, ALU.add, ALU.max).then_inc(dve_chain.sem, dve_chain.one())
                    dve.wait_ge(dve_chain.sem, dve_chain.all())
                    dve.reciprocal(row[1], row[4])
                    tt(row[5], row[5], row[3], ALU.add).then_inc(dve_chain.sem, dve_chain.one())
                    dve.wait_ge(dve_chain.sem, dve_chain.all())
                    dve.tensor_scalar(row[5], row[5], adt[0:8, 0:1], -1.0, ALU.mult, ALU.mult).then_inc(dve_chain.sem, dve_chain.one())
                    dve.wait_ge(dve_chain.sem, dve_chain.all())
                    dve.tensor_tensor_scan(row[0], carry[0:8, :], row[5], 0.0, ALU.mult, ALU.add).then_inc(dve_chain.sem, dve_chain.one())
                    dve.wait_ge(dve_chain.sem, dve_chain.all())
                    gcv = row[0][:, 0:NPR].rearrange("p (c t) -> p c t", t=C)
                    tt(row[2][:, 0:NPR].rearrange("p (c t) -> p c t", t=C),
                      gcv[:, :, C - 1:C].to_broadcast([8, NC, C]), gcv, ALU.subtract).then_inc(gdn_rows_d.sem, gdn_rows_d.one())
                    dve.wait_ge(gdn_rows_d.sem, gdn_rows_d.all())
                    dve.wait_ge(gdn_rows_a.sem, gdn_rows_a.next(dve))
                    stt(row[7], row[6], -1.0, row[1], ALU.mult, ALU.mult).then_inc(rows_ready.sem, rows_ready.one())
                    dve.wait_ge(rows_ready.sem, rows_ready.all())
                    dve.wait_ge(gdn_pe.sem, gdn_pe.at(1))
                    dve.tensor_copy(tks[:, :, :, :].rearrange("p a n h -> p (a n h)"), banks[7][:, 0:64]).then_inc(dve_chain.sem, dve_chain.one())
                    dve.wait_ge(dve_chain.sem, dve_chain.all())
                    for u in range(2 * H_B):
                        dve.wait_ge(unit_rs.sem, unit_rs.at(u + 1))
                        x = qk[:, u, 3:T + 3]
                        stt(x, x, HD_B ** -0.5 if u < H_B else 1.0, g_tmp[:, 2 + u % 2, :], ALU.mult, ALU.mult).then_inc(unit_done.sem, unit_done.one())
                        dve.wait_ge(unit_done.sem, unit_done.all())

                    def betas(n):
                        dve.wait_ge(gc_done.sem, gc_done.at(n + 1))
                        qn, kn = qk[:, n, 3:T + 3], qk[:, 8 + n, 3:T + 3]
                        tt(g_tmp[:, 2 * ((n + 1) % 2), 0:NPR], kn[:, 0:NPR], banks[3][:, 0:NPR])
                        dve.tensor_copy(beta_s[:, n, :], banks[3][:, NPR:T])
                        tt(qk_s[:, n, :], qn[:, NPR:T], kn[:, NPR:T])
                        dve.wait_ge(gdn_ra.sem, gdn_ra.at(2 * n + 1))
                        for c in range(NC):
                            hf, cp = HALVES[c % 2], c // 2
                            i = dve.tensor_scalar(g_tmp[hf, 1 + 2 * ((n + 1) % 2), cp * C:(cp + 1) * C],
                                                  banks[2][hf, c * C:(c + 1) * C], tks[hf, cp, 0, n:n + 1], 0.0,
                                                  ALU.subtract, ALU.min)
                        i.then_inc(gdn_rd.sem, gdn_rd.one())
                        dve.wait_ge(gdn_rd.sem, gdn_rd.all())

                    betas(0)
                    for n in range(H_B):
                        qn = qk[:, n, 3:T + 3]
                        dve.wait_ge(gdn_ra.sem, gdn_ra.at(2 * n + 2))
                        dd = g_tmp[:, 1 + 2 * ((n + 1) % 2), 0:P].rearrange("p (c t) -> p c t", c=2)
                        ds = g_tmp[:, 4, 0:P].rearrange("p (c t) -> p c t", c=2)
                        di = g_tmp[:, 5, 0:P].rearrange("p (c t) -> p c t", c=2)
                        tt(ds, dd, bm(strict[:, :], 2))
                        tt(di, dd, bm(incl[:, :], 2)).then_inc(dve_chain.sem, dve_chain.one())
                        dve.wait_ge(dve_chain.sem, dve_chain.all())
                        if n + 1 < H_B:
                            betas(n + 1)
                        dve.wait_ge(gdn_pe.sem, gdn_pe.at(1 + n + 1))
                        tt(g_lt[:, 2 * n:2 * n + 2, :], banks[4][:, 0:P].rearrange("p (c t) -> p c t", c=2), ds)
                        tt(g_at[:, 2 * n:2 * n + 2, :], banks[4][:, P:2 * P].rearrange("p (c t) -> p c t", c=2), di)
                        for cp in range(2):
                            dve.tensor_scalar(g_kd[:, cp, n, :], banks[5][:, cp * P:(cp + 1) * P],
                                              tks[:, cp, 2, n:n + 1], None, ALU.mult)
                            dve.tensor_scalar(g_bv[:, cp, n, :], banks[5][:, 256 + cp * P:256 + (cp + 1) * P],
                                              tks[:, cp, 1, n:n + 1], None, ALU.mult)
                        tt(qn[:, 0:NPR], qn[:, 0:NPR], g_eg[:, n, 0:NPR]).then_inc(gdn_dve.sem, gdn_dve.one())
                        dve.wait_ge(gdn_dve.sem, gdn_dve.all())
                    invert_dve(dve, 2)
                    dve.memset(g_s[:, :, :], 0.0).then_inc(gdn_dve.sem, gdn_dve.one())
                    dve.wait_ge(gdn_dve.sem, gdn_dve.all())
                    for c in range(NC):
                        hf, cp = HALVES[c % 2], c // 2
                        dve.wait_ge(gdn_pe.sem, gdn_pe.at(1 + H_B + 4 * c + 1))
                        for n in range(H_B):
                            i = stt(g_w[hf, n, :], banks[n // 4][hf, (n % 4) * P:(n % 4 + 1) * P],
                                    tks[hf, cp, 3, n:n + 1], g_bv[hf, cp, n, :], ALU.mult, ALU.add)
                        i.then_inc(gdn_dve.sem, gdn_dve.one())
                        dve.wait_ge(gdn_dve.sem, gdn_dve.all())
                        dve.wait_ge(gdn_pe.sem, gdn_pe.at(1 + H_B + 4 * c + 3))
                        dve.tensor_copy(y[:, :, c * C:(c + 1) * C], banks[4][:, :].rearrange("p (n t) -> p n t", n=H_B))
                        dve.wait_ge(gdn_pe.sem, gdn_pe.at(1 + H_B + 4 * c + 4))
                        for n in range(H_B):
                            i = stt(g_s[:, n, :], g_s[:, n, :], g_eg[:, n, c * C + C - 1:(c + 1) * C],
                                    banks[5 + n // 4][:, (n % 4) * P:(n % 4 + 1) * P], ALU.mult, ALU.add)
                        i.then_inc(gdn_dve.sem, gdn_dve.one())
                        dve.wait_ge(gdn_dve.sem, gdn_dve.all())
                    assert gdn_dve.posted == GD_SEQ
                    dve.wait_ge(gdn_pe.sem, gdn_pe.at(GP_SAMP))
                    dve.tensor_copy(qk_s[:, :, :].rearrange("p n b -> p (n b)"), banks[7][:, 0:64]).then_inc(gdn_dve.sem, gdn_dve.one())
                    dve.wait_ge(gdn_dve.sem, gdn_dve.all())
                    for n in range(H_B):
                        s = gs_s[n % 2]
                        dve.wait_ge(gdn_pe.sem, gdn_pe.at(GP_SAMP + 3 * n + 1))
                        both = banks[0][:, 0:2 * NS].rearrange("p (b g) -> p g b", g=2)
                        eg, vn = g_eg[:, n, NPR:T], sg[:, 1, :]
                        tt(sg[:, 2, :], both[:, 0, :], eg)
                        tt(sg[:, 0, :], both[:, 1, :], eg).then_inc(dve_chain.sem, dve_chain.one())
                        dve.wait_ge(dve_chain.sem, dve_chain.all())
                        tt(vn, qk[:, 16 + n, NPR + 3:T + 3], sg[:, 0, :], ALU.subtract).then_inc(dve_chain.sem, dve_chain.one())
                        dve.wait_ge(dve_chain.sem, dve_chain.all())
                        tt(vn, vn, beta_s[:, n, :]).then_inc(dve_chain.sem, dve_chain.one())
                        dve.wait_ge(dve_chain.sem, dve_chain.all())
                        tt(sg[:, 3, :], vn, qk_s[:, n, :]).then_inc(dve_chain.sem, dve_chain.one())
                        dve.wait_ge(dve_chain.sem, dve_chain.all())
                        tt(y[:, n, NPR:T], sg[:, 2, :], sg[:, 3, :], ALU.add).then_inc(gdn_dve.sem, gdn_dve.one())
                        dve.wait_ge(gdn_dve.sem, gdn_dve.all())
                        dve.wait_ge(gdn_pe.sem, gdn_pe.at(GP_SAMP + 3 * n + 2))
                        dve.tensor_copy(sgt[0:NS, :, :], banks[1][0:NS, 0:2 * P].rearrange("p (a f) -> p a f", a=2)).then_inc(dve_chain.sem, dve_chain.one())
                        dve.wait_ge(dve_chain.sem, dve_chain.all())
                        tt(gs_x[0:NS, :, :], bm(sgt[0:NS, 0, :], NS), bc(delta[0:NS, :], P)).then_inc(gdn_dve.sem, gdn_dve.one())
                        dve.wait_ge(gdn_dve.sem, gdn_dve.all())
                        tt(s, s, bc(eg, P)).then_inc(dve_chain.sem, dve_chain.one())
                        dve.wait_ge(dve_chain.sem, dve_chain.all())
                        dve.wait_ge(gdn_pe.sem, gdn_pe.at(GP_SAMP + 3 * n + 3))
                        for g in range(2):
                            i = tt(s[:, 4 * g:4 * g + 4, :], s[:, 4 * g:4 * g + 4, :],
                                   banks[2 + g][:, :].rearrange("p (b v) -> p b v", b=4), ALU.add)
                        i.then_inc(gdn_dve.sem, gdn_dve.one())
                        dve.wait_ge(gdn_dve.sem, gdn_dve.all())
                    for m in range(2):
                        low(dve, run_ends[1] + m)
                    for n in range(H_B):
                        dve.wait_ge(gdn_ra.sem, gdn_ra.at(2 * H_B + n + 1))
                        yn = y[:, n, :]
                        tt(yn, yn, g_tmp[:, 2 + n % 2, :]).then_inc(dve_chain.sem, dve_chain.one())
                        dve.wait_ge(dve_chain.sem, dve_chain.all())
                        stt(yn, yn, g_nw, zs[:, n, :], ALU.mult, ALU.mult).then_inc(dve_chain.sem, dve_chain.one())
                        dve.wait_ge(dve_chain.sem, dve_chain.all())
                        stt(yn, gates[:, NT + n, :], 1.0, yn, ALU.add, ALU.mult).then_inc(dve_chain.sem, dve_chain.one())
                        dve.wait_ge(dve_chain.sem, dve_chain.all())
                        tt(h[:, n, :], h[:, n, :], yn, ALU.add).then_inc(dve_chain.sem, dve_chain.one())
                        dve.wait_ge(dve_chain.sem, dve_chain.all())
                        dve.tensor_copy(hi_out[:, n, :], h[:, n, :]).then_inc(dve_chain.sem, dve_chain.one())
                        dve.wait_ge(dve_chain.sem, dve_chain.all())
                        tt(h_lo[:, n, :], h[:, n, :], hi_out[:, n, :].bitcast(F32), ALU.subtract).then_inc(merged.sem, merged.one())
                        dve.wait_ge(merged.sem, merged.all())
                    for o in range(NT):
                        ahead(dve, low, ("out", o))
                    sub_out(1)
                    ffn(1)

            end_of_part()

        with nc.Block() as block:
            @block.tensor
            def _(pe):
                for a in range(2):
                    for j in range(NT):
                        n = a * NT + j
                        pe.transpose(banks[n // 4][:, (n % 4) * P:(n % 4 + 1) * P], xT[:, j, a * P:(a + 1) * P], ident[:, :])
                for j in range(NT):
                    i = pe.transpose(banks[4 + j // 4][0:NS, (j % 4) * P:(j % 4 + 1) * P], xT[:, j, NPR:T], ident[:, :])
                i.then_inc(tr_done.sem, tr_done.one())

            @block.scalar
            def _(act):
                act.wait_ge(tr_done.sem, tr_done.next(act))
                flat = y[:, :, :].rearrange("p j t -> p (j t)")
                for n in range(4):
                    i = act.copy(flat[:, n * 512:(n + 1) * 512], banks[n][:, :])
                i.then_inc(act_chain.sem, act_chain.one())
                hf = h[:, :, :].rearrange("p j t -> p (j t)")
                for n in range(2):
                    i = act.copy(hf[0:NS, n * 512:(n + 1) * 512], banks[4 + n][0:NS, :])
                i.then_inc(act_chain.sem, act_chain.one())
                act.wait_ge(act_chain.sem, act_chain.next(act, 2))
                act.dma_start(O["y_prompt"][0].rearrange("(a p) f -> p a f", p=P),
                                          flat[:, 0:2 * D].rearrange("p (a f) -> p a f", a=2)).then_inc(st_out.sem, st_out.one())
                act.dma_start(O["y_sample"].rearrange("b a f -> (b a) f"), hf[0:NS, 0:D]).then_inc(st_out.sem, st_out.one())
                act.wait_ge(st_out.sem, st_out.next(act, 2))


_INS = ["x_prompt", "x_sample", "c_prompt", "c_sample", "state_rwkv_shift", "state_rwkv_wkv", "state_gdn_conv",
        "state_gdn_ssm", "w_ada", "b_ada", "norm_pre", "norm_post", "ffn_up", "ffn_down", "w_in", "w_out", "rwkv_mu",
        "rwkv_w0", "rwkv_w2", "rwkv_a0", "rwkv_a2", "rwkv_g2", "rwkv_k_k", "rwkv_k_a", "rwkv_r_k", "rwkv_ln_w",
        "rwkv_ln_b", "gdn_conv", "gdn_a_log", "gdn_dt_bias", "gdn_norm_w"]
_OUTS = [("y_prompt", (1, NPR, D)), ("y_sample", (NS, 1, D)),
         ("prompt_rwkv_shift", (DEPTH, 1, A_COLS)), ("prompt_rwkv_wkv", (DEPTH, 1, H_A, HD_A, HD_A)),
         ("prompt_gdn_conv", (DEPTH, 1, 3, Q_COLS)), ("prompt_gdn_ssm", (DEPTH, 1, H_B, HD_B, HD_B)),
         ("sample_rwkv_shift", (DEPTH, NS, A_COLS)), ("sample_rwkv_wkv", (DEPTH, NS, H_A, HD_A, HD_A)),
         ("sample_gdn_conv", (DEPTH, NS, 3, Q_COLS)), ("sample_gdn_ssm", (DEPTH, NS, H_B, HD_B, HD_B))]


def kernel(**inputs):
    import numpy as _np
    import concourse.bacc as _bacc
    from concourse.bass_utils import run_bass_kernel_spmd as _run

    nc = _bacc.Bacc("TRN2", target_bir_lowering=False, num_devices=1)
    arrays, ins, outs = {}, {}, {}
    for name in _INS:
        a = _np.ascontiguousarray(inputs[name])
        arrays[f"in_{name}"] = a
        ins[name] = nc.dram_tensor(f"in_{name}", a.shape, F32, kind="ExternalInput").ap()
    for name, shape in _OUTS:
        outs[name] = nc.dram_tensor(f"out_{name}", shape, F32, kind="ExternalOutput").ap()
    build(nc, ins, outs)
    r = _run(nc, [arrays], core_ids=[0])
    return tuple(r.results[0][f"out_{name}"] for name, _ in _OUTS)
```
